# Optimizing a Trainium2 kernel written in Bass

```python
import jax, jax.numpy as jnp
from jax import lax
import numpy as np

'''Hybrid streaming encoder trunk: one inference step over DEPTH interleaved layers.

Layer i uses token mixer (i mod 2): even layers = multi-scale retention (RetNet, chunkwise-recurrent
form with per-token causal decay), odd layers = stick-breaking attention (strictly causal, no positional
encoding). Every layer (pre-RMSNorm, plain residuals):
  x += 1/2 * SwiGLU_a(RMSNorm(x))
  x += mixer(RMSNorm(x))
  x += 1/2 * SwiGLU_b(RMSNorm(x))
  x += sigmoid(RMSNorm(x) @ W_gate) * (p[i] @ W_proj)        (per-layer input embedding)
followed by one final RMSNorm.

Inputs:
  x_prompt   (BATCH, SEQ, D_MODEL)          first SEQ frames of new streams, positions 0..SEQ-1
  x_sample   (DEC_BATCH, DEC_SEQ, D_MODEL)  next frames of running streams, positions PAST_LEN..
  p_prompt   (DEPTH, BATCH, SEQ, PLE_DIM)
  p_sample   (DEPTH, DEC_BATCH, DEC_SEQ, PLE_DIM)
  state_ret  (N_RET_LAYERS, DEC_BATCH, H_RET, DK_RET, DV_RET)   retention matrix state
  cache_sb_k (N_SB_LAYERS, DEC_BATCH, PAST_LEN, H_SB, HD_SB)    stick-breaking keys
  cache_sb_v (N_SB_LAYERS, DEC_BATCH, PAST_LEN, H_SB, HD_SB)    stick-breaking values
  followed by the weights.
Returns the tuple
  (y_prompt         (BATCH, SEQ, D_MODEL),
   y_sample         (DEC_BATCH, DEC_SEQ, D_MODEL),
   state_ret_prompt (N_RET_LAYERS, BATCH, H_RET, DK_RET, DV_RET),
   state_ret_sample (N_RET_LAYERS, DEC_BATCH, H_RET, DK_RET, DV_RET),
   sb_k_prompt      (N_SB_LAYERS, BATCH, SEQ, H_SB, HD_SB),
   sb_v_prompt      (N_SB_LAYERS, BATCH, SEQ, H_SB, HD_SB),
   sb_k_sample      (N_SB_LAYERS, DEC_BATCH, DEC_SEQ, H_SB, HD_SB),
   sb_v_sample      (N_SB_LAYERS, DEC_BATCH, DEC_SEQ, H_SB, HD_SB))
'''

D_MODEL = 1024
BATCH = 1
SEQ = 512
DEPTH = 2
DEC_BATCH = 8
DEC_SEQ = 16
PAST_LEN = 128

CHUNK = 64
QBLOCK = 128
PLE_DIM = 256
H_RET = 8
DK_RET = D_MODEL // H_RET
DV_RET = 2 * DK_RET
RET_QK = H_RET * DK_RET
RET_V = H_RET * DV_RET
RET_IN = 2 * RET_QK + 2 * RET_V
H_SB = 16
HD_SB = D_MODEL // H_SB
D_FF = 2816
N_RET_LAYERS = (DEPTH + 1) // 2
N_SB_LAYERS = DEPTH // 2
ROPE_BASE = 10000.0
EPS = 1e-6
GN_EPS = 1e-5

kernel_name = 'retnet_stickbreaking_macaron_stream_step'

F32 = jnp.float32

def rmsnorm(x, g):
    xf = x.astype(F32)
    y = xf * lax.rsqrt(jnp.mean(xf * xf, axis=-1, keepdims=True) + EPS)
    return (y * g.astype(F32)).astype(x.dtype)

def half_swiglu(x, g, w_gu, w_down):
    h = rmsnorm(x, g) @ w_gu
    a, b = jnp.split(h, 2, axis=-1)
    return x + 0.5 * ((jax.nn.silu(a) * b) @ w_down)

def ple_add(x, p_i, g, w_gate, w_proj):
    gate = jax.nn.sigmoid((rmsnorm(x, g) @ w_gate).astype(F32))
    return x + (gate * (p_i @ w_proj).astype(F32)).astype(x.dtype)

def rotary(x, pos):
    half = x.shape[-1] // 2
    freqs = ROPE_BASE ** (-jnp.arange(half, dtype=F32) / half)
    ang = pos.astype(F32)[:, None] * freqs[None, :]
    cos = jnp.cos(ang)[None, :, None, :]
    sin = jnp.sin(ang)[None, :, None, :]
    xf = x.astype(F32)
    x1, x2 = xf[..., :half], xf[..., half:]
    return jnp.concatenate([x1 * cos - x2 * sin, x1 * sin + x2 * cos], axis=-1)

def retention_scan(q, k, v, s0):
    B, L, H, DK = q.shape
    DV = v.shape[-1]
    C = min(CHUNK, L)
    nc = L // C
    log_g = jnp.log1p(-(2.0 ** (-5.0 - jnp.arange(H, dtype=F32))))
    idx = jnp.arange(C, dtype=F32)
    rel = idx[:, None] - idx[None, :]
    decay_in = jnp.where(rel[None] >= 0, jnp.exp(jnp.maximum(rel, 0.0)[None] * log_g[:, None, None]), 0.0)
    decay_q = jnp.exp((idx + 1.0)[:, None] * log_g[None, :])
    decay_k = jnp.exp((C - 1.0 - idx)[:, None] * log_g[None, :])
    decay_c = jnp.exp(C * log_g)

    def to_chunks(t):
        return t.reshape(B, nc, C, H, t.shape[-1]).swapaxes(0, 1)

    def step(s, inp):
        qi, ki, vi = inp
        scores = jnp.einsum('bnhd,bmhd->bhnm', qi, ki) * decay_in[None]
        o = (jnp.einsum('bhnm,bmhe->bnhe', scores, vi)
             + jnp.einsum('bnhd,bhde->bnhe', qi, s) * decay_q[None, :, :, None])
        s = (decay_c[None, :, None, None] * s
             + jnp.einsum('bmhd,bmhe->bhde', ki * decay_k[None, :, :, None], vi))
        return s, o

    s_final, o = lax.scan(step, s0.astype(F32), (to_chunks(q), to_chunks(k), to_chunks(v)))
    return o.swapaxes(0, 1).reshape(B, L, H, DV), s_final

def retention_mixer(xn, pos, s0, w_in, w_out):
    B, L, _ = xn.shape
    proj = xn @ w_in
    q = proj[..., :RET_QK].reshape(B, L, H_RET, DK_RET)
    k = proj[..., RET_QK:2 * RET_QK].reshape(B, L, H_RET, DK_RET)
    v = proj[..., 2 * RET_QK:2 * RET_QK + RET_V].reshape(B, L, H_RET, DV_RET).astype(F32)
    g = proj[..., 2 * RET_QK + RET_V:].astype(F32)
    q = rotary(q, pos)
    k = rotary(k, pos) * (DK_RET ** -0.5)
    o, s_new = retention_scan(q, k, v, s0)
    mu = jnp.mean(o, axis=-1, keepdims=True)
    var = jnp.mean(jnp.square(o - mu), axis=-1, keepdims=True)
    o = (o - mu) * lax.rsqrt(var + GN_EPS)
    y = (jax.nn.silu(g) * o.reshape(B, L, RET_V)).astype(xn.dtype) @ w_out
    return y, s_new

def sb_project(xn, w_qkv):
    B, L, _ = xn.shape
    qkv = (xn @ w_qkv).reshape(B, L, 3, H_SB, HD_SB)
    return qkv[:, :, 0], qkv[:, :, 1], qkv[:, :, 2]

def sb_block(q, k, v, q_pos, k_pos):
    z = jnp.einsum('bqhd,bkhd->bhqk', q.astype(F32), k.astype(F32)) * (HD_SB ** -0.5)
    valid = (k_pos[None, :] < q_pos[:, None])[None, None]
    log_1m = jnp.where(valid, jax.nn.log_sigmoid(-z), 0.0)
    log_a = jax.nn.log_sigmoid(z) + lax.cumsum(log_1m, axis=3, reverse=True) - log_1m
    a = jnp.where(valid, jnp.exp(log_a), 0.0)
    return jnp.einsum('bhqk,bkhd->bqhd', a, v.astype(F32)).astype(q.dtype)

def sb_prompt(q, k, v):
    B, S, H, D = q.shape
    nb = S // QBLOCK
    pos = jnp.arange(S)
    qb = q.reshape(B, nb, QBLOCK, H, D).swapaxes(0, 1)
    pb = pos.reshape(nb, QBLOCK)
    ob = lax.map(lambda args: sb_block(args[0], k, v, args[1], pos), (qb, pb))
    return ob.swapaxes(0, 1).reshape(B, S, H, D)

def setup_inputs(seed: int = 0) -> dict:
    key = jax.random.key(seed)
    ks = jax.random.split(key, 24)

    def nrm(k, shape, scale):
        return jax.random.normal(k, shape, F32) * scale

    def gain(k, shape):
        return 1.0 + 0.02 * jax.random.normal(k, shape, F32)

    return {
        'x_prompt': nrm(ks[0], (BATCH, SEQ, D_MODEL), 1.0),
        'x_sample': nrm(ks[1], (DEC_BATCH, DEC_SEQ, D_MODEL), 1.0),
        'p_prompt': nrm(ks[2], (DEPTH, BATCH, SEQ, PLE_DIM), 1.0),
        'p_sample': nrm(ks[3], (DEPTH, DEC_BATCH, DEC_SEQ, PLE_DIM), 1.0),
        'state_ret': nrm(ks[4], (N_RET_LAYERS, DEC_BATCH, H_RET, DK_RET, DV_RET), 0.5),
        'cache_sb_k': nrm(ks[5], (N_SB_LAYERS, DEC_BATCH, PAST_LEN, H_SB, HD_SB), 1.0),
        'cache_sb_v': nrm(ks[6], (N_SB_LAYERS, DEC_BATCH, PAST_LEN, H_SB, HD_SB), 1.0),
        'norm_ffn_a': gain(ks[7], (DEPTH, D_MODEL)),
        'w_ffn_a_gu': nrm(ks[8], (DEPTH, D_MODEL, 2 * D_FF), D_MODEL ** -0.5),
        'w_ffn_a_down': nrm(ks[9], (DEPTH, D_FF, D_MODEL), D_FF ** -0.5),
        'norm_mix': gain(ks[10], (DEPTH, D_MODEL)),
        'ret_w_in': nrm(ks[11], (N_RET_LAYERS, D_MODEL, RET_IN), D_MODEL ** -0.5),
        'ret_w_out': nrm(ks[12], (N_RET_LAYERS, RET_V, D_MODEL), RET_V ** -0.5),
        'sb_w_qkv': nrm(ks[13], (N_SB_LAYERS, D_MODEL, 3 * H_SB * HD_SB), D_MODEL ** -0.5),
        'sb_w_out': nrm(ks[14], (N_SB_LAYERS, H_SB * HD_SB, D_MODEL), (H_SB * HD_SB) ** -0.5),
        'norm_ffn_b': gain(ks[15], (DEPTH, D_MODEL)),
        'w_ffn_b_gu': nrm(ks[16], (DEPTH, D_MODEL, 2 * D_FF), D_MODEL ** -0.5),
        'w_ffn_b_down': nrm(ks[17], (DEPTH, D_FF, D_MODEL), D_FF ** -0.5),
        'norm_ple': gain(ks[18], (DEPTH, D_MODEL)),
        'ple_w_gate': nrm(ks[19], (DEPTH, D_MODEL, D_MODEL), D_MODEL ** -0.5),
        'ple_w_proj': nrm(ks[20], (DEPTH, PLE_DIM, D_MODEL), PLE_DIM ** -0.5),
        'norm_final': gain(ks[21], (D_MODEL,)),
    }

def reference(x_prompt, x_sample, p_prompt, p_sample, state_ret, cache_sb_k, cache_sb_v,
              norm_ffn_a, w_ffn_a_gu, w_ffn_a_down, norm_mix, ret_w_in, ret_w_out,
              sb_w_qkv, sb_w_out, norm_ffn_b, w_ffn_b_gu, w_ffn_b_down,
              norm_ple, ple_w_gate, ple_w_proj, norm_final):
    Bp, Sp, _ = x_prompt.shape
    Ls = x_sample.shape[1]
    past = cache_sb_k.shape[2]
    pos_p = jnp.arange(Sp)
    pos_s = past + jnp.arange(Ls)
    k_pos_s = jnp.arange(past + Ls)

    hp, hs = x_prompt, x_sample
    ret_p, ret_s, kp_l, vp_l, ks_l, vs_l = [], [], [], [], [], []
    for i in range(DEPTH):
        j = i // 2
        hp = half_swiglu(hp, norm_ffn_a[i], w_ffn_a_gu[i], w_ffn_a_down[i])
        hs = half_swiglu(hs, norm_ffn_a[i], w_ffn_a_gu[i], w_ffn_a_down[i])
        xn_p = rmsnorm(hp, norm_mix[i])
        xn_s = rmsnorm(hs, norm_mix[i])
        if i % 2 == 0:
            s0 = jnp.zeros((Bp, H_RET, DK_RET, DV_RET), F32)
            yp, sp = retention_mixer(xn_p, pos_p, s0, ret_w_in[j], ret_w_out[j])
            ys, ss = retention_mixer(xn_s, pos_s, state_ret[j], ret_w_in[j], ret_w_out[j])
            ret_p.append(sp)
            ret_s.append(ss)
        else:
            qp, kp, vp = sb_project(xn_p, sb_w_qkv[j])
            op = sb_prompt(qp, kp, vp)
            yp = op.reshape(Bp, Sp, H_SB * HD_SB) @ sb_w_out[j]
            qs, kn, vn = sb_project(xn_s, sb_w_qkv[j])
            k_all = jnp.concatenate([cache_sb_k[j].astype(kn.dtype), kn], axis=1)
            v_all = jnp.concatenate([cache_sb_v[j].astype(vn.dtype), vn], axis=1)
            os_ = sb_block(qs, k_all, v_all, pos_s, k_pos_s)
            ys = os_.reshape(os_.shape[0], Ls, H_SB * HD_SB) @ sb_w_out[j]
            kp_l.append(kp)
            vp_l.append(vp)
            ks_l.append(kn)
            vs_l.append(vn)
        hp = hp + yp.astype(hp.dtype)
        hs = hs + ys.astype(hs.dtype)
        hp = half_swiglu(hp, norm_ffn_b[i], w_ffn_b_gu[i], w_ffn_b_down[i])
        hs = half_swiglu(hs, norm_ffn_b[i], w_ffn_b_gu[i], w_ffn_b_down[i])
        hp = ple_add(hp, p_prompt[i], norm_ple[i], ple_w_gate[i], ple_w_proj[i])
        hs = ple_add(hs, p_sample[i], norm_ple[i], ple_w_gate[i], ple_w_proj[i])

    y_prompt = rmsnorm(hp, norm_final)
    y_sample = rmsnorm(hs, norm_final)
    state_ret_prompt = jnp.stack(ret_p)
    state_ret_sample = jnp.stack(ret_s)
    sb_k_prompt = jnp.stack(kp_l)
    sb_v_prompt = jnp.stack(vp_l)
    sb_k_sample = jnp.stack(ks_l)
    sb_v_sample = jnp.stack(vs_l)
    return (y_prompt, y_sample, state_ret_prompt, state_ret_sample,
            sb_k_prompt, sb_v_prompt, sb_k_sample, sb_v_sample)


_drawn_inputs = setup_inputs


def setup_inputs(seed=0):
    import zlib

    import numpy as np

    out = dict(_drawn_inputs(seed))
    spreads = {}
    factors = {'norm_ffn_a': 4.548,
     'norm_ffn_b': 6.433,
     'norm_ple': 64.0,
     'norm_final': 7.512,
     'cache_sb_k': 8.0,
     'cache_sb_v': 4.305}
    for name, (base, spread) in spreads.items():
        noise = np.random.default_rng([zlib.crc32(name.encode()), seed]).standard_normal(out[name].shape)
        drawn = base * np.exp(spread * noise) if base else spread * noise
        out[name] = __import__('jax').numpy.asarray(drawn.astype(out[name].dtype))
    for name, factor in factors.items():
        out[name] = (out[name] * factor).astype(out[name].dtype)
    return out
```

```python
import concourse.bass as bass
from concourse import mybir
from contextlib import ExitStack

P = 128
D = 1024
KT = D // P
SEQ, STREAMS, STEP = 512, 8, 16
TOK = SEQ + STREAMS * STEP
TT = TOK // P
HALF = TOK // 2
H_RET, DV = 8, 256
H_SB, HD = 16, 64
PAIRS = H_SB * HD // P
D_FF = 2816
PIECES = (8, 8, 6)
assert sum(PIECES) * P == D_FF
FFN_SLOTS = sum(2 * nf + KT for nf in PIECES)
RET_SLOTS, SB_SLOTS, PLE_SLOTS = 64, 32, 10
N_SLOTS = 4 * FFN_SLOTS + RET_SLOTS + SB_SLOTS + 2 * PLE_SLOTS
CREDIT = 4
EPS, GN_EPS = 1e-6, 1e-5
ZC = 1536
ZB = {0: (0, 0, 512), 1: (512, 128, 384), 3: (896, 384, 128), 2: (1024, 256, 256)}
Z_PAST, Z_NEW = 1280, 1408

RET_USES = []
for _h in range(2):
    RET_USES += [f"q{_h}"] + (["TO00", "TO01"] if _h else []) + [f"k{_h}", f"v{_h}0", f"Tk{_h}", f"v{_h}1",
                 f"Tv{_h}0", f"SC{_h}", f"g{_h}0", f"Tv{_h}1", f"g{_h}1", f"KV{_h}", f"OS{_h}", f"OP{_h}",
                 f"SS{_h}0", f"SS{_h}1"]
RET_USES += ["TO10", "TO11"] + [f"w{d}" for d in range(KT)]
SB_USES = ["q0", "k0", "v0", "T0", "ZA0", "ZB0"]
for _j in range(4):
    _n = _j + 1 if _j < 3 else None
    SB_USES += [f"q{_n}"] * (_n is not None) + [f"RA{_j}"] + [f"k{_n}"] * (_n is not None) + [f"RB{_j}", f"AA{_j}"]
    SB_USES += [f"v{_n}", f"T{_n}", f"ZA{_n}"] if _n is not None else []
    SB_USES += [f"AB{_j}"] + [f"ZB{_n}"] * (_n is not None)
SB_USES += [f"w{d}" for d in range(KT)]
SB_UNITS = [u for u in SB_USES if u[0] not in "ZR"]


class At:

    def __init__(self, phases):
        self.of = []
        n = fill = unit = fed = g = ple = 0
        for i, ph in enumerate(phases):
            self.of.append(dict(i=i, kind=ph, n=n, fill=fill, unit=unit, fed=fed, g=g, ple=ple, norm=i,
                                last=i == len(phases) - 1,
                                split_p=ph == "ffn" and phases[i + 1:i + 2] == ["ple"],
                                mixed=phases[i - 1] if i and phases[i - 1] in ("ret", "sb") else None))
            slots = {"ffn": FFN_SLOTS, "ret": RET_SLOTS, "sb": SB_SLOTS, "ple": PLE_SLOTS}[ph]
            fills = {"ffn": FFN_SLOTS, "ret": 4 * len(RET_USES), "sb": 2 * len(SB_USES), "ple": 16}[ph]
            units = {"ffn": FFN_SLOTS, "ret": 4 * len(RET_USES), "sb": 2 * len(SB_UNITS), "ple": 16}[ph]
            n, fill, unit, fed = n + slots, fill + fills, unit + units + 1, fed + KT
            g += sum(PIECES) * (ph == "ffn")
            ple += ph == "ple"
        self.n, self.fill, self.unit, self.fed = n, fill, unit, fed


def trunk(nc, phases, xT, pT, gains, wst, ones_d, ident_d, negtri_d, cs_d, dec_d, rmask_d, smask_d, gpow_d,
          bmask_d, bcap_d, st_d, kc_d, vc_d, y_o, stp_o, sts_o, k_o, v_o):
    F, R = mybir.dt.float32, mybir.dt.float32r
    ALU, ACT = mybir.AluOpType, mybir.ActivationFunctionType
    at = At(phases)
    plan = at.of
    kinds = set(phases)
    ctx = ExitStack()
    with ctx:
        def sb(name, shape, dt=F, on=ctx):
            return on.enter_context(nc.sbuf_tensor(name, shape, dt))

        x = sb("x", [P, KT, TOK])
        x_hi = sb("x_hi", [P, KT, TOK], R)
        x_lo = sb("x_lo", [P, KT, TOK], R)
        raw = sb("raw", [P, 4, D])
        w_hi = sb("w_hi", [P, 2, D], R)
        w_lo = sb("w_lo", [P, 2, D], R)
        sq = sb("sq", [P, 2, TOK])
        ssum = sb("ssum", [P, TOK])
        rstd = sb("rstd", [P, TOK])
        scr = sb("scr", [P, 4, TOK])
        gain = sb("gain", [P, 9, KT])
        ones = sb("ones", [P, P])
        ident = sb("ident", [P, P])
        with ExitStack() as s:
            g_hi = sb("g_hi", [P, 8, TOK], R, s)
            g_lo = sb("g_lo", [P, 8, TOK], R, s)
            proj = sb("proj", [P, KT, TOK], F, s)
            p_raw = sb("p_raw", [P, 2, TOK], F, s)
            p_hi = sb("p_hi", [P, 2, TOK], R, s)
            p_lo = sb("p_lo", [P, 2, TOK], R, s)
        y_hi = sb("y_hi", [P, 4, TOK], R)
        y_lo = sb("y_lo", [P, 4, TOK], R)
        with ExitStack() as s:
            cs = sb("cs", [P, 2, TOK], F, s)
            rd = sb("rd", [P, 2, TOK], F, s)
            rmask = sb("rmask", [P, TT, P], F, s)
            smask = sb("smask", [P, STREAMS], F, s)
            gpow = sb("gpow", [P, H_RET, 2], F, s)
            qf = sb("qf", [P, TOK], F, s)
            kf = sb("kf", [P, TOK], F, s)
            kn = sb("kn", [P, TT, P], F, s)
            km = sb("km", [P, STREAMS, P], F, s)
            qm = sb("qm", [P, STREAMS * (P + STEP)], F, s)
            vt_o = sb("vt_o", [P, 2 * TOK], F, s)
            vn = sb("vn", [P, TT, DV], F, s)
            sc = sb("sc", [P, TT, P], F, s)
            s0 = sb("s0", [P, STREAMS, DV], F, s)
            sp_ = sb("sp_", [P, 4, DV], F, s)
            stp = sb("stp", [P, DV], F, s)
            sg = sb("sg", [P, 2, TOK], F, s)
            bst = sb("bst", [P, TT, 6], F, s)
            mv = sb("mv", [P, TT, 2], F, s)
            gn = sb("gn", [P, 5, TT], F, s)
        with ExitStack() as s:
            negtri = sb("negtri", [P, 2, P], F, s)
            tri = sb("tri", [P, 2, P], R, s)
            bmask = sb("bmask", [P, 2, P], F, s)
            bcap = sb("bcap", [P, 2, P], F, s)
            bq = sb("bq", [P, 2, TOK], F, s)
            bk = sb("bk", [P, 2, TOK], F, s)
            bvt = sb("bvt", [P, TOK], F, s)
            bv = sb("bv", [P, 2, TT, P], F, s)
            kc = sb("kc", [P, 2, STREAMS, P], F, s)
            vc = sb("vc", [P, 2, STREAMS, P], F, s)
            e = sb("e", [P, 2, ZC], F, s)
            l_hi = sb("l_hi", [P, 2, ZC], R, s)
            l_lo = sb("l_lo", [P, 2, ZC], R, s)
        ps = ctx.enter_context(nc.psum_tensor("ps", [P, 8, 512], F))

        def sem(name):
            return ctx.enter_context(nc.semaphore(name))

        s_raw = [sem(f"s_raw{r}") for r in range(4)]
        s_const, s_x, s_p = sem("s_const"), sem("s_x"), sem("s_p")
        s_ret_in, s_dec, s_s0 = sem("s_ret_in"), sem("s_dec"), sem("s_s0")
        s_sb_in, s_kv = sem("s_sb_in"), [sem("s_kv0"), sem("s_kv1")]
        s_y_out = [sem(f"s_y_out{k}") for k in range(4)]
        s_stp_out, s_sts_out = sem("s_stp_out"), sem("s_sts_out")
        s_k_out, s_v_out = sem("s_k_out"), sem("s_v_out")
        s_fill = sem("s_fill")
        s_ss = sem("s_ss")
        s_whi, s_xhi, s_sq, s_root = sem("s_whi"), sem("s_xhi"), sem("s_sq"), sem("s_root")
        s_silu, s_sig, s_gate, s_tri = sem("s_silu"), sem("s_sig"), sem("s_gate"), sem("s_tri")
        s_ghi, s_phi, s_ohi = sem("s_ghi"), sem("s_phi"), sem("s_ohi")
        s_swap, s_stp, s_sts, s_groot, s_yhi = sem("s_swap"), sem("s_stp"), sem("s_sts"), sem("s_groot"), sem("s_yhi")
        s_soft, s_lhi, s_att = sem("s_soft"), sem("s_lhi"), sem("s_att")
        s_free = sem("s_free")
        s_wlo, s_xlo, s_rstd, s_glo, s_plo = sem("s_wlo"), sem("s_xlo"), sem("s_rstd"), sem("s_glo"), sem("s_plo")
        s_sr, s_pm, s_xup, s_out = sem("s_sr"), sem("s_pm"), sem("s_xup"), sem("s_out")
        s_rt, s_rot, s_kvs, s_aggr, s_gn, s_ylo = (sem(n) for n in ("s_rt", "s_rot", "s_kvs", "s_aggr", "s_gn", "s_ylo"))
        s_sp, s_llo, s_cap = sem("s_sp"), sem("s_llo"), sem("s_cap")
        s_apart = sem("s_apart")
        s_ssum, s_rd, s_km, s_qm = sem("s_ssum"), sem("s_rd"), sem("s_km"), sem("s_qm")
        s_stp_kept, s_k_kept, s_v_kept = sem("s_stp_kept"), sem("s_k_kept"), sem("s_v_kept")

        def apart(eng):
            eng.sem_inc(s_apart, 1)

        def halves(ap):
            return ap.rearrange("p (b c) -> p b c", b=2)

        def acc(u):
            return ps[:, 2 * u:2 * u + 2, 0:HALF]

        def flat(u):
            return ps[:, 2 * u:2 * u + 2, :].rearrange("p b c -> p (b c)")

        def zf(hh):
            return ps[:, 2 + 3 * hh:5 + 3 * hh, :].rearrange("p b c -> p (b c)")

        def z3(hh):
            return ps[:, 2 + 3 * hh:5 + 3 * hh, :]

        def landed(c, m, i=0, per=0):
            n = c["n"] + m
            return n % 4, 16 * (n // 4 + 1) + (4 * per) * i

        def slot_cols(kind, m):
            if kind == "ffn" and m >= FFN_SLOTS - KT:
                return PIECES[2] * P
            return D

        def next_cols(c, m):
            total = {"ffn": FFN_SLOTS, "ret": RET_SLOTS, "sb": SB_SLOTS, "ple": PLE_SLOTS}[c["kind"]]
            if m + 2 < total:
                return slot_cols(c["kind"], m + 2)
            return None if c["last"] else D

        block = ctx.enter_context(nc.Block())

        @block.sync
        def _(sp):
            sp.dma_start(gain[:], gains).then_inc(s_const, 16)
            sp.dma_start(ones[:], ones_d).then_inc(s_const, 16)
            sp.dma_start(ident[:], ident_d).then_inc(s_const, 16)
            for k in range(KT):
                sp.dma_start(x[:, k, :], xT[k]).then_inc(s_x, 16)

            def load(c, m, i=0, per=0, cols=D):
                n = c["n"] + m + per * i
                r, _ = landed(c, m)
                sp.wait_ge(s_wlo, CREDIT + n - 3)
                sp.dma_start(raw[:, r, 0:cols], wst[n, :, 0:cols]).then_inc(s_raw[r], 16)

            for c in plan:
                if c["kind"] == "ffn":
                    with sp.Fori(0, (FFN_SLOTS - KT) // 4) as i:
                        for j in range(4):
                            load(c, j, i, 4)
                    with sp.Fori(0, KT // 4) as i:
                        for j in range(4):
                            load(c, FFN_SLOTS - KT + j, i, 4, PIECES[2] * P)
                elif c["kind"] in ("ret", "sb"):
                    with sp.Fori(0, {"ret": RET_SLOTS, "sb": SB_SLOTS}[c["kind"]] // 4) as i:
                        for j in range(4):
                            load(c, j, i, 4)
                else:
                    for m in range(PLE_SLOTS):
                        load(c, m)
            for d in range(KT):
                sp.wait_ge(s_out, CREDIT + d + 1)
                sp.dma_start(y_o[d], scr[:, d % 4, :]).then_inc(s_y_out[d % 4], 16)
            for s in s_y_out:
                sp.wait_ge(s, 16 * KT // 4)

        @block.tensor
        def _(pe):
            for s in (s_fill, s_ss):
                pe.sem_inc(s, CREDIT)

            def mm3(out, wh, wl, xh, xl, start, stop):
                for q, (a, b) in enumerate(((wh, xh), (wh, xl), (wl, xh))):
                    for h in range(2):
                        last = nc.tensor.matmul(out[:, h, :], a, b[:, HALF * h:HALF * (h + 1)],
                                                start=start and q == 0, stop=stop and q == 2,
                                                skip_group_check=True)
                return last

            def project(c, m, i, per, u, blocks, src_hi, src_lo, before=None):
                p = (c["n"] + m) % 2
                for b, (wb, xb) in enumerate(blocks):
                    if before is not None:
                        before(b)
                    last = mm3(acc(u), w_hi[:, p, wb * P:(wb + 1) * P], w_lo[:, p, wb * P:(wb + 1) * P],
                               src_hi[:, xb, :], src_lo[:, xb, :], b == 0, b == len(blocks) - 1)
                last.then_inc(s_fill, 1)

            def sum_squares(c):
                u = c["unit"] % 4
                pe.wait_ge(s_ssum, CREDIT + c["fed"] + KT)
                for h in range(2):
                    last = nc.tensor.matmul(acc(u)[:, h, :], ones[:], ssum[:, HALF * h:HALF * (h + 1)],
                                            start=True, stop=True)
                last.then_inc(s_ss, 1)

            def fed(c):
                return lambda b: pe.wait_ge(s_xlo, CREDIT + c["fed"] + b + 1)

            def ffn(c):
                def step(m, i, per, first=False):
                    n, unit = c["n"] + m + per * i, c["unit"] + 1 + m + per * i
                    pe.wait_ge(s_wlo, CREDIT + n + 1)
                    pe.wait_ge(s_free, CREDIT + (unit - 3 if m > 2 or not first else c["unit"]))

                m = 0
                for nf_at, nf in enumerate(PIECES):
                    def body(i, m=m):
                        for j in range(4):
                            first = isinstance(i, int) and i == 0 and nf_at == 0
                            step(m + j, i, 4, first)
                            project(c, m + j, i, 4, (c["unit"] + 1 + m + j) % 4, [(k, k) for k in range(KT)],
                                    x_hi, x_lo, fed(c) if first and j == 0 else None)
                            if first and j == 1:
                                sum_squares(c)
                    lo = 0
                    if nf_at == 0:
                        body(0)
                        lo = 1
                    with pe.Fori(lo, nf // 2) as i:
                        body(i)
                    m += 2 * nf
                    done = c["g"] + sum(PIECES[:nf_at + 1])

                    def ready(b, nf=nf, done=done):
                        if b == 0:
                            pe.wait_ge(s_glo, CREDIT + done - 1)
                        if b == nf - 1:
                            pe.wait_ge(s_glo, CREDIT + done)
                    with pe.Fori(0, KT // 4) as i:
                        for j in range(4):
                            step(m + j, i, 4)
                            project(c, m + j, i, 4, (c["unit"] + 1 + m + j) % 4, [(k, k) for k in range(nf)],
                                    g_hi, g_lo, ready if j == 0 else None)
                    m += KT

            def ple(c):
                unit = c["unit"] + 1
                pe.wait_ge(s_plo, CREDIT + c["ple"] + 1)
                for m in range(2):
                    pe.wait_ge(s_wlo, CREDIT + c["n"] + m + 1)
                    for t in range(4):
                        if m == 0 and t == 3:
                            sum_squares(c)
                        pe.wait_ge(s_free, CREDIT + unit - 4 + 1)
                        project(c, m, 0, 0, unit % 4, [(2 * t, 0), (2 * t + 1, 1)], p_hi, p_lo)
                        unit += 1
                for m in range(2, PLE_SLOTS):
                    pe.wait_ge(s_wlo, CREDIT + c["n"] + m + 1)
                    pe.wait_ge(s_free, CREDIT + unit - 4 + 1)
                    project(c, m, 0, 0, unit % 4, [(k, k) for k in range(KT)], x_hi, x_lo,
                            fed(c) if m == 2 else None)
                    unit += 1

            def ret(c):
                pe.wait_ge(s_free, CREDIT + c["unit"] - 4 + 1)
                sum_squares(c)
                o = c["unit"] + 1
                uses = RET_USES

                def body(i):
                    for idx, use in enumerate(uses):
                        u = (o + idx) % 4
                        pe.wait_ge(s_free, CREDIT + (o + idx + len(uses) * i - (2 if idx < 2 else 4) + 1))
                        if use[0] == "w":
                            d = int(use[1:])
                            slot = 12 + d // 2
                            if d == 0:
                                pe.wait_ge(s_ylo, CREDIT + 4 * i + 3)
                            if d % 2 == 0:
                                pe.wait_ge(s_wlo, CREDIT + c["n"] + slot + 16 * i + 1)

                            def last_y(b, d=d):
                                if d == 0 and b == 3:
                                    pe.wait_ge(s_ylo, CREDIT + 4 * i + 4)
                            project(c, slot, i, 16, u, [(4 * (d % 2) + k, k) for k in range(4)], y_hi, y_lo, last_y)
                            continue
                        hh = int(use[2]) if use[:2] in ("Tk", "Tv", "SC", "KV", "SS", "OS", "OP", "TO") else int(use[1])
                        h = 2 * i + hh
                        if use[0] in "qkvg" and use[:2] != "Tk":
                            slot = 6 * hh + {"q": 0, "k": 1, "v": 2, "g": 4}[use[0]] + (int(use[2]) if len(use) > 2 else 0)
                            pe.wait_ge(s_wlo, CREDIT + c["n"] + slot + 16 * i + 1)
                            project(c, slot, i, 16, u, [(k, k) for k in range(KT)], x_hi, x_lo,
                                    fed(c) if use == "q0" else None)
                            continue
                        f = flat(u)
                        if use[:2] == "Tk":
                            pe.wait_ge(s_rot, CREDIT + 2 * h + 2)
                            for t in range(TT):
                                last = nc.tensor.transpose(f[:, t * P:(t + 1) * P], kf[:, t * P:(t + 1) * P], ident[:])
                        elif use[:2] == "Tv":
                            j = int(use[3])
                            pe.wait_ge(s_free, CREDIT + o + uses.index(f"v{hh}{j}") + len(uses) * i + 1)
                            for t in range(TT):
                                last = nc.tensor.transpose(
                                    f[:, t * P:(t + 1) * P], vt_o[:, j * TOK + t * P:j * TOK + (t + 1) * P], ident[:])
                        elif use[:2] == "SC":
                            for t in range(TT):
                                last = nc.tensor.matmul(f[:, t * P:(t + 1) * P], kf[:, t * P:(t + 1) * P],
                                                        qf[:, t * P:(t + 1) * P], start=True, stop=True)
                        elif use[:2] == "KV":
                            pe.wait_ge(s_free, CREDIT + o + uses.index(f"Tv{hh}1") + len(uses) * i + 1)
                            for t in range(4):
                                last = nc.tensor.matmul(f[:, t * DV:(t + 1) * DV], kn[:, t, :], vn[:, t, :],
                                                        start=True, stop=True)
                        elif use[:2] == "OS":
                            pe.wait_ge(s_qm, CREDIT + h + 1)
                            pe.wait_ge(s_s0, 16 * (1) + 16 * h)
                            for s in range(STREAMS):
                                nc.tensor.matmul(f[:, 0:DV], qm[:, s * P:(s + 1) * P], s0[:, s, :],
                                                 start=s == 0, stop=False)
                            last = nc.tensor.matmul(f[:, 0:DV], sc[:, 4, :], vn[:, 4, :], start=False, stop=True)
                        elif use[:2] == "OP":
                            pe.wait_ge(s_kvs, CREDIT + 3 * h + 3)
                            for t in range(4):
                                last = nc.tensor.matmul(f[:, t * DV:(t + 1) * DV], sc[:, t, :], vn[:, t, :],
                                                        start=True, stop=t == 0)
                                if t:
                                    last = nc.tensor.matmul(f[:, t * DV:(t + 1) * DV], qf[:, t * P:(t + 1) * P],
                                                            sp_[:, t - 1, :], start=False, stop=True)
                        elif use[:2] == "SS":
                            pe.wait_ge(s_km, CREDIT + h + 1)
                            half = int(use[3])
                            for s in range(4):
                                last = nc.tensor.matmul(f[:, s * DV:(s + 1) * DV], km[:, 4 * half + s, :], vn[:, 4, :],
                                                        start=True, stop=True)
                        elif use[:2] == "TO":
                            j = int(use[3])
                            pe.wait_ge(s_free, CREDIT + o + uses.index(f"OP{hh}") + len(uses) * i + 1)
                            for t in range(TT):
                                last = nc.tensor.transpose(f[:, t * P:(t + 1) * P],
                                                           vt_o[:, t * DV + j * P:t * DV + (j + 1) * P], ident[:])
                        last.then_inc(s_fill, 1)

                with pe.Fori(0, 3) as i:
                    body(i)
                body(3)

            def stick(c):
                pe.wait_ge(s_free, CREDIT + c["unit"])
                sum_squares(c)
                o = c["unit"] + 1
                u0 = 0

                def body(i):
                    for idx, use in enumerate(SB_USES):
                        j = int(use[-1])
                        pair = 4 * i + j
                        par = j % 2
                        k0 = use[0]
                        if k0 not in "ZR":
                            ui = SB_UNITS.index(use)
                            pe.wait_ge(s_free, CREDIT + o + ui + len(SB_UNITS) * i)
                        f = flat(u0)
                        if k0 in "qkv":
                            slot = 3 * j + "qkv".index(k0)
                            pe.wait_ge(s_wlo, CREDIT + c["n"] + slot + 16 * i + 1)
                            project(c, slot, i, 16, u0, [(k, k) for k in range(KT)], x_hi, x_lo,
                                    fed(c) if use == "q0" else None)
                            continue
                        if k0 == "w":
                            slot = 12 + j // 2
                            if j % 2 == 0:
                                pe.wait_ge(s_wlo, CREDIT + c["n"] + slot + 16 * i + 1)
                            project(c, slot, i, 16, u0, [(4 * (j % 2) + k, k) for k in range(4)], y_hi, y_lo)
                            continue
                        if k0 == "T":
                            pe.wait_ge(s_free, CREDIT + o + SB_UNITS.index(f"v{j}") + len(SB_UNITS) * i + 1)
                            for t in range(TT):
                                last = nc.tensor.transpose(f[:, t * P:(t + 1) * P], bvt[:, t * P:(t + 1) * P], ident[:])
                            last.then_inc(s_fill, 1)
                            continue
                        hh = "AB".index(use[1])
                        rows = slice(HD * hh, HD * (hh + 1))
                        head = 2 * pair + hh
                        z = zf(hh)
                        if k0 == "Z":
                            pe.wait_ge(s_free, CREDIT + o + SB_UNITS.index(f"k{j}") + len(SB_UNITS) * i + 1)
                            pe.wait_ge(s_att, CREDIT + head - 1)
                            if hh == 0:
                                pe.wait_ge(s_kv[par], 32 * (2 * i + j // 2 + 1))
                            for n, (b, (z0, q0, w)) in enumerate(ZB.items()):
                                nc.tensor.matmul(z[:, z0:z0 + w], bk[rows, par, b * P:(b + 1) * P], bq[rows, par, q0:q0 + w],
                                                 start=b != 3, stop=False, skip_group_check=True)
                            for s in range(STREAMS):
                                nc.tensor.matmul(z[:, Z_PAST + s * STEP:Z_PAST + (s + 1) * STEP], kc[rows, par, s, :],
                                                 bq[rows, par, SEQ + s * STEP:SEQ + (s + 1) * STEP],
                                                 start=False, stop=False, skip_group_check=True)
                            last = nc.tensor.matmul(z[:, Z_NEW:ZC], bk[rows, par, SEQ:TOK], bq[rows, par, SEQ:TOK],
                                                    start=False, stop=True, skip_group_check=True)
                        elif k0 == "R":
                            pe.wait_ge(s_llo, CREDIT + head + 1)
                            last = None
                            for src in (l_hi, l_lo):
                                for b, (z0, q0, w) in ZB.items():
                                    for b2 in range(b, 4):
                                        y0, p0, w2 = ZB[b2]
                                        nc.tensor.matmul(z[:, z0 + p0 - q0:z0 + w], tri[:, int(b2 > b), :],
                                                         src[:, hh, y0:y0 + w2], start=False, stop=False,
                                                         skip_group_check=True)
                                nc.tensor.matmul(z[:, Z_PAST:Z_NEW], tri[:, 0, :], src[:, hh, Z_PAST:Z_NEW],
                                                 start=False, stop=False, skip_group_check=True)
                                nc.tensor.matmul(z[:, Z_PAST:Z_NEW], tri[:, 1, :], src[:, hh, Z_NEW:ZC],
                                                 start=False, stop=False, skip_group_check=True)
                                last = nc.tensor.matmul(z[:, Z_NEW:ZC], tri[:, 0, :], src[:, hh, Z_NEW:ZC],
                                                        start=False, stop=src is l_lo, skip_group_check=True)
                        else:
                            pe.wait_ge(s_att, CREDIT + head + 1)
                            for b in range(4):
                                z0, q0, w = ZB[b]
                                nc.tensor.matmul(f[:, q0:SEQ], bv[:, par, b, :], e[:, hh, z0:z0 + w],
                                                 start=b == 0, stop=b == 3, skip_group_check=True)
                            nc.tensor.matmul(f[:, SEQ:TOK], bv[:, par, 4, :], e[:, hh, Z_NEW:ZC],
                                             start=True, stop=False, skip_group_check=True)
                            for s in range(STREAMS):
                                last = nc.tensor.matmul(f[:, SEQ + s * STEP:SEQ + (s + 1) * STEP], vc[:, par, s, :],
                                                        e[:, hh, Z_PAST + s * STEP:Z_PAST + (s + 1) * STEP],
                                                        start=False, stop=s == STREAMS - 1, skip_group_check=True)
                        last.then_inc(s_fill, 1)

                with pe.Fori(0, 2) as i:
                    body(i)

            pe.wait_ge(s_const, 48)
            for c in plan:
                {"ffn": ffn, "ret": ret, "sb": stick, "ple": ple}[c["kind"]](c)
            sum_squares(dict(unit=at.unit, fed=at.fed))

        @block.scalar
        def _(act):
            for s in (s_whi, s_xhi, s_sq, s_root, s_silu, s_sig, s_gate, s_tri, s_ghi, s_phi, s_ohi, s_swap,
                      s_stp, s_sts, s_groot, s_yhi, s_soft, s_lhi, s_att):
                act.sem_inc(s, CREDIT)

            def split_hi(c, m, i, per, fill):
                cols = next_cols(c, m)
                if cols is None:
                    return
                r, value = landed(c, m + 2)
                act.wait_ge(s_raw[r], value + (4 * per) * i)
                act.wait_ge(s_fill, CREDIT + fill)
                nc.scalar.activation(w_hi[:, (c["n"] + m) % 2, 0:cols], raw[:, r, 0:cols], ACT.Copy).then_inc(s_whi, 1)

            def feed(c_fed, norm, d, s, value, hi=True):
                act.wait_ge(s, CREDIT + value)
                if hi:
                    nc.scalar.activation(x_hi[:, d, :], x[:, d, :], ACT.Copy,
                                         scale=gain[:, norm, d:d + 1]).then_inc(s_xhi, 1)
                act.wait_ge(s_ssum, CREDIT + c_fed + d - 1)
                nc.scalar.activation(sq[:, d % 2, :], x[:, d, :], ACT.Square).then_inc(s_sq, 1)

            def root(c):
                act.wait_ge(s_free, CREDIT + c["unit"] + 1)
                nc.scalar.activation(scr[:, 1, :], scr[:, 0, :], ACT.Sqrt).then_inc(s_root, 1)

            def ffn(c):
                if c["mixed"] == "ret":
                    act.wait_ge(s_stp_kept, CREDIT + H_RET)
                    act.wait_ge(s_sts_out, 32 * H_RET)
                if c["mixed"] == "sb":
                    act.wait_ge(s_k_kept, CREDIT + PAIRS)
                    act.wait_ge(s_v_kept, CREDIT + PAIRS)
                m = 0
                o = c["unit"] + 1
                for nf_at, nf in enumerate(PIECES):
                    gbase = c["g"] + sum(PIECES[:nf_at])

                    def body(i, m=m, gbase=gbase, nf_at=nf_at):
                        first = isinstance(i, int) and i == 0 and nf_at == 0
                        if first:
                            for j in range(2):
                                split_hi(c, m + j, 0, 0, c["fill"] + m + j + 1)
                            root(c)
                        for j in range(4):
                            f = gbase + 2 * i + j // 2
                            if j >= 2 or not first:
                                if j % 2 == 0:
                                    split_hi(c, m + j, i, 4, c["fill"] + m + j + 4 * i + 1)
                            if j % 2 == 0:
                                act.wait_ge(s_free, CREDIT + o + m + j + 4 * i + 1)
                                nc.scalar.activation(scr[:, 2 + j // 2, :], scr[:, j // 2, :], ACT.Silu).then_inc(s_silu, 1)
                            else:
                                act.wait_ge(s_free, CREDIT + o + m + j + 4 * i + 1)
                                nc.scalar.activation(g_hi[:, 2 * i + j // 2, :], scr[:, j // 2, :], ACT.Copy).then_inc(s_ghi, 1)
                                if j >= 2 or not first:
                                    split_hi(c, m + j, i, 4, c["fill"] + m + j + 4 * i + 1)
                    lo = 0
                    if nf_at == 0:
                        body(0)
                        lo = 1
                    with act.Fori(lo, nf // 2) as i:
                        body(i)
                    m += 2 * nf
                    if nf_at == 0 and c["split_p"]:
                        act.wait_ge(s_p, 16 * (c["ple"] + 1))
                        nc.scalar.activation(p_hi[:], p_raw[:], ACT.Copy).then_inc(s_phi, 1)
                    if nf_at < 2:
                        with act.Fori(0, KT // 4) as i:
                            for j in range(4):
                                split_hi(c, m + j, i, 4, c["fill"] + m + j + 4 * i + 1)
                    else:
                        for d in range(KT):
                            split_hi(c, m + d, 0, 0, c["fill"] + m + d + 1)
                            feed(c["fed"] + KT, c["norm"] + 1, d, s_free, o + m + d + 1)
                    m += KT

            def ple(c):
                root(c)
                for m in range(2):
                    split_hi(c, m, 0, 0, c["fill"] + 4 * m + 4)
                for d in range(KT):
                    split_hi(c, 2 + d, 0, 0, c["fill"] + 8 + d + 1)
                    act.wait_ge(s_free, CREDIT + c["unit"] + 1 + 8 + d + 1)
                    act.wait_ge(s_xup, CREDIT + KT * c["ple"] + d - 1)
                    nc.scalar.activation(scr[:, 2 + d % 2, :], scr[:, d % 2, :], ACT.Sigmoid).then_inc(s_sig, 1)
                    if c["last"]:
                        if d:
                            feed(at.fed, 8, d - 1, s_xup, KT * c["ple"] + d, hi=False)
                if c["last"]:
                    feed(at.fed, 8, KT - 1, s_xup, KT * c["ple"] + KT, hi=False)
                else:
                    act.wait_ge(s_fill, CREDIT + c["fill"] + 16)
                    for d in range(KT):
                        feed(c["fed"] + KT, c["norm"] + 1, d, s_xup, KT * c["ple"] + d + 1)

            def ret(c):
                root(c)
                o = c["unit"] + 1
                uses = RET_USES
                n_u = len(uses)

                def body(i, last):
                    def fill(use):
                        return c["fill"] + uses.index(use) + n_u * i + 1

                    def free(use):
                        return o + uses.index(use) + n_u * i + 1

                    def to(hh):
                        for j in range(2):
                            act.wait_ge(s_free, CREDIT + free(f"TO{hh}{j}"))
                            nc.scalar.activation(y_hi[:, 2 * hh + j, :], scr[:, 2 + j, :], ACT.Copy).then_inc(s_yhi, 1)

                    for hh in range(2):
                        h = 2 * i + hh
                        for n, name in enumerate("qk"):
                            use = f"{name}{hh}"
                            act.wait_ge(s_free, CREDIT + free(use))
                            nc.scalar.activation(scr[0:64, 1, :], scr[64:128, 0, :], ACT.Copy).then_inc(s_swap, 1)
                            nc.scalar.activation(scr[64:128, 1, :], scr[0:64, 0, :], ACT.Copy).then_inc(s_swap, 1)
                            split_hi(c, 6 * hh + n, i, 16, fill(use))
                            if name == "q" and hh:
                                to(0)
                        for j in range(2):
                            split_hi(c, 6 * hh + 2 + j, i, 16, fill(f"v{hh}{j}"))
                        for j in range(2):
                            split_hi(c, 6 * hh + 4 + j, i, 16, fill(f"g{hh}{j}"))
                            act.wait_ge(s_free, CREDIT + free(f"g{hh}{j}"))
                            nc.scalar.activation(sg[:, j, :], sg[:, j, :], ACT.Silu).then_inc(s_gate, 1)
                        act.wait_ge(s_free, CREDIT + free(f"KV{hh}"))
                        act.wait_ge(s_stp_kept, CREDIT + h)
                        apart(act)
                        nc.scalar.activation(stp[:], sp_[:, 3, :], ACT.Copy,
                                             scale=gpow[:, h, 0:1]).then_inc(s_stp, 1)
                        act.wait_ge(s_gn, CREDIT + 7 * h + 2)
                        nc.scalar.activation(gn[:, 1, :], gn[:, 0, :], ACT.Sqrt).then_inc(s_groot, 1)
                        for half in range(2):
                            act.wait_ge(s_free, CREDIT + free(f"SS{hh}{half}"))
                            apart(act)
                            nc.scalar.activation(s0[:, 4 * half:4 * half + 4, :], s0[:, 4 * half:4 * half + 4, :], ACT.Copy,
                                                 scale=gpow[:, h, 1:2]).then_inc(s_sts, 1)
                    to(1)
                    for d in range(KT):
                        if d % 2:
                            split_hi(c, 12 + d // 2, i, 16, fill(f"w{d}"))
                        if last:
                            feed(c["fed"] + KT, c["norm"] + 1, d, s_free, free(f"w{d}"))

                act.wait_ge(s_ret_in, 64)
                with act.Fori(0, 3) as i:
                    body(i, False)
                body(3, True)

            def stick(c):
                act.wait_ge(s_sb_in, 48)
                nc.scalar.activation(tri[:], negtri[:], ACT.Copy).then_inc(s_tri, 1)
                root(c)
                o = c["unit"] + 1

                def body(i):
                    def fill(use):
                        return c["fill"] + SB_USES.index(use) + len(SB_USES) * i + 1

                    def free(use):
                        return o + SB_UNITS.index(use) + len(SB_UNITS) * i + 1

                    def soft(hh, j, k):
                        head = 8 * i + 2 * j + hh
                        if k == 0:
                            act.wait_ge(s_fill, CREDIT + fill(f"Z{'AB'[hh]}{j}"))
                            act.wait_ge(s_fill, CREDIT + (fill(f"A{'AB'[hh]}{j - 1}") if j else c["fill"] + len(SB_USES) * i))
                            nc.scalar.activation(e[:, hh, :], zf(hh), ACT.Abs).then_inc(s_soft, 1)
                            return
                        act.wait_ge(s_soft, CREDIT + 3 * head + k)
                        if k == 1:
                            nc.scalar.activation(e[:, hh, :], e[:, hh, :], ACT.Exp, scale=-1.0).then_inc(s_soft, 1)
                        else:
                            nc.scalar.activation(e[:, hh, :], e[:, hh, :], ACT.Ln, bias=1.0).then_inc(s_soft, 1)

                    def lhi(hh, j):
                        head = 8 * i + 2 * j + hh
                        act.wait_ge(s_sp, CREDIT + 3 * head + 3)
                        nc.scalar.activation(l_hi[:, hh, :], e[:, hh, :], ACT.Copy).then_inc(s_lhi, 1)

                    def att(hh, j):
                        head = 8 * i + 2 * j + hh
                        act.wait_ge(s_cap, CREDIT + 2 * head + 2)
                        nc.scalar.activation(e[:, hh, :], zf(hh), ACT.Exp).then_inc(s_att, 1)

                    def yhi(hh, j):
                        act.wait_ge(s_fill, CREDIT + fill(f"A{'AB'[hh]}{j}"))
                        rows = slice(HD * hh, HD * (hh + 1))
                        nc.scalar.activation(y_hi[rows, j, :], flat(0)[rows, 0:TOK], ACT.Copy).then_inc(s_ohi, 1)

                    def soft_both(j):
                        for hh in range(2):
                            for k in range(3):
                                soft(hh, j, k)
                            lhi(hh, j)

                    for m, name in enumerate("qkv"):
                        split_hi(c, m, i, 16, fill(f"{name}0"))
                    for k in range(3):
                        soft(0, 0, k)
                    lhi(0, 0)
                    for k in range(3):
                        soft(1, 0, k)
                    lhi(1, 0)
                    for j in range(4):
                        nxt = j < 3
                        if nxt:
                            split_hi(c, 3 * j + 3, i, 16, fill(f"q{j + 1}"))
                        att(0, j)
                        if nxt:
                            split_hi(c, 3 * j + 4, i, 16, fill(f"k{j + 1}"))
                        att(1, j)
                        yhi(0, j)
                        if nxt:
                            split_hi(c, 3 * j + 5, i, 16, fill(f"v{j + 1}"))
                            for k in range(3):
                                soft(0, j + 1, k)
                        yhi(1, j)
                        if nxt:
                            lhi(0, j + 1)
                            for k in range(3):
                                soft(1, j + 1, k)
                            lhi(1, j + 1)
                    for t in range(4):
                        split_hi(c, 12 + t, i, 16, fill(f"w{2 * t + 1}"))

                with act.Fori(0, 2) as i:
                    body(i)
                for d in range(KT):
                    feed(c["fed"] + KT, c["norm"] + 1, d, s_free, c["unit"] + 1 + 2 * len(SB_UNITS) - KT + d + 1)

            act.wait_ge(s_const, 48)
            for n in range(2):
                act.wait_ge(s_raw[n], 16)
                nc.scalar.activation(w_hi[:, n, :], raw[:, n, :], ACT.Copy).then_inc(s_whi, 1)
            for d in range(KT):
                act.wait_ge(s_x, 16 * KT)
                feed(0, 0, d, s_xup, 0)
            for c in plan:
                {"ffn": ffn, "ret": ret, "sb": stick, "ple": ple}[c["kind"]](c)
            root(dict(unit=at.unit))

        @block.gpsimd
        def _(pool):
            for s in (s_ssum, s_rd, s_km, s_qm, s_stp_kept, s_k_kept, s_v_kept):
                pool.sem_inc(s, CREDIT)

            def add_squares(fed, norm):
                for d in range(KT):
                    pool.wait_ge(s_sq, CREDIT + fed + d + 1)
                    if d == 0:
                        pool.wait_ge(s_ss, CREDIT + norm)
                        nc.gpsimd.tensor_copy(ssum[:], sq[:, 0, :]).then_inc(s_ssum, 1)
                    else:
                        pool.wait_ge(s_ssum, CREDIT + fed + d)
                        nc.gpsimd.tensor_tensor(ssum[:], ssum[:], sq[:, d % 2, :], ALU.add).then_inc(s_ssum, 1)

            def ffn(c):
                if c["split_p"]:
                    pool.wait_ge(s_fill, CREDIT + c["fill"])
                    pool.dma_start(p_raw[:], pT[c["ple"]].rearrange("k p t -> p k t")).then_inc(s_p, 16)

            def ret(c):
                o = c["unit"] + 1
                n_u = len(RET_USES)
                pool.wait_ge(s_fill, CREDIT + c["fill"])
                pool.dma_start(cs[:], cs_d).then_inc(s_ret_in, 16)
                pool.dma_start(rmask[:], rmask_d).then_inc(s_ret_in, 16)
                pool.dma_start(smask[:], smask_d).then_inc(s_ret_in, 16)
                pool.dma_start(gpow[:], gpow_d).then_inc(s_ret_in, 16)
                pool.dma_start(rd[:], dec_d[0]).then_inc(s_dec, 16)
                pool.dma_start(s0[:], st_d[0]).then_inc(s_s0, 16)
                nc.gpsimd.memset(qm[:], 0.0)
                pool.wait_ge(s_rstd, CREDIT + 5 * (c["norm"] + 1))

                def decay(h):
                    pool.wait_ge(s_dec, 16 * (h + 1))
                    nc.gpsimd.tensor_tensor(rd[:, 0, :], rd[:, 0, :], rstd[:], ALU.mult)
                    nc.gpsimd.tensor_tensor(rd[:, 1, :], rd[:, 1, :], rstd[:], ALU.mult).then_inc(s_rd, 1)

                decay(0)
                pool.wait_ge(s_ret_in, 64)

                def body(i, last):
                    for hh in range(2):
                        h = 2 * i + hh
                        pool.wait_ge(s_rot, CREDIT + 2 * h + 1)
                        apart(pool)
                        nc.gpsimd.tensor_copy(qm[:].rearrange("p (s c) -> p s c", s=STREAMS)[:, :, 0:STEP],
                                              qf[:, SEQ:TOK].rearrange("p (s c) -> p s c", s=STREAMS)).then_inc(s_qm, 1)
                        pool.wait_ge(s_free, CREDIT + o + RET_USES.index(f"Tk{hh}") + n_u * i + 1)
                        nc.gpsimd.tensor_tensor(km[:], kn[:, 4, :].unsqueeze(1).to_broadcast([P, STREAMS, P]),
                                                smask[:].unsqueeze(2).to_broadcast([P, STREAMS, P]),
                                                ALU.mult).then_inc(s_km, 1)
                        if not (last and hh):
                            apart(pool)
                            pool.dma_start(rd[:], dec_d[h + 1]).then_inc(s_dec, 16)
                            decay(h + 1)
                        pool.wait_ge(s_stp, CREDIT + h + 1)
                        apart(pool)
                        pool.dma_start(stp_o[h], stp[:]).then_inc(s_stp_out, 16)
                        for half in range(2):
                            pool.wait_ge(s_sts, CREDIT + 2 * h + half + 1)
                            apart(pool)
                            pool.dma_start(sts_o[h, :, 4 * half:4 * half + 4, :],
                                           s0[:, 4 * half:4 * half + 4, :]).then_inc(s_sts_out, 16)
                        pool.wait_ge(s_stp_out, 16 * (h + 1))
                        pool.sem_inc(s_stp_kept, 1)
                        if not (last and hh):
                            pool.wait_ge(s_sts_out, 32 * (h + 1))
                            apart(pool)
                            pool.dma_start(s0[:], st_d[h + 1]).then_inc(s_s0, 16)

                with pool.Fori(0, 3) as i:
                    body(i, False)
                body(3, True)
                pool.wait_ge(s_stp_out, 16 * H_RET)
                pool.wait_ge(s_sts_out, 32 * H_RET)

            def stick(c):
                o = c["unit"] + 1
                pool.wait_ge(s_fill, CREDIT + c["fill"])
                pool.dma_start(negtri[:], negtri_d).then_inc(s_sb_in, 16)
                pool.dma_start(bmask[:], bmask_d).then_inc(s_sb_in, 16)
                pool.dma_start(bcap[:], bcap_d).then_inc(s_sb_in, 16)

                def body(i):
                    def load(j):
                        if j < 2:
                            pool.wait_ge(s_fill, CREDIT + c["fill"] + SB_USES.index(f"AB{j + 2}") + 1 + len(SB_USES) * (i - 1))
                        else:
                            pool.wait_ge(s_fill, CREDIT + c["fill"] + SB_USES.index(f"AB{j - 2}") + 1 + len(SB_USES) * i)
                        apart(pool)
                        pool.dma_start(kc[:, j % 2, :, :], kc_d[4 * i + j]).then_inc(s_kv[j % 2], 16)
                        pool.dma_start(vc[:, j % 2, :, :], vc_d[4 * i + j]).then_inc(s_kv[j % 2], 16)

                    load(0)
                    load(1)
                    for j in range(4):
                        if j >= 2:
                            load(j)
                        pool.wait_ge(s_free, CREDIT + o + SB_UNITS.index(f"k{j}") + len(SB_UNITS) * i + 1)
                        apart(pool)
                        pool.dma_start(k_o[4 * i + j], bk[:, j % 2, :]).then_inc(s_k_out, 16)
                        pool.wait_ge(s_k_out, 16 * (4 * i + j + 1))
                        pool.sem_inc(s_k_kept, 1)
                        pool.wait_ge(s_free, CREDIT + o + SB_UNITS.index(f"v{j}") + len(SB_UNITS) * i + 1)
                        apart(pool)
                        pool.dma_start(v_o[4 * i + j], bvt[:]).then_inc(s_v_out, 16)
                        pool.wait_ge(s_v_out, 16 * (4 * i + j + 1))
                        pool.sem_inc(s_v_kept, 1)

                with pool.Fori(0, 2) as i:
                    body(i)
                pool.wait_ge(s_k_out, 16 * PAIRS)
                pool.wait_ge(s_v_out, 16 * PAIRS)

            add_squares(0, 0)
            for c in plan:
                {"ffn": ffn, "ret": ret, "sb": stick, "ple": lambda c: None}[c["kind"]](c)
                add_squares(c["fed"] + KT, c["norm"] + 1)

        @block.vector
        def _(dve):
            for s in (s_free, s_wlo, s_xlo, s_rstd, s_glo, s_plo, s_sr, s_pm, s_xup, s_out, s_rt, s_rot, s_kvs,
                      s_aggr, s_gn, s_ylo, s_sp, s_llo, s_cap):
                dve.sem_inc(s, CREDIT)
            tt, ts, stt = nc.vector.tensor_tensor, nc.vector.tensor_scalar, nc.vector.scalar_tensor_tensor

            def split_lo(c, m, i, per):
                cols = next_cols(c, m)
                if cols is None:
                    return
                n = c["n"] + m + 2 + per * i
                r, _ = landed(c, m + 2)
                p = (c["n"] + m) % 2
                dve.wait_ge(s_whi, CREDIT + n + 1)
                tt(w_lo[:, p, 0:cols], raw[:, r, 0:cols], w_hi[:, p, 0:cols].bitcast(F), ALU.subtract).then_inc(s_wlo, 1)

            def feed_lo(c_fed, norm, d):
                dve.wait_ge(s_xhi, CREDIT + c_fed + d + 1)
                stt(out=x_lo[:, d, :], in0=x[:, d, :], scalar=gain[:, norm, d:d + 1],
                    in1=x_hi[:, d, :].bitcast(F), op0=ALU.mult, op1=ALU.subtract).then_inc(s_xlo, 1)

            def one_over_rms(c, norm):
                u = c["unit"] % 4
                dve.wait_ge(s_ss, CREDIT + norm + 1)
                ts(halves(scr[:, 0, :]), acc(u), 1.0 / D, EPS, ALU.mult, ALU.add).then_inc(s_free, 1)
                k = 5 * norm
                dve.wait_ge(s_root, CREDIT + norm + 1)
                nc.vector.reciprocal(scr[:, 2, :], scr[:, 1, :]).then_inc(s_rstd, 1)
                dve.wait_ge(s_rstd, CREDIT + k + 1)
                tt(scr[:, 3, :], scr[:, 2, :], scr[:, 2, :], ALU.mult).then_inc(s_rstd, 1)
                dve.wait_ge(s_rstd, CREDIT + k + 2)
                tt(scr[:, 1, :], scr[:, 3, :], scr[:, 0, :], ALU.mult).then_inc(s_rstd, 1)
                dve.wait_ge(s_rstd, CREDIT + k + 3)
                ts(scr[:, 3, :], scr[:, 1, :], -0.5, 1.5, ALU.mult, ALU.add).then_inc(s_rstd, 1)
                dve.wait_ge(s_rstd, CREDIT + k + 4)
                tt(rstd[:], scr[:, 2, :], scr[:, 3, :], ALU.mult).then_inc(s_rstd, 1)
                dve.wait_ge(s_rstd, CREDIT + k + 5)

            def ffn(c):
                m = 0
                o = c["unit"] + 1
                for nf_at, nf in enumerate(PIECES):
                    gbase = c["g"] + sum(PIECES[:nf_at])

                    def body(i, m=m, gbase=gbase, nf_at=nf_at):
                        first = isinstance(i, int) and i == 0 and nf_at == 0
                        if first:
                            for j in range(2):
                                split_lo(c, m + j, 0, 0)
                            one_over_rms(c, c["norm"])
                        for j in range(4):
                            u = (o + m + j) % 4
                            f = gbase + 2 * i + j // 2
                            t = scr[:, j // 2, :]
                            dve.wait_ge(s_fill, CREDIT + c["fill"] + m + j + 4 * i + 1)
                            if j % 2 == 0:
                                dve.wait_ge(s_glo, CREDIT + f - 1)
                                tt(halves(t), acc(u), halves(rstd[:]), ALU.mult).then_inc(s_free, 1)
                                if j or not first:
                                    split_lo(c, m + j, i, 4)
                                dve.wait_ge(s_silu, CREDIT + f + 1)
                                tt(scr[:, 2 + j // 2, :], scr[:, 2 + j // 2, :], rstd[:], ALU.mult).then_inc(s_sr, 1)
                            else:
                                dve.wait_ge(s_sr, CREDIT + f + 1)
                                tt(halves(t), acc(u), halves(scr[:, 2 + j // 2, :]), ALU.mult).then_inc(s_free, 1)
                                dve.wait_ge(s_ghi, CREDIT + f + 1)
                                fi = 2 * i + j // 2
                                tt(g_lo[:, fi, :], t, g_hi[:, fi, :].bitcast(F), ALU.subtract).then_inc(s_glo, 1)
                                if j >= 2 or not first:
                                    split_lo(c, m + j, i, 4)
                    lo = 0
                    if nf_at == 0:
                        body(0)
                        lo = 1
                    with dve.Fori(lo, nf // 2) as i:
                        body(i)
                    m += 2 * nf
                    if nf_at == 0 and c["split_p"]:
                        dve.wait_ge(s_phi, CREDIT + c["ple"] + 1)
                        tt(p_lo[:], p_raw[:], p_hi[:].bitcast(F), ALU.subtract).then_inc(s_plo, 1)

                    def down(i, j, feed, m=m):
                        u = (o + m + j) % 4
                        d = 4 * i + j
                        dve.wait_ge(s_fill, CREDIT + c["fill"] + m + d + 1)
                        xd = halves(x[:, d, :])
                        stt(out=xd, in0=acc(u), scalar=0.5, in1=xd, op0=ALU.mult, op1=ALU.add).then_inc(s_free, 1)
                        split_lo(c, m + j, i, 4) if not isinstance(i, int) else split_lo(c, m + d, 0, 0)
                        if feed:
                            feed_lo(c["fed"] + KT, c["norm"] + 1, d)
                    if nf_at < 2:
                        with dve.Fori(0, KT // 4) as i:
                            for j in range(4):
                                down(i, j, False)
                    else:
                        for d in range(KT):
                            down(d // 4, d % 4, True)
                    m += KT

            def ple(c):
                unit = c["unit"] + 1
                fill = c["fill"]
                for m in range(2):
                    if m == 0:
                        one_over_rms(c, c["norm"])
                    for t in range(4):
                        dve.wait_ge(s_fill, CREDIT + fill + 1)
                        nc.vector.tensor_copy(halves(proj[:, 4 * m + t, :]), acc(unit % 4)).then_inc(s_free, 1)
                        unit, fill = unit + 1, fill + 1
                    split_lo(c, m, 0, 0)
                for d in range(KT):
                    dve.wait_ge(s_fill, CREDIT + fill + 1)
                    dve.wait_ge(s_sig, CREDIT + KT * c["ple"] + d - 1)
                    tt(halves(scr[:, d % 2, :]), acc(unit % 4), halves(rstd[:]), ALU.mult).then_inc(s_free, 1)
                    unit, fill = unit + 1, fill + 1
                    split_lo(c, 2 + d, 0, 0)
                    t = scr[:, 2 + d % 2, :]
                    dve.wait_ge(s_sig, CREDIT + KT * c["ple"] + d + 1)
                    tt(t, t, proj[:, d, :], ALU.mult).then_inc(s_pm, 1)
                    dve.wait_ge(s_pm, CREDIT + KT * c["ple"] + d + 1)
                    tt(x[:, d, :], x[:, d, :], t, ALU.add).then_inc(s_xup, 1)
                if not c["last"]:
                    for d in range(KT):
                        feed_lo(c["fed"] + KT, c["norm"] + 1, d)

            def ret(c):
                one_over_rms(c, c["norm"])
                o = c["unit"] + 1
                uses = RET_USES
                n_u = len(uses)
                dve.wait_ge(s_ret_in, 64)

                def body(i, last):
                    def u(use):
                        return (o + uses.index(use)) % 4

                    def fill(use):
                        return c["fill"] + uses.index(use) + n_u * i + 1

                    for hh in range(2):
                        h = 2 * i + hh
                        gk = 7 * h

                        def rot(name, out):
                            use = f"{name}{hh}"
                            n = "qk".index(name)
                            dve.wait_ge(s_fill, CREDIT + fill(use))
                            dve.wait_ge(s_rd, CREDIT + h + 1)
                            tt(halves(scr[:, 0, :]), acc(u(use)), halves(rd[:, n, :]), ALU.mult).then_inc(s_free, 1)
                            dve.wait_ge(s_free, CREDIT + o + uses.index(use) + n_u * i + 1)
                            tt(out, scr[:, 0, :], cs[:, 0, :], ALU.mult).then_inc(s_rt, 1)
                            dve.wait_ge(s_swap, CREDIT + 4 * h + 2 * n + 2)
                            tt(scr[:, 1, :], scr[:, 1, :], cs[:, 1, :], ALU.mult).then_inc(s_rt, 1)
                            dve.wait_ge(s_rt, CREDIT + 4 * h + 2 * n + 2)
                            tt(out, out, scr[:, 1, :], ALU.add).then_inc(s_rot, 1)
                            split_lo(c, 6 * hh + n, i, 16)

                        def to(ho):
                            for j in range(2):
                                use = f"TO{ho}{j}"
                                dve.wait_ge(s_fill, CREDIT + fill(use))
                                hcount = 2 * i + ho
                                dve.wait_ge(s_gate, CREDIT + 2 * hcount + j + 1)
                                dve.wait_ge(s_ylo, CREDIT + 2 * hcount + j - 1)
                                tt(scr[:, 2 + j, :], flat(u(use))[:, 0:TOK], sg[:, j, :], ALU.mult).then_inc(s_free, 1)
                                dve.wait_ge(s_yhi, CREDIT + 2 * hcount + j + 1)
                                tt(y_lo[:, 2 * ho + j, :], scr[:, 2 + j, :], y_hi[:, 2 * ho + j, :].bitcast(F),
                                   ALU.subtract).then_inc(s_ylo, 1)

                        rot("q", qf[:])
                        if hh:
                            to(0)
                        rot("k", kf[:])
                        dve.wait_ge(s_fill, CREDIT + fill(f"v{hh}0"))
                        tt(halves(vt_o[:, 0:TOK]), acc(u(f"v{hh}0")), halves(rstd[:]), ALU.mult).then_inc(s_free, 1)
                        split_lo(c, 6 * hh + 2, i, 16)
                        dve.wait_ge(s_fill, CREDIT + fill(f"Tk{hh}"))
                        nc.vector.tensor_copy(kn[:].rearrange("p t c -> p (t c)"), flat(u(f"Tk{hh}"))[:, 0:TOK]).then_inc(s_free, 1)
                        dve.wait_ge(s_fill, CREDIT + fill(f"v{hh}1"))
                        tt(halves(vt_o[:, TOK:2 * TOK]), acc(u(f"v{hh}1")), halves(rstd[:]), ALU.mult).then_inc(s_free, 1)
                        split_lo(c, 6 * hh + 3, i, 16)

                        def by_token(j):
                            use = f"Tv{hh}{j}"
                            dve.wait_ge(s_fill, CREDIT + fill(use))
                            nc.vector.tensor_copy(vn[:, :, j * P:(j + 1) * P],
                                                  flat(u(use))[:, 0:TOK].rearrange("p (t c) -> p t c", t=TT)).then_inc(s_free, 1)
                        by_token(0)
                        dve.wait_ge(s_fill, CREDIT + fill(f"SC{hh}"))
                        tt(sc[:].rearrange("p t c -> p (t c)"), flat(u(f"SC{hh}"))[:, 0:TOK],
                           rmask[:].rearrange("p t c -> p (t c)"), ALU.mult).then_inc(s_free, 1)

                        def gate(j):
                            use = f"g{hh}{j}"
                            dve.wait_ge(s_fill, CREDIT + fill(use))
                            tt(halves(sg[:, j, :]), acc(u(use)), halves(rstd[:]), ALU.mult).then_inc(s_free, 1)
                            split_lo(c, 6 * hh + 4 + j, i, 16)
                        gate(0)
                        by_token(1)
                        gate(1)
                        dve.wait_ge(s_fill, CREDIT + fill(f"KV{hh}"))
                        dve.wait_ge(s_stp, CREDIT + h)
                        kv = flat(u(f"KV{hh}"))
                        nc.vector.tensor_copy(sp_[:, 0, :], kv[:, 0:DV]).then_inc(s_kvs, 1)
                        for t in range(1, 4):
                            dve.wait_ge(s_kvs, CREDIT + 3 * h + t)
                            tt(sp_[:, t, :], kv[:, t * DV:(t + 1) * DV], sp_[:, t - 1, :],
                               ALU.add).then_inc(s_kvs if t < 3 else s_free, 1)
                        dve.wait_ge(s_fill, CREDIT + fill(f"OS{hh}"))
                        osf = flat(u(f"OS{hh}"))
                        nc.vector.bn_stats(bst[:, 4, :], osf[:, 0:DV])
                        dve.wait_ge(s_fill, CREDIT + fill(f"OP{hh}"))
                        opf = flat(u(f"OP{hh}"))
                        for t in range(4):
                            op = nc.vector.bn_stats(bst[:, t, :], opf[:, t * DV:(t + 1) * DV])
                        op.then_inc(s_gn, 1)
                        dve.wait_ge(s_gn, CREDIT + gk + 1)
                        apart(dve)
                        for t in range(TT):
                            op = nc.vector.bn_aggr(mv[:, t, :], bst[:, t, :])
                        op.then_inc(s_aggr, 1)
                        dve.wait_ge(s_aggr, CREDIT + h + 1)
                        ts(gn[:, 0, :], mv[:, :, 1], GN_EPS, None, ALU.add).then_inc(s_gn, 1)
                        dve.wait_ge(s_groot, CREDIT + h + 1)
                        nc.vector.reciprocal(gn[:, 2, :], gn[:, 1, :]).then_inc(s_gn, 1)
                        dve.wait_ge(s_gn, CREDIT + gk + 3)
                        tt(gn[:, 3, :], gn[:, 2, :], gn[:, 2, :], ALU.mult).then_inc(s_gn, 1)
                        dve.wait_ge(s_gn, CREDIT + gk + 4)
                        tt(gn[:, 3, :], gn[:, 3, :], gn[:, 0, :], ALU.mult).then_inc(s_gn, 1)
                        dve.wait_ge(s_gn, CREDIT + gk + 5)
                        ts(gn[:, 3, :], gn[:, 3, :], -0.5, 1.5, ALU.mult, ALU.add).then_inc(s_gn, 1)
                        dve.wait_ge(s_gn, CREDIT + gk + 6)
                        tt(gn[:, 4, :], gn[:, 2, :], gn[:, 3, :], ALU.mult).then_inc(s_gn, 1)
                        dve.wait_ge(s_gn, CREDIT + gk + 7)
                        for t in (4, 0, 1, 2, 3):
                            src = osf[:, 0:DV] if t == 4 else opf[:, t * DV:(t + 1) * DV]
                            op = ts(vt_o[:, t * DV:(t + 1) * DV], src, mv[:, t, 0:1], gn[:, 4, t:t + 1], ALU.subtract, ALU.mult)
                            if t in (3, 4):
                                op.then_inc(s_free, 1)
                        for half in range(2):
                            use = f"SS{hh}{half}"
                            dve.wait_ge(s_fill, CREDIT + fill(use))
                            s4 = s0[:, 4 * half:4 * half + 4, :].rearrange("p s c -> p (s c)")
                            tt(s4, s4, flat(u(use)), ALU.add).then_inc(s_free, 1)
                    to(1)
                    for d in range(KT):
                        use = f"w{d}"
                        dve.wait_ge(s_fill, CREDIT + fill(use))
                        xd = halves(x[:, d, :])
                        tt(xd, xd, acc(u(use)), ALU.add).then_inc(s_free, 1)
                        if d % 2:
                            split_lo(c, 12 + d // 2, i, 16)
                        if last:
                            feed_lo(c["fed"] + KT, c["norm"] + 1, d)

                with dve.Fori(0, 3) as i:
                    body(i, False)
                body(3, True)

            def stick(c):
                one_over_rms(c, c["norm"])
                o = c["unit"] + 1
                dve.wait_ge(s_sb_in, 48)

                def body(i):
                    def fill(use):
                        return c["fill"] + SB_USES.index(use) + len(SB_USES) * i + 1

                    def slot(name, j):
                        dve.wait_ge(s_fill, CREDIT + fill(f"{name}{j}"))
                        pair = 4 * i + j
                        par = j % 2
                        if name == "q":
                            stt(out=halves(bq[:, par, :]), in0=acc(0), scalar=HD ** -0.5, in1=halves(rstd[:]),
                                op0=ALU.mult, op1=ALU.mult).then_inc(s_free, 1)
                        elif name == "k":
                            dve.wait_ge(s_k_kept, CREDIT + pair - 1)
                            tt(halves(bk[:, par, :]), acc(0), halves(rstd[:]), ALU.mult).then_inc(s_free, 1)
                        else:
                            dve.wait_ge(s_v_kept, CREDIT + pair)
                            tt(halves(bvt[:]), acc(0), halves(rstd[:]), ALU.mult).then_inc(s_free, 1)
                        split_lo(c, 3 * j + "qkv".index(name), i, 16)

                    def by_token(j):
                        dve.wait_ge(s_fill, CREDIT + fill(f"T{j}"))
                        nc.vector.tensor_copy(bv[:, j % 2, :, :].rearrange("p t c -> p (t c)"),
                                              flat(0)[:, 0:TOK]).then_inc(s_free, 1)

                    def softplus(hh, j):
                        head = 8 * i + 2 * j + hh
                        sk = 3 * head
                        dve.wait_ge(s_soft, CREDIT + 3 * head + 3)
                        stt(out=e[:, hh, :], in0=zf(hh), scalar=0.0, in1=e[:, hh, :], op0=ALU.max, op1=ALU.add).then_inc(s_sp, 1)
                        dve.wait_ge(s_sp, CREDIT + sk + 1)
                        e3 = e[:, hh, :].rearrange("p (b c) -> p b c", b=3)
                        tt(e3[:, :, 0:P], e3[:, :, 0:P], bmask[:, 0:1, :].to_broadcast([P, 3, P]), ALU.mult).then_inc(s_sp, 1)
                        tt(e3[:, 1:3, 384:512], e3[:, 1:3, 384:512], bmask[:], ALU.mult).then_inc(s_sp, 1)
                        dve.wait_ge(s_lhi, CREDIT + head + 1)
                        tt(l_lo[:, hh, :], e[:, hh, :], l_hi[:, hh, :].bitcast(F), ALU.subtract).then_inc(s_llo, 1)

                    def cap(hh, j):
                        dve.wait_ge(s_fill, CREDIT + fill(f"R{'AB'[hh]}{j}"))
                        z = z3(hh)
                        tt(z[:, :, 0:P], z[:, :, 0:P], bcap[:, 0:1, :].to_broadcast([P, 3, P]), ALU.min).then_inc(s_cap, 1)
                        tt(z[:, 1:3, 384:512], z[:, 1:3, 384:512], bcap[:], ALU.min).then_inc(s_cap, 1)

                    def ylo(hh, j):
                        head = 8 * i + 2 * j + hh
                        rows = slice(HD * hh, HD * (hh + 1))
                        dve.wait_ge(s_ohi, CREDIT + head + 1)
                        tt(y_lo[rows, j, :], flat(0)[rows, 0:TOK], y_hi[rows, j, :].bitcast(F), ALU.subtract).then_inc(s_free, 1)

                    for name in "qkv":
                        slot(name, 0)
                    by_token(0)
                    softplus(0, 0)
                    softplus(1, 0)
                    for j in range(4):
                        nxt = j < 3
                        if nxt:
                            slot("q", j + 1)
                        cap(0, j)
                        if nxt:
                            slot("k", j + 1)
                        cap(1, j)
                        ylo(0, j)
                        if nxt:
                            slot("v", j + 1)
                            by_token(j + 1)
                        ylo(1, j)
                        if nxt:
                            softplus(0, j + 1)
                            softplus(1, j + 1)
                    for d in range(KT):
                        dve.wait_ge(s_fill, CREDIT + fill(f"w{d}"))
                        xd = halves(x[:, d, :])
                        tt(xd, xd, acc(0), ALU.add).then_inc(s_free, 1)
                        if d % 2:
                            split_lo(c, 12 + d // 2, i, 16)

                with dve.Fori(0, 2) as i:
                    body(i)
                for d in range(KT):
                    feed_lo(c["fed"] + KT, c["norm"] + 1, d)

            dve.wait_ge(s_const, 48)
            for n in range(2):
                dve.wait_ge(s_whi, CREDIT + n + 1)
                tt(w_lo[:, n, :], raw[:, n, :], w_hi[:, n, :].bitcast(F), ALU.subtract).then_inc(s_wlo, 1)
            for d in range(KT):
                feed_lo(0, 0, d)
            for c in plan:
                {"ffn": ffn, "ret": ret, "sb": stick, "ple": ple}[c["kind"]](c)
            one_over_rms(dict(unit=at.unit), len(plan))
            for d in range(KT):
                if d >= 4:
                    dve.wait_ge(s_y_out[d % 4], 16 * (d // 4))
                stt(out=scr[:, d % 4, :], in0=x[:, d, :], scalar=gain[:, len(plan), d:d + 1], in1=rstd[:],
                    op0=ALU.mult, op1=ALU.mult).then_inc(s_out, 1)


PHASES = ["ffn", "ret", "ffn", "ple", "ffn", "sb", "ffn", "ple"]


def _slots(w, np):
    k, n = w.shape[0] // P, w.shape[1] // P
    return w.reshape(k, P, n, P).transpose(2, 1, 0, 3)


def _stream(inputs, phases, np):
    out, ffn_at, ret_at, sb_at, ple_at = [], 0, 0, 0, 0

    def put(blocks):
        for b in blocks:
            b = b.reshape(P, -1)
            if b.shape[1] < D:
                b = np.concatenate([b, np.zeros((P, D - b.shape[1]), b.dtype)], 1)
            out.append(b)

    def w_out_part(w, i):
        s = _slots(w[4 * i * P:4 * (i + 1) * P], np)
        put(np.concatenate([s[2 * t], s[2 * t + 1]], 1) for t in range(KT // 2))

    for ph in phases:
        if ph == "ffn":
            ab, layer = "ab"[ffn_at % 2], ffn_at // 2
            gu = _slots(inputs[f"w_ffn_{ab}_gu"][layer], np)
            down = inputs[f"w_ffn_{ab}_down"][layer]
            f0 = 0
            for nf in PIECES:
                for f in range(f0, f0 + nf):
                    put([gu[f], gu[D_FF // P + f]])
                put(_slots(down[f0 * P:(f0 + nf) * P], np))
                f0 += nf
            ffn_at += 1
        elif ph == "ret":
            s = _slots(inputs["ret_w_in"][ret_at], np)
            for i in range(4):
                for h in (2 * i, 2 * i + 1):
                    put([s[h], s[8 + h], s[16 + 2 * h], s[17 + 2 * h], s[32 + 2 * h], s[33 + 2 * h]])
                w_out_part(inputs["ret_w_out"][ret_at], i)
            ret_at += 1
        elif ph == "sb":
            s = _slots(inputs["sb_w_qkv"][sb_at], np)
            for i in range(2):
                for p in range(4 * i, 4 * i + 4):
                    put([s[p], s[8 + p], s[16 + p]])
                w_out_part(inputs["sb_w_out"][sb_at], i)
            sb_at += 1
        else:
            s = _slots(inputs["ple_w_proj"][ple_at], np)
            put(np.concatenate([s[4 * m + t] for t in range(4)], 1) for m in range(2))
            put(_slots(inputs["ple_w_gate"][ple_at], np))
            ple_at += 1
    return np.stack(out)


def _constants(np):
    f32 = np.float32
    pos = np.concatenate([np.arange(SEQ), np.tile(128 + np.arange(STEP), STREAMS)]).astype(f32)
    idx = np.concatenate([np.arange(SEQ), np.tile(np.arange(STEP), STREAMS)]).astype(np.float64)
    freqs = (f32(10000.0) ** (-np.arange(64, dtype=f32) / f32(64))).astype(f32)
    ang = (freqs[:, None] * pos[None, :]).astype(f32).astype(np.float64)
    cos, sin = np.cos(ang), np.sin(ang)
    cs = np.stack([np.concatenate([cos, cos]), np.concatenate([-sin, sin])], 1)
    log_g = np.log1p(-(2.0 ** (-5.0 - np.arange(H_RET))))
    dq = np.exp((idx[None] + 1) * log_g[:, None])
    dk = np.exp(-(idx[None] + 1) * log_g[:, None]) * P ** -0.5
    dec = np.broadcast_to(np.stack([dq, dk], 1)[:, None], (H_RET, P, 2, TOK))
    gpow = np.broadcast_to(np.stack([np.exp(SEQ * log_g), np.exp(STEP * log_g)], 1)[None], (P, H_RET, 2))
    a = np.arange(P)
    same = a[:, None] // STEP == a[None, :] // STEP
    incl, strict = a[:, None] <= a[None, :], a[:, None] < a[None, :]
    rmask = np.stack([incl] * 4 + [incl & same], 1)
    seen = np.stack([strict, strict & same], 1)
    smask = a[:, None] // STEP == np.arange(STREAMS)[None, :]
    negtri = np.stack([-(a[:, None] >= a[None, :]).astype(f32), -np.ones((P, P), f32)], 1)
    out = dict(ones_d=np.ones((P, P)), ident_d=np.eye(P), negtri_d=negtri, cs_d=cs, dec_d=dec, rmask_d=rmask,
               smask_d=smask, gpow_d=gpow, bmask_d=seen, bcap_d=np.where(seen, 3e38, -1e30))
    return {k: np.ascontiguousarray(v, dtype=f32) for k, v in out.items()}


def _lay_out(inputs, phases, np):
    def tokens(prompt, sample):
        t = np.concatenate([prompt.reshape(SEQ, -1), sample.reshape(TOK - SEQ, -1)])
        return t.T.reshape(-1, P, TOK)

    a = dict(xT=tokens(inputs["x_prompt"], inputs["x_sample"]))
    a["pT"] = np.stack([tokens(inputs["p_prompt"][i], inputs["p_sample"][i]) for i in range(2)])
    layers = [inputs[n][i] for i in range(2) for n in ("norm_ffn_a", "norm_mix", "norm_ffn_b", "norm_ple")]
    gains = np.stack(layers[:len(phases)] + [inputs["norm_final"]] * (9 - len(layers[:len(phases)])))
    a["gains"] = gains.reshape(9, KT, P).transpose(2, 0, 1)
    a["wst"] = _stream(inputs, phases, np)
    a.update(_constants(np))
    a["st_d"] = inputs["state_ret"][0].transpose(1, 2, 0, 3)
    k, v = inputs["cache_sb_k"][0], inputs["cache_sb_v"][0]
    a["kc_d"] = k.reshape(STREAMS, P, PAIRS, P).transpose(2, 3, 0, 1)
    a["vc_d"] = v.reshape(STREAMS, P, PAIRS, P).transpose(2, 1, 0, 3)
    return {k: np.ascontiguousarray(v) for k, v in a.items()}


_ORDER = ["xT", "pT", "gains", "wst", "ones_d", "ident_d", "negtri_d", "cs_d", "dec_d", "rmask_d", "smask_d", "gpow_d",
          "bmask_d", "bcap_d", "st_d", "kc_d", "vc_d"]
_OUTS = [("y_o", (KT, P, TOK)), ("stp_o", (H_RET, P, DV)), ("sts_o", (H_RET, P, STREAMS, DV)),
         ("k_o", (PAIRS, P, TOK)), ("v_o", (PAIRS, P, TOK))]


def _program(nc, arrays, phases, mybir):
    args = [nc.dram_tensor(n, arrays[n].shape, mybir.dt.float32, kind="ExternalInput").ap() for n in _ORDER]
    args += [nc.dram_tensor(n, shape, mybir.dt.float32, kind="ExternalOutput").ap() for n, shape in _OUTS]
    trunk(nc, phases, *args)


def kernel(**inputs):
    import numpy as np
    import concourse.bacc as bacc
    from concourse import mybir
    from concourse.bass_utils import run_bass_kernel_spmd

    inputs = {k: np.asarray(v) for k, v in inputs.items()}
    arrays = _lay_out(inputs, PHASES, np)
    nc = bacc.Bacc("TRN2", target_bir_lowering=False, num_devices=1)
    _program(nc, arrays, PHASES, mybir)
    r = run_bass_kernel_spmd(nc, [arrays], core_ids=[0]).results[0]

    def back(t, tail):
        t = t.reshape(D, TOK).T
        return (np.ascontiguousarray(t[:SEQ]).reshape((1, SEQ) + tail),
                np.ascontiguousarray(t[SEQ:]).reshape((STREAMS, STEP) + tail))

    y_p, y_s = back(r["y_o"], (D,))
    k_p, k_s = back(r["k_o"], (H_SB, HD))
    v_p, v_s = back(r["v_o"], (H_SB, HD))
    st_p = np.ascontiguousarray(r["stp_o"]).reshape(1, 1, H_RET, P, DV)
    st_s = np.ascontiguousarray(r["sts_o"].transpose(2, 0, 1, 3))[None]
    return y_p, y_s, st_p, st_s, k_p[None], v_p[None], k_s[None], v_s[None]
```

```python
import concourse.bass as bass
from concourse import mybir
from contextlib import ExitStack

P = 128
D = 1024
KT = D // P
SEQ, STREAMS, STEP = 512, 8, 16
TOK = SEQ + STREAMS * STEP
TT = TOK // P
HALF = TOK // 2
H_RET, DV = 8, 256
H_SB, HD = 16, 64
PAIRS = H_SB * HD // P
D_FF = 2816
PIECES = (8, 8, 6)
assert sum(PIECES) * P == D_FF
FFN_SLOTS = sum(2 * nf + KT for nf in PIECES)
RET_SLOTS, SB_SLOTS, PLE_SLOTS = 64, 32, 10
N_SLOTS = 4 * FFN_SLOTS + RET_SLOTS + SB_SLOTS + 2 * PLE_SLOTS
CREDIT = 4
EPS, GN_EPS = 1e-6, 1e-5
ZC = 1536
ZB = {(0, 0): (0, 0), (0, 1): (0, 512), (0, 3): (0, 896), (0, 2): (0, 1024), (1, 2): (0, 1280),
      (1, 0): (1, 0), (1, 1): (1, 512), (1, 3): (1, 896)}
ZW = [SEQ - P * _b for _b in range(4)]
Z_PAST, Z_NEW = 1024, 1280

RET_USES = []
for _h in range(2):
    RET_USES += [f"q{_h}"] + (["TO00", "TO01"] if _h else []) + [f"k{_h}", f"v{_h}0", f"Tk{_h}", f"v{_h}1",
                 f"Tv{_h}0", f"SC{_h}", f"g{_h}0", f"Tv{_h}1", f"g{_h}1", f"KV{_h}", f"OS{_h}", f"OP{_h}",
                 f"SS{_h}0", f"SS{_h}1"]
RET_USES += ["TO10", "TO11"] + [f"w{d}" for d in range(KT)]
def _sb_half_uses(r, a):
    out = [f"{n}{r}{h}" for n in "qkv" for h in "ab"]
    return out + [f"RA{a}", f"T{r}", f"RB{a}", f"AA{a}", f"AB{a}", f"ZA{r}", f"AS{a}", f"ZB{r}"]


def _w_uses(n):
    return [f"{n}{d}{h}" for d in range(KT) for h in "ab"]


SB_PRE = [f"{n}0{h}" for n in "qkv" for h in "ab"] + ["T0", "ZA0", "ZB0"]
SB_BODY = _sb_half_uses(1, 0) + _sb_half_uses(2, 1) + _w_uses("w")
SB_LAST = _sb_half_uses(1, 0) + _w_uses("y") + ["RA1", "RB1", "AA1", "AB1", "AS1"] + _w_uses("w")
SB_STEPS = H_SB // 4 - 1


def units(uses, use=None):
    upto = uses if use is None else uses[:uses.index(use) + 1]
    return sum(0 if u[0] in "ZR" else 2 if u[0] == "T" or u[:2] == "AS" else 1 for u in upto)


SB_FILLS = len(SB_PRE) + SB_STEPS * len(SB_BODY) + len(SB_LAST)
SB_UNITS = units(SB_PRE) + SB_STEPS * units(SB_BODY) + units(SB_LAST)


class At:

    def __init__(self, phases):
        self.of = []
        n = fill = unit = fed = g = ple = 0
        for i, ph in enumerate(phases):
            self.of.append(dict(i=i, kind=ph, n=n, fill=fill, unit=unit, fed=fed, g=g, ple=ple, norm=i,
                                ss=3 if ph == "sb" else unit % 4,
                                last=i == len(phases) - 1,
                                split_p=ph == "ffn" and phases[i + 1:i + 2] == ["ple"],
                                mixed=phases[i - 1] if i and phases[i - 1] in ("ret", "sb") else None))
            slots = {"ffn": FFN_SLOTS, "ret": RET_SLOTS, "sb": SB_SLOTS, "ple": PLE_SLOTS}[ph]
            fills = {"ffn": FFN_SLOTS, "ret": 4 * len(RET_USES), "sb": SB_FILLS, "ple": 16}[ph]
            units = {"ffn": FFN_SLOTS, "ret": 4 * len(RET_USES), "sb": SB_UNITS, "ple": 16}[ph]
            n, fill, unit, fed = n + slots, fill + fills, unit + units + 1, fed + KT
            g += sum(PIECES) * (ph == "ffn")
            ple += ph == "ple"
        self.n, self.fill, self.unit, self.fed = n, fill, unit, fed


def trunk(nc, phases, xT, pT, gains, wst, ones_d, ident_d, negtri_d, cs_d, dec_d, rmask_d, smask_d, gpow_d,
          bmask_d, bcap_d, st_d, kc_d, vc_d, y_o, stp_o, sts_o, k_o, v_o):
    F, R = mybir.dt.float32, mybir.dt.float32r
    ALU, ACT = mybir.AluOpType, mybir.ActivationFunctionType
    at = At(phases)
    plan = at.of
    kinds = set(phases)
    ctx = ExitStack()
    with ctx:
        def sb(name, shape, dt=F, on=ctx):
            return on.enter_context(nc.sbuf_tensor(name, shape, dt))

        x = sb("x", [P, KT, TOK])
        x_hi = sb("x_hi", [P, KT, TOK], R)
        x_lo = sb("x_lo", [P, KT, TOK], R)
        raw = sb("raw", [P, 4, D])
        w_hi = sb("w_hi", [P, 2, D], R)
        w_lo = sb("w_lo", [P, 2, D], R)
        sq = sb("sq", [P, 2, TOK])
        ssum = sb("ssum", [P, TOK])
        rstd = sb("rstd", [P, TOK])
        scr = sb("scr", [P, 4, TOK])
        gain = sb("gain", [P, 9, KT])
        ones = sb("ones", [P, P])
        ident = sb("ident", [P, P])
        with ExitStack() as s:
            g_hi = sb("g_hi", [P, 8, TOK], R, s)
            g_lo = sb("g_lo", [P, 8, TOK], R, s)
            proj = sb("proj", [P, KT, TOK], F, s)
            p_raw = sb("p_raw", [P, 2, TOK], F, s)
            p_hi = sb("p_hi", [P, 2, TOK], R, s)
            p_lo = sb("p_lo", [P, 2, TOK], R, s)
        y_hi = sb("y_hi", [P, 4, TOK], R)
        y_lo = sb("y_lo", [P, 4, TOK], R)
        with ExitStack() as s:
            cs = sb("cs", [P, 2, TOK], F, s)
            rd = sb("rd", [P, 2, TOK], F, s)
            rmask = sb("rmask", [P, TT, P], F, s)
            smask = sb("smask", [P, STREAMS], F, s)
            gpow = sb("gpow", [P, H_RET, 2], F, s)
            qf = sb("qf", [P, TOK], F, s)
            kf = sb("kf", [P, TOK], F, s)
            kn = sb("kn", [P, TT, P], F, s)
            km = sb("km", [P, STREAMS, P], F, s)
            qm = sb("qm", [P, STREAMS * (P + STEP)], F, s)
            vt_o = sb("vt_o", [P, 2 * TOK], F, s)
            vn = sb("vn", [P, TT, DV], F, s)
            sc = sb("sc", [P, TT, P], F, s)
            s0 = sb("s0", [P, STREAMS, DV], F, s)
            sp_ = sb("sp_", [P, 4, DV], F, s)
            stp = sb("stp", [P, DV], F, s)
            sg = sb("sg", [P, 2, TOK], F, s)
            bst = sb("bst", [P, TT, 6], F, s)
            mv = sb("mv", [P, TT, 2], F, s)
            gn = sb("gn", [P, 5, TT], F, s)
        with ExitStack() as s:
            negtri = sb("negtri", [P, 2, P], F, s)
            tri = sb("tri", [P, 2, P], R, s)
            bmask = sb("bmask", [P, 2, P], F, s)
            bcap = sb("bcap", [P, 2, P], F, s)
            bq = sb("bq", [P, 2, TOK], F, s)
            bqs = sb("bqs", [P, STREAMS, 2, STEP], F, s)
            bk = sb("bk", [P, 2, TOK], F, s)
            bvt = sb("bvt", [P, TOK], F, s)
            bv = sb("bv", [P, 2, TT, P], F, s)
            kc = sb("kc", [P, 2, STREAMS, P], F, s)
            vc = sb("vc", [P, 2, STREAMS, P], F, s)
            e = sb("e", [P, 2, ZC], F, s)
            l_hi = sb("l_hi", [P, 2, ZC], R, s)
            l_lo = sb("l_lo", [P, 2, ZC], R, s)
        ps = ctx.enter_context(nc.psum_tensor("ps", [P, 8, 512], F))

        def sem(name):
            return ctx.enter_context(nc.semaphore(name))

        s_raw = [sem(f"s_raw{r}") for r in range(4)]
        s_const, s_x, s_p = sem("s_const"), sem("s_x"), sem("s_p")
        s_ret_in, s_dec, s_s0 = sem("s_ret_in"), sem("s_dec"), sem("s_s0")
        s_sb_in, s_kv = sem("s_sb_in"), [sem("s_kv0"), sem("s_kv1")]
        s_y_out = [sem(f"s_y_out{k}") for k in range(4)]
        s_stp_out, s_sts_out = sem("s_stp_out"), sem("s_sts_out")
        s_k_out, s_v_out = sem("s_k_out"), sem("s_v_out")
        s_fill = sem("s_fill")
        s_ss = sem("s_ss")
        s_row = sem("s_row")
        s_whi, s_xhi, s_sq, s_root = sem("s_whi"), sem("s_xhi"), sem("s_sq"), sem("s_root")
        s_silu, s_sig, s_gate, s_tri = sem("s_silu"), sem("s_sig"), sem("s_gate"), sem("s_tri")
        s_ghi, s_phi, s_ohi = sem("s_ghi"), sem("s_phi"), sem("s_ohi")
        s_swap, s_stp, s_sts, s_groot, s_yhi = sem("s_swap"), sem("s_stp"), sem("s_sts"), sem("s_groot"), sem("s_yhi")
        s_soft, s_lhi, s_att = sem("s_soft"), sem("s_lhi"), sem("s_att")
        s_free = sem("s_free")
        s_wlo, s_xlo, s_rstd, s_glo, s_plo = sem("s_wlo"), sem("s_xlo"), sem("s_rstd"), sem("s_glo"), sem("s_plo")
        s_sr, s_pm, s_xup, s_out = sem("s_sr"), sem("s_pm"), sem("s_xup"), sem("s_out")
        s_rt, s_rot, s_kvs, s_aggr, s_gn, s_ylo = (sem(n) for n in ("s_rt", "s_rot", "s_kvs", "s_aggr", "s_gn", "s_ylo"))
        s_sp, s_llo, s_cap = sem("s_sp"), sem("s_llo"), sem("s_cap")
        s_apart = sem("s_apart")
        s_ssum, s_rd, s_km, s_qm = sem("s_ssum"), sem("s_rd"), sem("s_km"), sem("s_qm")
        s_stp_kept, s_k_kept, s_v_kept = sem("s_stp_kept"), sem("s_k_kept"), sem("s_v_kept")

        def apart(eng):
            eng.sem_inc(s_apart, 1)

        def halves(ap):
            return ap.rearrange("p (b c) -> p b c", b=2)

        def acc(u):
            return ps[:, 2 * u:2 * u + 2, 0:HALF]

        def flat(u):
            return ps[:, 2 * u:2 * u + 2, :].rearrange("p b c -> p (b c)")

        def zf(piece):
            return ps[:, 2 + 3 * piece:5 + 3 * piece, :].rearrange("p b c -> p (b c)")

        def by_stream(cols, s):
            return cols.rearrange("p (h s q) -> p h s q", h=2, s=STREAMS)[:, :, s, :]

        def landed(c, m, i=0, per=0):
            n = c["n"] + m
            return n % 4, 16 * (n // 4 + 1) + (4 * per) * i

        def slot_cols(kind, m):
            if kind == "ffn" and m >= FFN_SLOTS - KT:
                return PIECES[2] * P
            return D

        def next_cols(c, m):
            total = {"ffn": FFN_SLOTS, "ret": RET_SLOTS, "sb": SB_SLOTS, "ple": PLE_SLOTS}[c["kind"]]
            if m + 2 < total:
                return slot_cols(c["kind"], m + 2)
            return None if c["last"] else D

        def y_parts(what):
            top, bottom = slice(0, HD), slice(HD, P)
            return {"A": [(top, 0, slice(0, SEQ), slice(0, SEQ))],
                    "B": [(bottom, 1, slice(0, SEQ), slice(0, SEQ))],
                    "S": [(top, 0, slice(0, P), slice(SEQ, TOK)), (bottom, 0, slice(P, 2 * P), slice(SEQ, TOK))]}[what]

        block = ctx.enter_context(nc.Block())

        @block.sync
        def _(sp):
            sp.dma_start(gain[:], gains).then_inc(s_const, 16)
            sp.dma_start(ones[:], ones_d).then_inc(s_const, 16)
            sp.dma_start(ident[:], ident_d).then_inc(s_const, 16)
            for k in range(KT):
                sp.dma_start(x[:, k, :], xT[k]).then_inc(s_x, 16)

            def load(c, m, i=0, per=0, cols=D):
                n = c["n"] + m + per * i
                r, _ = landed(c, m)
                sp.wait_ge(s_wlo, CREDIT + n - 3)
                sp.dma_start(raw[:, r, 0:cols], wst[n, :, 0:cols]).then_inc(s_raw[r], 16)

            for c in plan:
                if c["kind"] == "ffn":
                    with sp.Fori(0, (FFN_SLOTS - KT) // 4) as i:
                        for j in range(4):
                            load(c, j, i, 4)
                    with sp.Fori(0, KT // 4) as i:
                        for j in range(4):
                            load(c, FFN_SLOTS - KT + j, i, 4, PIECES[2] * P)
                elif c["kind"] in ("ret", "sb"):
                    with sp.Fori(0, {"ret": RET_SLOTS, "sb": SB_SLOTS}[c["kind"]] // 4) as i:
                        for j in range(4):
                            load(c, j, i, 4)
                else:
                    for m in range(PLE_SLOTS):
                        load(c, m)
            for d in range(KT):
                sp.wait_ge(s_out, CREDIT + d + 1)
                sp.dma_start(y_o[d], scr[:, d % 4, :]).then_inc(s_y_out[d % 4], 16)
            for s in s_y_out:
                sp.wait_ge(s, 16 * KT // 4)

        @block.tensor
        def _(pe):
            for s in (s_fill, s_ss, s_row):
                pe.sem_inc(s, CREDIT)

            def mm3(out, wh, wl, xh, xl, start, stop):
                for q, (a, b) in enumerate(((wh, xh), (wh, xl), (wl, xh))):
                    for h in range(2):
                        last = nc.tensor.matmul(out[:, h, :], a, b[:, HALF * h:HALF * (h + 1)],
                                                start=start and q == 0, stop=stop and q == 2,
                                                skip_group_check=True)
                return last

            def project(c, m, i, per, u, blocks, src_hi, src_lo, before=None):
                p = (c["n"] + m) % 2
                for b, (wb, xb) in enumerate(blocks):
                    if before is not None:
                        before(b)
                    last = mm3(acc(u), w_hi[:, p, wb * P:(wb + 1) * P], w_lo[:, p, wb * P:(wb + 1) * P],
                               src_hi[:, xb, :], src_lo[:, xb, :], b == 0, b == len(blocks) - 1)
                last.then_inc(s_fill, 1)

            def sum_squares(c):
                u = c["ss"]
                pe.wait_ge(s_ssum, CREDIT + c["fed"] + KT)
                for h in range(2):
                    last = nc.tensor.matmul(acc(u)[:, h, :], ones[:], ssum[:, HALF * h:HALF * (h + 1)],
                                            start=True, stop=True)
                last.then_inc(s_ss, 1)

            def fed(c):
                return lambda b: pe.wait_ge(s_xlo, CREDIT + c["fed"] + b + 1)

            def ffn(c):
                def step(m, i, per, first=False):
                    n, unit = c["n"] + m + per * i, c["unit"] + 1 + m + per * i
                    pe.wait_ge(s_wlo, CREDIT + n + 1)
                    pe.wait_ge(s_free, CREDIT + (unit - 3 if m > 2 or not first else c["unit"]))

                m = 0
                for nf_at, nf in enumerate(PIECES):
                    def body(i, m=m):
                        for j in range(4):
                            first = isinstance(i, int) and i == 0 and nf_at == 0
                            step(m + j, i, 4, first)
                            project(c, m + j, i, 4, (c["unit"] + 1 + m + j) % 4, [(k, k) for k in range(KT)],
                                    x_hi, x_lo, fed(c) if first and j == 0 else None)
                            if first and j == 1:
                                sum_squares(c)
                    lo = 0
                    if nf_at == 0:
                        body(0)
                        lo = 1
                    with pe.Fori(lo, nf // 2) as i:
                        body(i)
                    m += 2 * nf
                    done = c["g"] + sum(PIECES[:nf_at + 1])

                    def ready(b, nf=nf, done=done):
                        if b == 0:
                            pe.wait_ge(s_glo, CREDIT + done - 1)
                        if b == nf - 1:
                            pe.wait_ge(s_glo, CREDIT + done)
                    with pe.Fori(0, KT // 4) as i:
                        for j in range(4):
                            step(m + j, i, 4)
                            project(c, m + j, i, 4, (c["unit"] + 1 + m + j) % 4, [(k, k) for k in range(nf)],
                                    g_hi, g_lo, ready if j == 0 else None)
                    m += KT

            def ple(c):
                unit = c["unit"] + 1
                pe.wait_ge(s_plo, CREDIT + c["ple"] + 1)
                for m in range(2):
                    pe.wait_ge(s_wlo, CREDIT + c["n"] + m + 1)
                    for t in range(4):
                        if m == 0 and t == 3:
                            sum_squares(c)
                        pe.wait_ge(s_free, CREDIT + unit - 4 + 1)
                        project(c, m, 0, 0, unit % 4, [(2 * t, 0), (2 * t + 1, 1)], p_hi, p_lo)
                        unit += 1
                for m in range(2, PLE_SLOTS):
                    pe.wait_ge(s_wlo, CREDIT + c["n"] + m + 1)
                    pe.wait_ge(s_free, CREDIT + unit - 4 + 1)
                    project(c, m, 0, 0, unit % 4, [(k, k) for k in range(KT)], x_hi, x_lo,
                            fed(c) if m == 2 else None)
                    unit += 1

            def ret(c):
                pe.wait_ge(s_free, CREDIT + c["unit"] - 4 + 1)
                sum_squares(c)
                o = c["unit"] + 1
                uses = RET_USES

                def body(i):
                    for idx, use in enumerate(uses):
                        u = (o + idx) % 4
                        pe.wait_ge(s_free, CREDIT + (o + idx + len(uses) * i - (2 if idx < 2 else 4) + 1))
                        if use[0] == "w":
                            d = int(use[1:])
                            slot = 12 + d // 2
                            if d == 0:
                                pe.wait_ge(s_ylo, CREDIT + 4 * i + 3)
                            if d % 2 == 0:
                                pe.wait_ge(s_wlo, CREDIT + c["n"] + slot + 16 * i + 1)

                            def last_y(b, d=d):
                                if d == 0 and b == 3:
                                    pe.wait_ge(s_ylo, CREDIT + 4 * i + 4)
                            project(c, slot, i, 16, u, [(4 * (d % 2) + k, k) for k in range(4)], y_hi, y_lo, last_y)
                            continue
                        hh = int(use[2]) if use[:2] in ("Tk", "Tv", "SC", "KV", "SS", "OS", "OP", "TO") else int(use[1])
                        h = 2 * i + hh
                        if use[0] in "qkvg" and use[:2] != "Tk":
                            slot = 6 * hh + {"q": 0, "k": 1, "v": 2, "g": 4}[use[0]] + (int(use[2]) if len(use) > 2 else 0)
                            pe.wait_ge(s_wlo, CREDIT + c["n"] + slot + 16 * i + 1)
                            project(c, slot, i, 16, u, [(k, k) for k in range(KT)], x_hi, x_lo,
                                    fed(c) if use == "q0" else None)
                            continue
                        f = flat(u)
                        if use[:2] == "Tk":
                            pe.wait_ge(s_rot, CREDIT + 2 * h + 2)
                            for t in range(TT):
                                last = nc.tensor.transpose(f[:, t * P:(t + 1) * P], kf[:, t * P:(t + 1) * P], ident[:])
                        elif use[:2] == "Tv":
                            j = int(use[3])
                            pe.wait_ge(s_free, CREDIT + o + uses.index(f"v{hh}{j}") + len(uses) * i + 1)
                            for t in range(TT):
                                last = nc.tensor.transpose(
                                    f[:, t * P:(t + 1) * P], vt_o[:, j * TOK + t * P:j * TOK + (t + 1) * P], ident[:])
                        elif use[:2] == "SC":
                            for t in range(TT):
                                last = nc.tensor.matmul(f[:, t * P:(t + 1) * P], kf[:, t * P:(t + 1) * P],
                                                        qf[:, t * P:(t + 1) * P], start=True, stop=True)
                        elif use[:2] == "KV":
                            pe.wait_ge(s_free, CREDIT + o + uses.index(f"Tv{hh}1") + len(uses) * i + 1)
                            for t in range(4):
                                last = nc.tensor.matmul(f[:, t * DV:(t + 1) * DV], kn[:, t, :], vn[:, t, :],
                                                        start=True, stop=True)
                        elif use[:2] == "OS":
                            pe.wait_ge(s_qm, CREDIT + h + 1)
                            pe.wait_ge(s_s0, 16 * (1) + 16 * h)
                            for s in range(STREAMS):
                                nc.tensor.matmul(f[:, 0:DV], qm[:, s * P:(s + 1) * P], s0[:, s, :],
                                                 start=s == 0, stop=False)
                            last = nc.tensor.matmul(f[:, 0:DV], sc[:, 4, :], vn[:, 4, :], start=False, stop=True)
                        elif use[:2] == "OP":
                            pe.wait_ge(s_kvs, CREDIT + 3 * h + 3)
                            for t in range(4):
                                last = nc.tensor.matmul(f[:, t * DV:(t + 1) * DV], sc[:, t, :], vn[:, t, :],
                                                        start=True, stop=t == 0)
                                if t:
                                    last = nc.tensor.matmul(f[:, t * DV:(t + 1) * DV], qf[:, t * P:(t + 1) * P],
                                                            sp_[:, t - 1, :], start=False, stop=True)
                        elif use[:2] == "SS":
                            pe.wait_ge(s_km, CREDIT + h + 1)
                            half = int(use[3])
                            for s in range(4):
                                last = nc.tensor.matmul(f[:, s * DV:(s + 1) * DV], km[:, 4 * half + s, :], vn[:, 4, :],
                                                        start=True, stop=True)
                        elif use[:2] == "TO":
                            j = int(use[3])
                            pe.wait_ge(s_free, CREDIT + o + uses.index(f"OP{hh}") + len(uses) * i + 1)
                            for t in range(TT):
                                last = nc.tensor.transpose(f[:, t * P:(t + 1) * P],
                                                           vt_o[:, t * DV + j * P:t * DV + (j + 1) * P], ident[:])
                        last.then_inc(s_fill, 1)

                with pe.Fori(0, 3) as i:
                    body(i)
                body(3)

            def stick(c):
                pe.wait_ge(s_free, CREDIT + c["unit"])
                sum_squares(c)

                def logits(z, par, head, b, z0, start):
                    rows = slice(HD * head, HD * (head + 1))
                    w, end = (P, TOK) if b == 4 else (ZW[b], SEQ)
                    return nc.tensor.matmul(z[:, z0:z0 + w], bk[rows, par, b * P:(b + 1) * P],
                                            bq[rows, par, b * P:end], start=start, stop=False, skip_group_check=True)

                def run(uses, slots, frees, t):
                    for use in uses:
                        kind, r = use[0], int(use[1] if use[0] in "qkvwyT" else use[2])
                        par = r % 2
                        if kind not in "ZR":
                            pe.wait_ge(s_free, CREDIT + frees + units(uses, use) - 2)
                        if kind in "qkvwy":
                            half = "ab".index(use[2])
                            slot, blocks, src = slots(kind, r)
                            if half == 0:
                                pe.wait_ge(s_wlo, CREDIT + c["n"] + slot + 8 * t + 1)
                            p = (c["n"] + slot) % 2
                            hi, lo = (x_hi, x_lo) if src == "x" else (y_hi, y_lo)
                            cols = slice(HALF * half, HALF * (half + 1))
                            for n, (wb, xb) in enumerate(blocks):
                                if use == "q0a":
                                    pe.wait_ge(s_xlo, CREDIT + c["fed"] + n + 1)
                                wh, wl = w_hi[:, p, wb * P:(wb + 1) * P], w_lo[:, p, wb * P:(wb + 1) * P]
                                for q, (a, b) in enumerate(((wh, hi), (wh, lo), (wl, hi))):
                                    last = nc.tensor.matmul(ps[:, half, 0:HALF], a, b[:, xb, cols],
                                                            start=n == 0 and q == 0,
                                                            stop=n == len(blocks) - 1 and q == 2)
                            last.then_inc(s_fill, 1)
                            continue
                        f = flat(0)
                        if kind == "T":
                            pe.wait_ge(s_free, CREDIT + frees + units(uses, f"v{r}b"))
                            for k in range(TT):
                                last = nc.tensor.transpose(f[:, k * P:(k + 1) * P], bvt[:, k * P:(k + 1) * P], ident[:])
                            last.then_inc(s_fill, 1)
                            continue
                        pair = 2 * t + r
                        piece = int(use[1] != "A")
                        z = zf(piece)
                        if kind == "Z":
                            pe.wait_ge(s_free, CREDIT + frees + units(uses, f"k{r}b"))
                            if piece == 0:
                                for n, b in enumerate((2, 0, 1, 3)):
                                    op = logits(z, par, 0, b, ZB[0, b][1], b != 3)
                                    if n == 0:
                                        op.then_inc(s_row, 1)
                                pe.wait_ge(s_row, CREDIT + 2 * pair + 1)
                                last = logits(z, par, 1, 2, ZB[1, 2][1], False)
                            else:
                                logits(z, par, 0, 4, Z_NEW, True).then_inc(s_row, 1)
                                for b in (0, 1, 3):
                                    logits(z, par, 1, b, ZB[1, b][1], b != 3)
                                pe.wait_ge(s_row, CREDIT + 2 * pair + 2)
                                logits(z, par, 1, 4, Z_NEW + P, False)
                                pe.wait_ge(s_kv[par], 32 * (t + r // 2 + 1))
                                for s in range(STREAMS):
                                    last = nc.tensor.matmul(by_stream(z[:, Z_PAST:Z_NEW], s), kc[:, par, s, :],
                                                            bqs[:, s, :, :], start=False, stop=s == STREAMS - 1,
                                                            skip_group_check=True)
                        elif kind == "R":
                            pe.wait_ge(s_llo, CREDIT + 2 * pair + 2)
                            for src in (l_hi, l_lo):
                                for (head, b), (at_piece, z0) in ZB.items():
                                    for b2 in range(b, 4):
                                        if at_piece == piece:
                                            from_piece, from_col = ZB[head, b2]
                                            last = nc.tensor.matmul(
                                                z[:, z0 + P * (b2 - b):z0 + ZW[b]], tri[:, int(b2 > b), :],
                                                src[:, from_piece, from_col:from_col + ZW[b2]], start=False,
                                                stop=False, skip_group_check=True)
                                if piece == 1:
                                    nc.tensor.matmul(z[:, Z_PAST:Z_NEW], tri[:, 0, :], src[:, 1, Z_PAST:Z_NEW],
                                                     start=False, stop=False, skip_group_check=True)
                                    nc.tensor.matmul(z[:, Z_PAST:Z_NEW], tri[:, 1, :], src[:, 1, Z_NEW:ZC],
                                                     start=False, stop=False, skip_group_check=True)
                                    last = nc.tensor.matmul(z[:, Z_NEW:ZC], tri[:, 0, :], src[:, 1, Z_NEW:ZC],
                                                            start=False, stop=src is l_lo, skip_group_check=True)
                        elif use[1] == "S":
                            f = f[:, 0:2 * P]
                            nc.tensor.matmul(f, bv[:, par, 4, :], e[:, 1, Z_NEW:ZC], start=True, stop=False,
                                             skip_group_check=True)
                            for s in range(STREAMS):
                                last = nc.tensor.matmul(by_stream(f, s), vc[:, par, s, :],
                                                        by_stream(e[:, 1, Z_PAST:Z_NEW], s),
                                                        start=False, stop=s == STREAMS - 1, skip_group_check=True)
                        else:
                            head = piece
                            pe.wait_ge(s_att, CREDIT + 2 * pair + head + 1)
                            for b in range(4):
                                at_piece, z0 = ZB[head, b]
                                last = nc.tensor.matmul(ps[:, head, b * P:SEQ], bv[:, par, b, :],
                                                        e[:, at_piece, z0:z0 + ZW[b]],
                                                        start=b == 0, stop=b == 3, skip_group_check=True)
                        last.then_inc(s_fill, 1)

                whole = [(k, k) for k in range(KT)]

                def first_slots(kind, r):
                    return "qkv".index(kind), whole, "x"

                def body_slots(kind, r):
                    if kind == "w":
                        return 9 + r // 4, [(2 * (r % 4) + k, k) for k in range(2)], "y"
                    return 3 * r + "qkv".index(kind), whole, "x"

                def last_slots(kind, r):
                    if kind in "yw":
                        return 6 + "yw".index(kind), [(r, "yw".index(kind))], "y"
                    return 3 + "qkv".index(kind), whole, "x"

                frees = c["unit"] + 1
                run(SB_PRE, first_slots, frees, 0)
                frees += units(SB_PRE)
                with pe.Fori(0, SB_STEPS) as t:
                    run(SB_BODY, body_slots, frees + units(SB_BODY) * t, t)
                run(SB_LAST, last_slots, frees + units(SB_BODY) * SB_STEPS, SB_STEPS)

            pe.wait_ge(s_const, 48)
            for c in plan:
                {"ffn": ffn, "ret": ret, "sb": stick, "ple": ple}[c["kind"]](c)
            sum_squares(dict(ss=at.unit % 4, fed=at.fed))

        @block.scalar
        def _(act):
            for s in (s_whi, s_xhi, s_sq, s_root, s_silu, s_sig, s_gate, s_tri, s_ghi, s_phi, s_ohi, s_swap,
                      s_stp, s_sts, s_groot, s_yhi, s_soft, s_lhi, s_att):
                act.sem_inc(s, CREDIT)

            def split_hi(c, m, i, per, fill):
                cols = next_cols(c, m)
                if cols is None:
                    return
                r, value = landed(c, m + 2)
                act.wait_ge(s_raw[r], value + (4 * per) * i)
                act.wait_ge(s_fill, CREDIT + fill)
                nc.scalar.activation(w_hi[:, (c["n"] + m) % 2, 0:cols], raw[:, r, 0:cols], ACT.Copy).then_inc(s_whi, 1)

            def feed(c_fed, norm, d, s, value, hi=True):
                act.wait_ge(s, CREDIT + value)
                if hi:
                    nc.scalar.activation(x_hi[:, d, :], x[:, d, :], ACT.Copy,
                                         scale=gain[:, norm, d:d + 1]).then_inc(s_xhi, 1)
                act.wait_ge(s_ssum, CREDIT + c_fed + d - 1)
                nc.scalar.activation(sq[:, d % 2, :], x[:, d, :], ACT.Square).then_inc(s_sq, 1)

            def root(c):
                act.wait_ge(s_free, CREDIT + c["unit"] + 1)
                nc.scalar.activation(scr[:, 1, :], scr[:, 0, :], ACT.Sqrt).then_inc(s_root, 1)

            def ffn(c):
                if c["mixed"] == "ret":
                    act.wait_ge(s_stp_kept, CREDIT + H_RET)
                    act.wait_ge(s_sts_out, 32 * H_RET)
                if c["mixed"] == "sb":
                    act.wait_ge(s_k_kept, CREDIT + PAIRS)
                    act.wait_ge(s_v_kept, CREDIT + PAIRS)
                m = 0
                o = c["unit"] + 1
                for nf_at, nf in enumerate(PIECES):
                    gbase = c["g"] + sum(PIECES[:nf_at])

                    def body(i, m=m, gbase=gbase, nf_at=nf_at):
                        first = isinstance(i, int) and i == 0 and nf_at == 0
                        if first:
                            for j in range(2):
                                split_hi(c, m + j, 0, 0, c["fill"] + m + j + 1)
                            root(c)
                        for j in range(4):
                            f = gbase + 2 * i + j // 2
                            if j >= 2 or not first:
                                if j % 2 == 0:
                                    split_hi(c, m + j, i, 4, c["fill"] + m + j + 4 * i + 1)
                            if j % 2 == 0:
                                act.wait_ge(s_free, CREDIT + o + m + j + 4 * i + 1)
                                nc.scalar.activation(scr[:, 2 + j // 2, :], scr[:, j // 2, :], ACT.Silu).then_inc(s_silu, 1)
                            else:
                                act.wait_ge(s_free, CREDIT + o + m + j + 4 * i + 1)
                                nc.scalar.activation(g_hi[:, 2 * i + j // 2, :], scr[:, j // 2, :], ACT.Copy).then_inc(s_ghi, 1)
                                if j >= 2 or not first:
                                    split_hi(c, m + j, i, 4, c["fill"] + m + j + 4 * i + 1)
                    lo = 0
                    if nf_at == 0:
                        body(0)
                        lo = 1
                    with act.Fori(lo, nf // 2) as i:
                        body(i)
                    m += 2 * nf
                    if nf_at == 0 and c["split_p"]:
                        act.wait_ge(s_p, 16 * (c["ple"] + 1))
                        nc.scalar.activation(p_hi[:], p_raw[:], ACT.Copy).then_inc(s_phi, 1)
                    if nf_at < 2:
                        with act.Fori(0, KT // 4) as i:
                            for j in range(4):
                                split_hi(c, m + j, i, 4, c["fill"] + m + j + 4 * i + 1)
                    else:
                        for d in range(KT):
                            split_hi(c, m + d, 0, 0, c["fill"] + m + d + 1)
                            feed(c["fed"] + KT, c["norm"] + 1, d, s_free, o + m + d + 1)
                    m += KT

            def ple(c):
                root(c)
                for m in range(2):
                    split_hi(c, m, 0, 0, c["fill"] + 4 * m + 4)
                for d in range(KT):
                    split_hi(c, 2 + d, 0, 0, c["fill"] + 8 + d + 1)
                    act.wait_ge(s_free, CREDIT + c["unit"] + 1 + 8 + d + 1)
                    act.wait_ge(s_xup, CREDIT + KT * c["ple"] + d - 1)
                    nc.scalar.activation(scr[:, 2 + d % 2, :], scr[:, d % 2, :], ACT.Sigmoid).then_inc(s_sig, 1)
                    if c["last"]:
                        if d:
                            feed(at.fed, 8, d - 1, s_xup, KT * c["ple"] + d, hi=False)
                if c["last"]:
                    feed(at.fed, 8, KT - 1, s_xup, KT * c["ple"] + KT, hi=False)
                else:
                    act.wait_ge(s_fill, CREDIT + c["fill"] + 16)
                    for d in range(KT):
                        feed(c["fed"] + KT, c["norm"] + 1, d, s_xup, KT * c["ple"] + d + 1)

            def ret(c):
                root(c)
                o = c["unit"] + 1
                uses = RET_USES
                n_u = len(uses)

                def body(i, last):
                    def fill(use):
                        return c["fill"] + uses.index(use) + n_u * i + 1

                    def free(use):
                        return o + uses.index(use) + n_u * i + 1

                    def to(hh):
                        for j in range(2):
                            act.wait_ge(s_free, CREDIT + free(f"TO{hh}{j}"))
                            nc.scalar.activation(y_hi[:, 2 * hh + j, :], scr[:, 2 + j, :], ACT.Copy).then_inc(s_yhi, 1)

                    for hh in range(2):
                        h = 2 * i + hh
                        for n, name in enumerate("qk"):
                            use = f"{name}{hh}"
                            act.wait_ge(s_free, CREDIT + free(use))
                            nc.scalar.activation(scr[0:64, 1, :], scr[64:128, 0, :], ACT.Copy).then_inc(s_swap, 1)
                            nc.scalar.activation(scr[64:128, 1, :], scr[0:64, 0, :], ACT.Copy).then_inc(s_swap, 1)
                            split_hi(c, 6 * hh + n, i, 16, fill(use))
                            if name == "q" and hh:
                                to(0)
                        for j in range(2):
                            split_hi(c, 6 * hh + 2 + j, i, 16, fill(f"v{hh}{j}"))
                        for j in range(2):
                            split_hi(c, 6 * hh + 4 + j, i, 16, fill(f"g{hh}{j}"))
                            act.wait_ge(s_free, CREDIT + free(f"g{hh}{j}"))
                            nc.scalar.activation(sg[:, j, :], sg[:, j, :], ACT.Silu).then_inc(s_gate, 1)
                        act.wait_ge(s_free, CREDIT + free(f"KV{hh}"))
                        act.wait_ge(s_stp_kept, CREDIT + h)
                        apart(act)
                        nc.scalar.activation(stp[:], sp_[:, 3, :], ACT.Copy,
                                             scale=gpow[:, h, 0:1]).then_inc(s_stp, 1)
                        act.wait_ge(s_gn, CREDIT + 7 * h + 2)
                        nc.scalar.activation(gn[:, 1, :], gn[:, 0, :], ACT.Sqrt).then_inc(s_groot, 1)
                        for half in range(2):
                            act.wait_ge(s_free, CREDIT + free(f"SS{hh}{half}"))
                            apart(act)
                            nc.scalar.activation(s0[:, 4 * half:4 * half + 4, :], s0[:, 4 * half:4 * half + 4, :], ACT.Copy,
                                                 scale=gpow[:, h, 1:2]).then_inc(s_sts, 1)
                    to(1)
                    for d in range(KT):
                        if d % 2:
                            split_hi(c, 12 + d // 2, i, 16, fill(f"w{d}"))
                        if last:
                            feed(c["fed"] + KT, c["norm"] + 1, d, s_free, free(f"w{d}"))

                act.wait_ge(s_ret_in, 64)
                with act.Fori(0, 3) as i:
                    body(i, False)
                body(3, True)

            def stick(c):
                act.wait_ge(s_sb_in, 48)
                nc.scalar.activation(tri[:], negtri[:], ACT.Copy).then_inc(s_tri, 1)
                root(c)
                nc.scalar.preload_act_table_set("natural_log_exp_and_others")

                def soft(hh, pair, k, filled):
                    if k == 0:
                        act.wait_ge(s_fill, CREDIT + filled)
                        nc.scalar.activation(e[:, hh, :], zf(hh), ACT.Abs).then_inc(s_soft, 1)
                        return
                    act.wait_ge(s_soft, CREDIT + 6 * pair + 2 * (k - 1) + hh + 1)
                    if k == 1:
                        nc.scalar.activation(e[:, hh, :], e[:, hh, :], ACT.Exp, scale=-1.0).then_inc(s_soft, 1)
                    else:
                        nc.scalar.activation(e[:, hh, :], e[:, hh, :], ACT.Ln, bias=1.0).then_inc(s_soft, 1)

                def soft_rest(pair):
                    for k in (1, 2):
                        for hh in range(2):
                            soft(hh, pair, k, 0)

                def lhi(pair, hh):
                    act.wait_ge(s_sp, CREDIT + 2 * (2 * pair + hh) + 2)
                    nc.scalar.activation(l_hi[:, hh, :], e[:, hh, :], ACT.Copy).then_inc(s_lhi, 1)

                def att(pair, hh):
                    act.wait_ge(s_cap, CREDIT + 2 * pair + hh + 1)
                    nc.scalar.activation(e[:, hh, :], zf(hh), ACT.Exp).then_inc(s_att, 1)

                def yhi(what, a, filled):
                    act.wait_ge(s_fill, CREDIT + filled)
                    for rows, bank, src, dst in y_parts(what):
                        nc.scalar.activation(y_hi[rows, a, dst], ps[rows, bank, src], ACT.Copy).then_inc(s_ohi, 1)

                def section(uses, fills, slot, t, r, a):
                    def fill(use):
                        return fills + uses.index(use) + 1

                    split_hi(c, slot, t, 8, fill(f"q{r}b"))
                    lhi(2 * t + a, 0)
                    lhi(2 * t + a, 1)
                    split_hi(c, slot + 1, t, 8, fill(f"k{r}b"))
                    split_hi(c, slot + 2, t, 8, fill(f"v{r}b"))
                    att(2 * t + a, 0)
                    att(2 * t + a, 1)
                    yhi("A", a, fill(f"AA{a}"))
                    yhi("B", a, fill(f"AB{a}"))
                    soft(0, 2 * t + r, 0, fill(f"ZA{r}"))
                    yhi("S", a, fill(f"AS{a}"))
                    soft(1, 2 * t + r, 0, fill(f"ZB{r}"))
                    soft_rest(2 * t + r)

                fills = c["fill"]
                for m, name in enumerate("qkv"):
                    split_hi(c, m, 0, 0, fills + SB_PRE.index(f"{name}0b") + 1)
                soft(0, 0, 0, fills + SB_PRE.index("ZA0") + 1)
                soft(1, 0, 0, fills + SB_PRE.index("ZB0") + 1)
                soft_rest(0)
                fills += len(SB_PRE)
                with act.Fori(0, SB_STEPS) as t:
                    before = fills + len(SB_BODY) * t
                    section(SB_BODY, before, 3, t, 1, 0)
                    section(SB_BODY, before, 6, t, 2, 1)
                    split_hi(c, 9, t, 8, before + SB_BODY.index("w3b") + 1)
                    split_hi(c, 10, t, 8, before + SB_BODY.index("w7b") + 1)
                fills += len(SB_BODY) * SB_STEPS
                t = SB_STEPS
                section(SB_LAST, fills, 3, t, 1, 0)
                lhi(2 * t + 1, 0)
                lhi(2 * t + 1, 1)
                split_hi(c, 6 + 8 * t, 0, 0, fills + SB_LAST.index("y7b") + 1)
                att(2 * t + 1, 0)
                att(2 * t + 1, 1)
                for what in "ABS":
                    yhi(what, 1, fills + SB_LAST.index(f"A{what}1") + 1)
                frees = c["unit"] + 1 + SB_UNITS - units(SB_LAST)
                for d in range(KT):
                    feed(c["fed"] + KT, c["norm"] + 1, d, s_free, frees + units(SB_LAST, f"w{d}b"))
                split_hi(c, 7 + 8 * t, 0, 0, fills + SB_LAST.index("w7b") + 1)

            act.wait_ge(s_const, 48)
            for n in range(2):
                act.wait_ge(s_raw[n], 16)
                nc.scalar.activation(w_hi[:, n, :], raw[:, n, :], ACT.Copy).then_inc(s_whi, 1)
            for d in range(KT):
                act.wait_ge(s_x, 16 * KT)
                feed(0, 0, d, s_xup, 0)
            for c in plan:
                {"ffn": ffn, "ret": ret, "sb": stick, "ple": ple}[c["kind"]](c)
            root(dict(unit=at.unit))

        @block.gpsimd
        def _(pool):
            for s in (s_ssum, s_rd, s_km, s_qm, s_stp_kept, s_k_kept, s_v_kept):
                pool.sem_inc(s, CREDIT)

            def add_squares(fed, norm):
                for d in range(KT):
                    pool.wait_ge(s_sq, CREDIT + fed + d + 1)
                    if d == 0:
                        pool.wait_ge(s_ss, CREDIT + norm)
                        nc.gpsimd.tensor_copy(ssum[:], sq[:, 0, :]).then_inc(s_ssum, 1)
                    else:
                        pool.wait_ge(s_ssum, CREDIT + fed + d)
                        nc.gpsimd.tensor_tensor(ssum[:], ssum[:], sq[:, d % 2, :], ALU.add).then_inc(s_ssum, 1)

            def ffn(c):
                if c["split_p"]:
                    pool.wait_ge(s_fill, CREDIT + c["fill"])
                    pool.dma_start(p_raw[:], pT[c["ple"]].rearrange("k p t -> p k t")).then_inc(s_p, 16)

            def ret(c):
                o = c["unit"] + 1
                n_u = len(RET_USES)
                pool.wait_ge(s_fill, CREDIT + c["fill"])
                pool.dma_start(cs[:], cs_d).then_inc(s_ret_in, 16)
                pool.dma_start(rmask[:], rmask_d).then_inc(s_ret_in, 16)
                pool.dma_start(smask[:], smask_d).then_inc(s_ret_in, 16)
                pool.dma_start(gpow[:], gpow_d).then_inc(s_ret_in, 16)
                pool.dma_start(rd[:], dec_d[0]).then_inc(s_dec, 16)
                pool.dma_start(s0[:], st_d[0]).then_inc(s_s0, 16)
                nc.gpsimd.memset(qm[:], 0.0)
                pool.wait_ge(s_rstd, CREDIT + 5 * (c["norm"] + 1))

                def decay(h):
                    pool.wait_ge(s_dec, 16 * (h + 1))
                    nc.gpsimd.tensor_tensor(rd[:, 0, :], rd[:, 0, :], rstd[:], ALU.mult)
                    nc.gpsimd.tensor_tensor(rd[:, 1, :], rd[:, 1, :], rstd[:], ALU.mult).then_inc(s_rd, 1)

                decay(0)
                pool.wait_ge(s_ret_in, 64)

                def body(i, last):
                    for hh in range(2):
                        h = 2 * i + hh
                        pool.wait_ge(s_rot, CREDIT + 2 * h + 1)
                        apart(pool)
                        nc.gpsimd.tensor_copy(qm[:].rearrange("p (s c) -> p s c", s=STREAMS)[:, :, 0:STEP],
                                              qf[:, SEQ:TOK].rearrange("p (s c) -> p s c", s=STREAMS)).then_inc(s_qm, 1)
                        pool.wait_ge(s_free, CREDIT + o + RET_USES.index(f"Tk{hh}") + n_u * i + 1)
                        nc.gpsimd.tensor_tensor(km[:], kn[:, 4, :].unsqueeze(1).to_broadcast([P, STREAMS, P]),
                                                smask[:].unsqueeze(2).to_broadcast([P, STREAMS, P]),
                                                ALU.mult).then_inc(s_km, 1)
                        if not (last and hh):
                            apart(pool)
                            pool.dma_start(rd[:], dec_d[h + 1]).then_inc(s_dec, 16)
                            decay(h + 1)
                        pool.wait_ge(s_stp, CREDIT + h + 1)
                        apart(pool)
                        pool.dma_start(stp_o[h], stp[:]).then_inc(s_stp_out, 16)
                        for half in range(2):
                            pool.wait_ge(s_sts, CREDIT + 2 * h + half + 1)
                            apart(pool)
                            pool.dma_start(sts_o[h, :, 4 * half:4 * half + 4, :],
                                           s0[:, 4 * half:4 * half + 4, :]).then_inc(s_sts_out, 16)
                        pool.wait_ge(s_stp_out, 16 * (h + 1))
                        pool.sem_inc(s_stp_kept, 1)
                        if not (last and hh):
                            pool.wait_ge(s_sts_out, 32 * (h + 1))
                            apart(pool)
                            pool.dma_start(s0[:], st_d[h + 1]).then_inc(s_s0, 16)

                with pool.Fori(0, 3) as i:
                    body(i, False)
                body(3, True)
                pool.wait_ge(s_stp_out, 16 * H_RET)
                pool.wait_ge(s_sts_out, 32 * H_RET)

            def stick(c):
                o = c["unit"] + 1
                pool.wait_ge(s_fill, CREDIT + c["fill"])
                pool.dma_start(negtri[:], negtri_d).then_inc(s_sb_in, 16)
                pool.dma_start(bmask[:], bmask_d).then_inc(s_sb_in, 16)
                pool.dma_start(bcap[:], bcap_d).then_inc(s_sb_in, 16)

                def load(pair, par):
                    pool.dma_start(kc[:, par, :, :], kc_d[pair]).then_inc(s_kv[par], 16)
                    pool.dma_start(vc[:, par, :, :], vc_d[pair]).then_inc(s_kv[par], 16)

                def store(pair, par, k_free, v_free):
                    pool.wait_ge(s_free, CREDIT + k_free)
                    apart(pool)
                    pool.dma_start(k_o[pair], bk[:, par, :]).then_inc(s_k_out, 16)
                    pool.wait_ge(s_k_out, 16 * pair + 16)
                    pool.sem_inc(s_k_kept, 1)
                    pool.wait_ge(s_free, CREDIT + v_free)
                    apart(pool)
                    pool.dma_start(v_o[pair], bvt[:]).then_inc(s_v_out, 16)
                    pool.wait_ge(s_v_out, 16 * pair + 16)
                    pool.sem_inc(s_v_kept, 1)

                load(0, 0)
                load(1, 1)
                store(0, 0, o + units(SB_PRE, "k0b"), o + units(SB_PRE, "v0b"))
                o += units(SB_PRE)
                fills = c["fill"] + len(SB_PRE)
                with pool.Fori(0, SB_STEPS) as t:
                    for r, a in ((1, 0), (2, 1)):
                        store(2 * t + r, r % 2, o + units(SB_BODY, f"k{r}b") + units(SB_BODY) * t,
                              o + units(SB_BODY, f"v{r}b") + units(SB_BODY) * t)
                        pool.wait_ge(s_fill, CREDIT + fills + SB_BODY.index(f"AS{a}") + 1 + len(SB_BODY) * t)
                        apart(pool)
                        load(2 * t + a + 2, a)
                o += units(SB_BODY) * SB_STEPS
                store(PAIRS - 1, 1, o + units(SB_LAST, "k1b"), o + units(SB_LAST, "v1b"))
                pool.wait_ge(s_k_out, 16 * PAIRS)
                pool.wait_ge(s_v_out, 16 * PAIRS)

            add_squares(0, 0)
            for c in plan:
                {"ffn": ffn, "ret": ret, "sb": stick, "ple": lambda c: None}[c["kind"]](c)
                add_squares(c["fed"] + KT, c["norm"] + 1)

        @block.vector
        def _(dve):
            for s in (s_free, s_wlo, s_xlo, s_rstd, s_glo, s_plo, s_sr, s_pm, s_xup, s_out, s_rt, s_rot, s_kvs,
                      s_aggr, s_gn, s_ylo, s_sp, s_llo, s_cap):
                dve.sem_inc(s, CREDIT)
            tt, ts, stt = nc.vector.tensor_tensor, nc.vector.tensor_scalar, nc.vector.scalar_tensor_tensor

            def split_lo(c, m, i, per):
                cols = next_cols(c, m)
                if cols is None:
                    return
                n = c["n"] + m + 2 + per * i
                r, _ = landed(c, m + 2)
                p = (c["n"] + m) % 2
                dve.wait_ge(s_whi, CREDIT + n + 1)
                tt(w_lo[:, p, 0:cols], raw[:, r, 0:cols], w_hi[:, p, 0:cols].bitcast(F), ALU.subtract).then_inc(s_wlo, 1)

            def feed_lo(c_fed, norm, d):
                dve.wait_ge(s_xhi, CREDIT + c_fed + d + 1)
                stt(out=x_lo[:, d, :], in0=x[:, d, :], scalar=gain[:, norm, d:d + 1],
                    in1=x_hi[:, d, :].bitcast(F), op0=ALU.mult, op1=ALU.subtract).then_inc(s_xlo, 1)

            def one_over_rms(c, norm):
                u = c["ss"]
                dve.wait_ge(s_ss, CREDIT + norm + 1)
                ts(halves(scr[:, 0, :]), acc(u), 1.0 / D, EPS, ALU.mult, ALU.add).then_inc(s_free, 1)
                k = 5 * norm
                dve.wait_ge(s_root, CREDIT + norm + 1)
                nc.vector.reciprocal(scr[:, 2, :], scr[:, 1, :]).then_inc(s_rstd, 1)
                dve.wait_ge(s_rstd, CREDIT + k + 1)
                tt(scr[:, 3, :], scr[:, 2, :], scr[:, 2, :], ALU.mult).then_inc(s_rstd, 1)
                dve.wait_ge(s_rstd, CREDIT + k + 2)
                tt(scr[:, 1, :], scr[:, 3, :], scr[:, 0, :], ALU.mult).then_inc(s_rstd, 1)
                dve.wait_ge(s_rstd, CREDIT + k + 3)
                ts(scr[:, 3, :], scr[:, 1, :], -0.5, 1.5, ALU.mult, ALU.add).then_inc(s_rstd, 1)
                dve.wait_ge(s_rstd, CREDIT + k + 4)
                tt(rstd[:], scr[:, 2, :], scr[:, 3, :], ALU.mult).then_inc(s_rstd, 1)
                dve.wait_ge(s_rstd, CREDIT + k + 5)

            def ffn(c):
                m = 0
                o = c["unit"] + 1
                for nf_at, nf in enumerate(PIECES):
                    gbase = c["g"] + sum(PIECES[:nf_at])

                    def body(i, m=m, gbase=gbase, nf_at=nf_at):
                        first = isinstance(i, int) and i == 0 and nf_at == 0
                        if first:
                            for j in range(2):
                                split_lo(c, m + j, 0, 0)
                            one_over_rms(c, c["norm"])
                        for j in range(4):
                            u = (o + m + j) % 4
                            f = gbase + 2 * i + j // 2
                            t = scr[:, j // 2, :]
                            dve.wait_ge(s_fill, CREDIT + c["fill"] + m + j + 4 * i + 1)
                            if j % 2 == 0:
                                dve.wait_ge(s_glo, CREDIT + f - 1)
                                tt(halves(t), acc(u), halves(rstd[:]), ALU.mult).then_inc(s_free, 1)
                                if j or not first:
                                    split_lo(c, m + j, i, 4)
                                dve.wait_ge(s_silu, CREDIT + f + 1)
                                tt(scr[:, 2 + j // 2, :], scr[:, 2 + j // 2, :], rstd[:], ALU.mult).then_inc(s_sr, 1)
                            else:
                                dve.wait_ge(s_sr, CREDIT + f + 1)
                                tt(halves(t), acc(u), halves(scr[:, 2 + j // 2, :]), ALU.mult).then_inc(s_free, 1)
                                dve.wait_ge(s_ghi, CREDIT + f + 1)
                                fi = 2 * i + j // 2
                                tt(g_lo[:, fi, :], t, g_hi[:, fi, :].bitcast(F), ALU.subtract).then_inc(s_glo, 1)
                                if j >= 2 or not first:
                                    split_lo(c, m + j, i, 4)
                    lo = 0
                    if nf_at == 0:
                        body(0)
                        lo = 1
                    with dve.Fori(lo, nf // 2) as i:
                        body(i)
                    m += 2 * nf
                    if nf_at == 0 and c["split_p"]:
                        dve.wait_ge(s_phi, CREDIT + c["ple"] + 1)
                        tt(p_lo[:], p_raw[:], p_hi[:].bitcast(F), ALU.subtract).then_inc(s_plo, 1)

                    def down(i, j, feed, m=m):
                        u = (o + m + j) % 4
                        d = 4 * i + j
                        dve.wait_ge(s_fill, CREDIT + c["fill"] + m + d + 1)
                        xd = halves(x[:, d, :])
                        stt(out=xd, in0=acc(u), scalar=0.5, in1=xd, op0=ALU.mult, op1=ALU.add).then_inc(s_free, 1)
                        split_lo(c, m + j, i, 4) if not isinstance(i, int) else split_lo(c, m + d, 0, 0)
                        if feed:
                            feed_lo(c["fed"] + KT, c["norm"] + 1, d)
                    if nf_at < 2:
                        with dve.Fori(0, KT // 4) as i:
                            for j in range(4):
                                down(i, j, False)
                    else:
                        for d in range(KT):
                            down(d // 4, d % 4, True)
                    m += KT

            def ple(c):
                unit = c["unit"] + 1
                fill = c["fill"]
                for m in range(2):
                    if m == 0:
                        one_over_rms(c, c["norm"])
                    for t in range(4):
                        dve.wait_ge(s_fill, CREDIT + fill + 1)
                        nc.vector.tensor_copy(halves(proj[:, 4 * m + t, :]), acc(unit % 4)).then_inc(s_free, 1)
                        unit, fill = unit + 1, fill + 1
                    split_lo(c, m, 0, 0)
                for d in range(KT):
                    dve.wait_ge(s_fill, CREDIT + fill + 1)
                    dve.wait_ge(s_sig, CREDIT + KT * c["ple"] + d - 1)
                    tt(halves(scr[:, d % 2, :]), acc(unit % 4), halves(rstd[:]), ALU.mult).then_inc(s_free, 1)
                    unit, fill = unit + 1, fill + 1
                    split_lo(c, 2 + d, 0, 0)
                    t = scr[:, 2 + d % 2, :]
                    dve.wait_ge(s_sig, CREDIT + KT * c["ple"] + d + 1)
                    tt(t, t, proj[:, d, :], ALU.mult).then_inc(s_pm, 1)
                    dve.wait_ge(s_pm, CREDIT + KT * c["ple"] + d + 1)
                    tt(x[:, d, :], x[:, d, :], t, ALU.add).then_inc(s_xup, 1)
                if not c["last"]:
                    for d in range(KT):
                        feed_lo(c["fed"] + KT, c["norm"] + 1, d)

            def ret(c):
                one_over_rms(c, c["norm"])
                o = c["unit"] + 1
                uses = RET_USES
                n_u = len(uses)
                dve.wait_ge(s_ret_in, 64)

                def body(i, last):
                    def u(use):
                        return (o + uses.index(use)) % 4

                    def fill(use):
                        return c["fill"] + uses.index(use) + n_u * i + 1

                    for hh in range(2):
                        h = 2 * i + hh
                        gk = 7 * h

                        def rot(name, out):
                            use = f"{name}{hh}"
                            n = "qk".index(name)
                            dve.wait_ge(s_fill, CREDIT + fill(use))
                            dve.wait_ge(s_rd, CREDIT + h + 1)
                            tt(halves(scr[:, 0, :]), acc(u(use)), halves(rd[:, n, :]), ALU.mult).then_inc(s_free, 1)
                            dve.wait_ge(s_free, CREDIT + o + uses.index(use) + n_u * i + 1)
                            tt(out, scr[:, 0, :], cs[:, 0, :], ALU.mult).then_inc(s_rt, 1)
                            dve.wait_ge(s_swap, CREDIT + 4 * h + 2 * n + 2)
                            tt(scr[:, 1, :], scr[:, 1, :], cs[:, 1, :], ALU.mult).then_inc(s_rt, 1)
                            dve.wait_ge(s_rt, CREDIT + 4 * h + 2 * n + 2)
                            tt(out, out, scr[:, 1, :], ALU.add).then_inc(s_rot, 1)
                            split_lo(c, 6 * hh + n, i, 16)

                        def to(ho):
                            for j in range(2):
                                use = f"TO{ho}{j}"
                                dve.wait_ge(s_fill, CREDIT + fill(use))
                                hcount = 2 * i + ho
                                dve.wait_ge(s_gate, CREDIT + 2 * hcount + j + 1)
                                dve.wait_ge(s_ylo, CREDIT + 2 * hcount + j - 1)
                                tt(scr[:, 2 + j, :], flat(u(use))[:, 0:TOK], sg[:, j, :], ALU.mult).then_inc(s_free, 1)
                                dve.wait_ge(s_yhi, CREDIT + 2 * hcount + j + 1)
                                tt(y_lo[:, 2 * ho + j, :], scr[:, 2 + j, :], y_hi[:, 2 * ho + j, :].bitcast(F),
                                   ALU.subtract).then_inc(s_ylo, 1)

                        rot("q", qf[:])
                        if hh:
                            to(0)
                        rot("k", kf[:])
                        dve.wait_ge(s_fill, CREDIT + fill(f"v{hh}0"))
                        tt(halves(vt_o[:, 0:TOK]), acc(u(f"v{hh}0")), halves(rstd[:]), ALU.mult).then_inc(s_free, 1)
                        split_lo(c, 6 * hh + 2, i, 16)
                        dve.wait_ge(s_fill, CREDIT + fill(f"Tk{hh}"))
                        nc.vector.tensor_copy(kn[:].rearrange("p t c -> p (t c)"), flat(u(f"Tk{hh}"))[:, 0:TOK]).then_inc(s_free, 1)
                        dve.wait_ge(s_fill, CREDIT + fill(f"v{hh}1"))
                        tt(halves(vt_o[:, TOK:2 * TOK]), acc(u(f"v{hh}1")), halves(rstd[:]), ALU.mult).then_inc(s_free, 1)
                        split_lo(c, 6 * hh + 3, i, 16)

                        def by_token(j):
                            use = f"Tv{hh}{j}"
                            dve.wait_ge(s_fill, CREDIT + fill(use))
                            nc.vector.tensor_copy(vn[:, :, j * P:(j + 1) * P],
                                                  flat(u(use))[:, 0:TOK].rearrange("p (t c) -> p t c", t=TT)).then_inc(s_free, 1)
                        by_token(0)
                        dve.wait_ge(s_fill, CREDIT + fill(f"SC{hh}"))
                        tt(sc[:].rearrange("p t c -> p (t c)"), flat(u(f"SC{hh}"))[:, 0:TOK],
                           rmask[:].rearrange("p t c -> p (t c)"), ALU.mult).then_inc(s_free, 1)

                        def gate(j):
                            use = f"g{hh}{j}"
                            dve.wait_ge(s_fill, CREDIT + fill(use))
                            tt(halves(sg[:, j, :]), acc(u(use)), halves(rstd[:]), ALU.mult).then_inc(s_free, 1)
                            split_lo(c, 6 * hh + 4 + j, i, 16)
                        gate(0)
                        by_token(1)
                        gate(1)
                        dve.wait_ge(s_fill, CREDIT + fill(f"KV{hh}"))
                        dve.wait_ge(s_stp, CREDIT + h)
                        kv = flat(u(f"KV{hh}"))
                        nc.vector.tensor_copy(sp_[:, 0, :], kv[:, 0:DV]).then_inc(s_kvs, 1)
                        for t in range(1, 4):
                            dve.wait_ge(s_kvs, CREDIT + 3 * h + t)
                            tt(sp_[:, t, :], kv[:, t * DV:(t + 1) * DV], sp_[:, t - 1, :],
                               ALU.add).then_inc(s_kvs if t < 3 else s_free, 1)
                        dve.wait_ge(s_fill, CREDIT + fill(f"OS{hh}"))
                        osf = flat(u(f"OS{hh}"))
                        nc.vector.bn_stats(bst[:, 4, :], osf[:, 0:DV])
                        dve.wait_ge(s_fill, CREDIT + fill(f"OP{hh}"))
                        opf = flat(u(f"OP{hh}"))
                        for t in range(4):
                            op = nc.vector.bn_stats(bst[:, t, :], opf[:, t * DV:(t + 1) * DV])
                        op.then_inc(s_gn, 1)
                        dve.wait_ge(s_gn, CREDIT + gk + 1)
                        apart(dve)
                        for t in range(TT):
                            op = nc.vector.bn_aggr(mv[:, t, :], bst[:, t, :])
                        op.then_inc(s_aggr, 1)
                        dve.wait_ge(s_aggr, CREDIT + h + 1)
                        ts(gn[:, 0, :], mv[:, :, 1], GN_EPS, None, ALU.add).then_inc(s_gn, 1)
                        dve.wait_ge(s_groot, CREDIT + h + 1)
                        nc.vector.reciprocal(gn[:, 2, :], gn[:, 1, :]).then_inc(s_gn, 1)
                        dve.wait_ge(s_gn, CREDIT + gk + 3)
                        tt(gn[:, 3, :], gn[:, 2, :], gn[:, 2, :], ALU.mult).then_inc(s_gn, 1)
                        dve.wait_ge(s_gn, CREDIT + gk + 4)
                        tt(gn[:, 3, :], gn[:, 3, :], gn[:, 0, :], ALU.mult).then_inc(s_gn, 1)
                        dve.wait_ge(s_gn, CREDIT + gk + 5)
                        ts(gn[:, 3, :], gn[:, 3, :], -0.5, 1.5, ALU.mult, ALU.add).then_inc(s_gn, 1)
                        dve.wait_ge(s_gn, CREDIT + gk + 6)
                        tt(gn[:, 4, :], gn[:, 2, :], gn[:, 3, :], ALU.mult).then_inc(s_gn, 1)
                        dve.wait_ge(s_gn, CREDIT + gk + 7)
                        for t in (4, 0, 1, 2, 3):
                            src = osf[:, 0:DV] if t == 4 else opf[:, t * DV:(t + 1) * DV]
                            op = ts(vt_o[:, t * DV:(t + 1) * DV], src, mv[:, t, 0:1], gn[:, 4, t:t + 1], ALU.subtract, ALU.mult)
                            if t in (3, 4):
                                op.then_inc(s_free, 1)
                        for half in range(2):
                            use = f"SS{hh}{half}"
                            dve.wait_ge(s_fill, CREDIT + fill(use))
                            s4 = s0[:, 4 * half:4 * half + 4, :].rearrange("p s c -> p (s c)")
                            tt(s4, s4, flat(u(use)), ALU.add).then_inc(s_free, 1)
                    to(1)
                    for d in range(KT):
                        use = f"w{d}"
                        dve.wait_ge(s_fill, CREDIT + fill(use))
                        xd = halves(x[:, d, :])
                        tt(xd, xd, acc(u(use)), ALU.add).then_inc(s_free, 1)
                        if d % 2:
                            split_lo(c, 12 + d // 2, i, 16)
                        if last:
                            feed_lo(c["fed"] + KT, c["norm"] + 1, d)

                with dve.Fori(0, 3) as i:
                    body(i, False)
                body(3, True)

            def stick(c):
                one_over_rms(c, c["norm"])
                dve.wait_ge(s_sb_in, 48)

                def masked(t, piece, table, op):
                    by_bank = t.rearrange("p (b c) -> p b c", b=3)
                    last_two = t[:, 768:ZC].rearrange("p (b c) -> p b c", b=2)[:, :, P:2 * P]
                    if piece == 0:
                        first = by_bank[:, :, 0:P]
                        tt(first, first, table[:, 0:1, :].to_broadcast([P, 3, P]), op)
                        return tt(last_two, last_two, table[:, 0:1, :].to_broadcast([P, 2, P]), op)
                    first, end = by_bank[:, 0:2, 0:P], t[:, Z_NEW + P:ZC]
                    tt(first, first, table[:, 0:1, :].to_broadcast([P, 2, P]), op)
                    tt(last_two, last_two, table[:], op)
                    return tt(end, end, table[:, 1, :], op)

                def softplus(piece, pair):
                    dve.wait_ge(s_soft, CREDIT + 6 * pair + 4 + piece + 1)
                    stt(out=e[:, piece, :], in0=zf(piece), scalar=0.0, in1=e[:, piece, :],
                        op0=ALU.max, op1=ALU.add).then_inc(s_sp, 1)
                    dve.wait_ge(s_sp, CREDIT + 2 * (2 * pair + piece) + 1)
                    masked(e[:, piece, :], piece, bmask, ALU.mult).then_inc(s_sp, 1)

                def llo(piece, pair):
                    dve.wait_ge(s_lhi, CREDIT + 2 * pair + piece + 1)
                    tt(l_lo[:, piece, :], e[:, piece, :], l_hi[:, piece, :].bitcast(F), ALU.subtract).then_inc(s_llo, 1)

                def cap(piece, filled):
                    dve.wait_ge(s_fill, CREDIT + filled)
                    masked(zf(piece), piece, bcap, ALU.min).then_inc(s_cap, 1)

                def ylo(what, pair, a):
                    for n, (rows, bank, src, dst) in enumerate(y_parts(what)):
                        dve.wait_ge(s_ohi, CREDIT + 4 * pair + "ABS".index(what) + n + 1)
                        op = tt(y_lo[rows, a, dst], ps[rows, bank, src], y_hi[rows, a, dst].bitcast(F), ALU.subtract)
                    op.then_inc(s_free, 2 if what == "S" else 1)

                def half(name, pair, par, h, filled):
                    cols = slice(HALF * h, HALF * (h + 1))
                    dve.wait_ge(s_fill, CREDIT + filled)
                    if name == "q":
                        op = stt(out=bq[:, par, cols], in0=ps[:, h, 0:HALF], scalar=HD ** -0.5, in1=rstd[:, cols],
                                 op0=ALU.mult, op1=ALU.mult)
                        for head in range(2 * h):
                            rows = slice(HD * head, HD * (head + 1))
                            op = stt(out=bqs[rows, :, head, :],
                                     in0=ps[rows, 1, SEQ - HALF:HALF].rearrange("p (s q) -> p s q", s=STREAMS),
                                     scalar=HD ** -0.5,
                                     in1=rstd[rows, SEQ:TOK].rearrange("p (s q) -> p s q", s=STREAMS),
                                     op0=ALU.mult, op1=ALU.mult)
                        op.then_inc(s_free, 1)
                    elif name == "k":
                        if h == 0:
                            dve.wait_ge(s_k_kept, CREDIT + pair - 1)
                        tt(bk[:, par, cols], ps[:, h, 0:HALF], rstd[:, cols], ALU.mult).then_inc(s_free, 1)
                    else:
                        if h == 0:
                            dve.wait_ge(s_v_kept, CREDIT + pair)
                        tt(bvt[:, cols], ps[:, h, 0:HALF], rstd[:, cols], ALU.mult).then_inc(s_free, 1)

                def by_token(par, filled):
                    dve.wait_ge(s_fill, CREDIT + filled)
                    nc.vector.tensor_copy(bv[:, par, :, :].rearrange("p t c -> p (t c)"),
                                          flat(0)[:, 0:TOK]).then_inc(s_free, 2)

                def section(uses, fills, slot, t, r, a):
                    def fill(use):
                        return fills + uses.index(use) + 1

                    pr, pa, par = 2 * t + r, 2 * t + a, r % 2
                    half("q", pr, par, 0, fill(f"q{r}a"))
                    softplus(0, pa)
                    half("q", pr, par, 1, fill(f"q{r}b"))
                    split_lo(c, slot, t, 8)
                    softplus(1, pa)
                    half("k", pr, par, 0, fill(f"k{r}a"))
                    llo(0, pa)
                    half("k", pr, par, 1, fill(f"k{r}b"))
                    llo(1, pa)
                    split_lo(c, slot + 1, t, 8)
                    half("v", pr, par, 0, fill(f"v{r}a"))
                    half("v", pr, par, 1, fill(f"v{r}b"))
                    split_lo(c, slot + 2, t, 8)
                    cap(0, fill(f"RA{a}"))
                    by_token(par, fill(f"T{r}"))
                    cap(1, fill(f"RB{a}"))
                    for what in "ABS":
                        ylo(what, pa, a)

                def add(d, h, filled):
                    cols = slice(HALF * h, HALF * (h + 1))
                    dve.wait_ge(s_fill, CREDIT + filled)
                    tt(x[:, d, cols], x[:, d, cols], ps[:, h, 0:HALF], ALU.add).then_inc(s_free, 1)

                nc.vector.memset(bqs[0:HD, :, 1, :], 0.0)
                nc.vector.memset(bqs[HD:P, :, 0, :], 0.0)
                fills = c["fill"]
                for m, name in enumerate("qkv"):
                    for h in range(2):
                        half(name, 0, 0, h, fills + SB_PRE.index(f"{name}0{'ab'[h]}") + 1)
                    split_lo(c, m, 0, 0)
                by_token(0, fills + SB_PRE.index("T0") + 1)
                fills += len(SB_PRE)
                with dve.Fori(0, SB_STEPS) as t:
                    before = fills + len(SB_BODY) * t
                    section(SB_BODY, before, 3, t, 1, 0)
                    section(SB_BODY, before, 6, t, 2, 1)
                    for d in range(KT):
                        for h in range(2):
                            add(d, h, before + SB_BODY.index(f"w{d}{'ab'[h]}") + 1)
                        if d % 4 == 3:
                            split_lo(c, 9 + d // 4, t, 8)
                fills += len(SB_BODY) * SB_STEPS
                t = SB_STEPS
                section(SB_LAST, fills, 3, t, 1, 0)
                for d in range(KT):
                    for h in range(2):
                        add(d, h, fills + SB_LAST.index(f"y{d}{'ab'[h]}") + 1)
                    if d in (3, 5):
                        softplus(d // 4, 2 * t + 1)
                for hh in range(2):
                    llo(hh, 2 * t + 1)
                split_lo(c, 6 + 8 * t, 0, 0)
                for hh in range(2):
                    cap(hh, fills + SB_LAST.index(f"R{'AB'[hh]}1") + 1)
                for what in "ABS":
                    ylo(what, 2 * t + 1, 1)
                for d in range(KT):
                    for h in range(2):
                        add(d, h, fills + SB_LAST.index(f"w{d}{'ab'[h]}") + 1)
                    feed_lo(c["fed"] + KT, c["norm"] + 1, d)
                split_lo(c, 7 + 8 * t, 0, 0)

            dve.wait_ge(s_const, 48)
            for n in range(2):
                dve.wait_ge(s_whi, CREDIT + n + 1)
                tt(w_lo[:, n, :], raw[:, n, :], w_hi[:, n, :].bitcast(F), ALU.subtract).then_inc(s_wlo, 1)
            for d in range(KT):
                feed_lo(0, 0, d)
            for c in plan:
                {"ffn": ffn, "ret": ret, "sb": stick, "ple": ple}[c["kind"]](c)
            one_over_rms(dict(ss=at.unit % 4), len(plan))
            for d in range(KT):
                if d >= 4:
                    dve.wait_ge(s_y_out[d % 4], 16 * (d // 4))
                stt(out=scr[:, d % 4, :], in0=x[:, d, :], scalar=gain[:, len(plan), d:d + 1], in1=rstd[:],
                    op0=ALU.mult, op1=ALU.mult).then_inc(s_out, 1)


PHASES = ["ffn", "ret", "ffn", "ple", "ffn", "sb", "ffn", "ple"]


def _slots(w, np):
    k, n = w.shape[0] // P, w.shape[1] // P
    return w.reshape(k, P, n, P).transpose(2, 1, 0, 3)


def _stream(inputs, phases, np):
    out, ffn_at, ret_at, sb_at, ple_at = [], 0, 0, 0, 0

    def put(blocks):
        for b in blocks:
            b = b.reshape(P, -1)
            if b.shape[1] < D:
                b = np.concatenate([b, np.zeros((P, D - b.shape[1]), b.dtype)], 1)
            out.append(b)

    def w_out_part(w, i):
        s = _slots(w[4 * i * P:4 * (i + 1) * P], np)
        put(np.concatenate([s[2 * t], s[2 * t + 1]], 1) for t in range(KT // 2))

    for ph in phases:
        if ph == "ffn":
            ab, layer = "ab"[ffn_at % 2], ffn_at // 2
            gu = _slots(inputs[f"w_ffn_{ab}_gu"][layer], np)
            down = inputs[f"w_ffn_{ab}_down"][layer]
            f0 = 0
            for nf in PIECES:
                for f in range(f0, f0 + nf):
                    put([gu[f], gu[D_FF // P + f]])
                put(_slots(down[f0 * P:(f0 + nf) * P], np))
                f0 += nf
            ffn_at += 1
        elif ph == "ret":
            s = _slots(inputs["ret_w_in"][ret_at], np)
            for i in range(4):
                for h in (2 * i, 2 * i + 1):
                    put([s[h], s[8 + h], s[16 + 2 * h], s[17 + 2 * h], s[32 + 2 * h], s[33 + 2 * h]])
                w_out_part(inputs["ret_w_out"][ret_at], i)
            ret_at += 1
        elif ph == "sb":
            s = _slots(inputs["sb_w_qkv"][sb_at], np)
            w = _slots(inputs["sb_w_out"][sb_at], np)

            def qkv(p):
                put([s[p], s[8 + p], s[16 + p]])

            qkv(0)
            for t in range(SB_STEPS):
                qkv(2 * t + 1)
                qkv(2 * t + 2)
                put(np.concatenate([w[d][:, 2 * t:2 * t + 2] for d in range(4 * m, 4 * m + 4)], 1) for m in range(2))
            qkv(PAIRS - 1)
            put(np.concatenate([w[d][:, p:p + 1] for d in range(KT)], 1) for p in (PAIRS - 2, PAIRS - 1))
            sb_at += 1
        else:
            s = _slots(inputs["ple_w_proj"][ple_at], np)
            put(np.concatenate([s[4 * m + t] for t in range(4)], 1) for m in range(2))
            put(_slots(inputs["ple_w_gate"][ple_at], np))
            ple_at += 1
    return np.stack(out)


def _constants(np):
    f32 = np.float32
    pos = np.concatenate([np.arange(SEQ), np.tile(128 + np.arange(STEP), STREAMS)]).astype(f32)
    idx = np.concatenate([np.arange(SEQ), np.tile(np.arange(STEP), STREAMS)]).astype(np.float64)
    freqs = (f32(10000.0) ** (-np.arange(64, dtype=f32) / f32(64))).astype(f32)
    ang = (freqs[:, None] * pos[None, :]).astype(f32).astype(np.float64)
    cos, sin = np.cos(ang), np.sin(ang)
    cs = np.stack([np.concatenate([cos, cos]), np.concatenate([-sin, sin])], 1)
    log_g = np.log1p(-(2.0 ** (-5.0 - np.arange(H_RET))))
    dq = np.exp((idx[None] + 1) * log_g[:, None])
    dk = np.exp(-(idx[None] + 1) * log_g[:, None]) * P ** -0.5
    dec = np.broadcast_to(np.stack([dq, dk], 1)[:, None], (H_RET, P, 2, TOK))
    gpow = np.broadcast_to(np.stack([np.exp(SEQ * log_g), np.exp(STEP * log_g)], 1)[None], (P, H_RET, 2))
    a = np.arange(P)
    same = a[:, None] // STEP == a[None, :] // STEP
    incl, strict = a[:, None] <= a[None, :], a[:, None] < a[None, :]
    rmask = np.stack([incl] * 4 + [incl & same], 1)
    seen = np.stack([strict, strict & same], 1)
    smask = a[:, None] // STEP == np.arange(STREAMS)[None, :]
    negtri = np.stack([-(a[:, None] >= a[None, :]).astype(f32), -np.ones((P, P), f32)], 1)
    out = dict(ones_d=np.ones((P, P)), ident_d=np.eye(P), negtri_d=negtri, cs_d=cs, dec_d=dec, rmask_d=rmask,
               smask_d=smask, gpow_d=gpow, bmask_d=seen, bcap_d=np.where(seen, 3e38, -1e30))
    return {k: np.ascontiguousarray(v, dtype=f32) for k, v in out.items()}


def _lay_out(inputs, phases, np):
    def tokens(prompt, sample):
        t = np.concatenate([prompt.reshape(SEQ, -1), sample.reshape(TOK - SEQ, -1)])
        return t.T.reshape(-1, P, TOK)

    a = dict(xT=tokens(inputs["x_prompt"], inputs["x_sample"]))
    a["pT"] = np.stack([tokens(inputs["p_prompt"][i], inputs["p_sample"][i]) for i in range(2)])
    layers = [inputs[n][i] for i in range(2) for n in ("norm_ffn_a", "norm_mix", "norm_ffn_b", "norm_ple")]
    gains = np.stack(layers[:len(phases)] + [inputs["norm_final"]] * (9 - len(layers[:len(phases)])))
    a["gains"] = gains.reshape(9, KT, P).transpose(2, 0, 1)
    a["wst"] = _stream(inputs, phases, np)
    a.update(_constants(np))
    a["st_d"] = inputs["state_ret"][0].transpose(1, 2, 0, 3)
    k, v = inputs["cache_sb_k"][0], inputs["cache_sb_v"][0]
    a["kc_d"] = k.reshape(STREAMS, P, PAIRS, P).transpose(2, 3, 0, 1)
    a["vc_d"] = v.reshape(STREAMS, P, PAIRS, P).transpose(2, 1, 0, 3)
    return {k: np.ascontiguousarray(v) for k, v in a.items()}


_ORDER = ["xT", "pT", "gains", "wst", "ones_d", "ident_d", "negtri_d", "cs_d", "dec_d", "rmask_d", "smask_d", "gpow_d",
          "bmask_d", "bcap_d", "st_d", "kc_d", "vc_d"]
_OUTS = [("y_o", (KT, P, TOK)), ("stp_o", (H_RET, P, DV)), ("sts_o", (H_RET, P, STREAMS, DV)),
         ("k_o", (PAIRS, P, TOK)), ("v_o", (PAIRS, P, TOK))]


def _program(nc, arrays, phases, mybir):
    args = [nc.dram_tensor(n, arrays[n].shape, mybir.dt.float32, kind="ExternalInput").ap() for n in _ORDER]
    args += [nc.dram_tensor(n, shape, mybir.dt.float32, kind="ExternalOutput").ap() for n, shape in _OUTS]
    trunk(nc, phases, *args)


def kernel(**inputs):
    import numpy as np
    import concourse.bacc as bacc
    from concourse import mybir
    from concourse.bass_utils import run_bass_kernel_spmd

    inputs = {k: np.asarray(v) for k, v in inputs.items()}
    arrays = _lay_out(inputs, PHASES, np)
    nc = bacc.Bacc("TRN2", target_bir_lowering=False, num_devices=1)
    _program(nc, arrays, PHASES, mybir)
    r = run_bass_kernel_spmd(nc, [arrays], core_ids=[0]).results[0]

    def back(t, tail):
        t = t.reshape(D, TOK).T
        return (np.ascontiguousarray(t[:SEQ]).reshape((1, SEQ) + tail),
                np.ascontiguousarray(t[SEQ:]).reshape((STREAMS, STEP) + tail))

    y_p, y_s = back(r["y_o"], (D,))
    k_p, k_s = back(r["k_o"], (H_SB, HD))
    v_p, v_s = back(r["v_o"], (H_SB, HD))
    st_p = np.ascontiguousarray(r["stp_o"]).reshape(1, 1, H_RET, P, DV)
    st_s = np.ascontiguousarray(r["sts_o"].transpose(2, 0, 1, 3))[None]
    return y_p, y_s, st_p, st_s, k_p[None], v_p[None], k_s[None], v_s[None]
```

```python
import math
from concourse import mybir
from contextlib import ExitStack

P = 128
D = 1024
KT = D // P
SEQ, STREAMS, STEP = 512, 8, 16
TOK = SEQ + STREAMS * STEP
TT = TOK // P
HALF = TOK // 2
H_RET, DV = 8, 256
H_SB, HD = 16, 64
PAIRS = H_SB * HD // P
D_FF = 2816
PIECES = (8, 8, 6)
assert sum(PIECES) * P == D_FF
FFN_SLOTS = sum(2 * nf + KT for nf in PIECES)
RET_SLOTS, SB_SLOTS, PLE_SLOTS = 64, 32, 10
N_SLOTS = 4 * FFN_SLOTS + RET_SLOTS + SB_SLOTS + 2 * PLE_SLOTS
CREDIT = 4
EPS, GN_EPS = 1e-6, 1e-5
LN_SHIFT = -40
ZC = 1536
ZB = {(0, 0): (0, 0), (0, 1): (0, 512), (0, 3): (0, 896), (0, 2): (0, 1024), (1, 2): (0, 1280),
      (1, 0): (1, 0), (1, 1): (1, 512), (1, 3): (1, 896)}
ZW = [SEQ - P * _b for _b in range(4)]
Z_PAST, Z_NEW = 1024, 1280

RET_PRE = ["q0", "k0"]
RET_BODY = []
for _h in range(2):
    RET_BODY += ["q1", "TO00", "TO01", "k1"] if _h else []
    RET_BODY += [f"V{_h}", f"U{_h}", f"Tk{_h}", f"SC{_h}", f"g{_h}0", f"g{_h}1",
                 f"KV{_h}", f"OS{_h}", f"OP{_h}", f"SS{_h}0", f"SS{_h}1"]
RET_LAST = [u for u in RET_BODY if u not in ("g11", "SS10", "SS11")]
RET_LAST += ["g11", "TO10", "TO11", "SS10", "SS11"] + [f"w{d}" for d in range(KT)]
RET_BODY += ["Q0", "TO10", "TO11", "K0"] + [f"w{d}" for d in range(KT)]
RET_STEPS = H_RET // 2
RET_FILLS = len(RET_PRE) + (RET_STEPS - 1) * len(RET_BODY) + len(RET_LAST)


def ret_slot(use, last=False):
    own = ["q0", "k0", "V0", "U0", "g00", "g01", "q1", "k1", "V1", "U1", "g10", "g11"] + ["Q0", "K0"] * (not last)
    return len(own) + int(use[1]) // 2 if use[0] == "w" else own.index(use)


def _sb_half_uses(r, a):
    out = [f"{n}{r}{h}" for n in "qkv" for h in "ab"]
    return out + [f"RA{a}", f"T{r}", f"RB{a}", f"AA{a}", f"AB{a}", f"ZA{r}", f"AS{a}", f"ZB{r}"]


def _w_uses(n):
    return [f"{n}{d}{h}" for d in range(KT) for h in "ab"]


SB_PRE = [f"{n}0{h}" for n in "qkv" for h in "ab"] + ["T0", "ZA0", "ZB0"]
SB_BODY = _sb_half_uses(1, 0) + _sb_half_uses(2, 1) + _w_uses("w")
SB_MID = _sb_half_uses(1, 0) + _sb_half_uses(2, 1)
SB_LAST = _sb_half_uses(1, 0) + _w_uses("w") + ["RA1", "RB1", "AA1", "AB1", "AS1"] + _w_uses("y")
SB_STEPS = H_SB // 4 - 2


PLE_USES = [(_k, _d) for _f in (0, 4) for _k in "gp" for _d in range(_f, _f + 4)]


def ple_slot(kind, d):
    return 4 + 5 * (d // 4) if kind == "p" else d + d // 4


def units(uses, use=None):
    upto = uses if use is None else uses[:uses.index(use) + 1]
    return sum(0 if u[0] in "ZR" else 2 if u[0] == "T" or u[:2] == "AS" else 1 for u in upto)


SB_FILLS = len(SB_PRE) + SB_STEPS * len(SB_BODY) + len(SB_MID) + len(SB_LAST)
SB_UNITS = units(SB_PRE) + SB_STEPS * units(SB_BODY) + units(SB_MID) + units(SB_LAST)


class At:

    def __init__(self, phases):
        self.of = []
        n = fill = unit = fed = g = ple = 0
        for i, ph in enumerate(phases):
            self.of.append(dict(i=i, kind=ph, n=n, fill=fill, unit=unit, fed=fed, g=g, ple=ple, norm=i,
                                ss=3 if ph == "sb" else unit % 4,
                                last=i == len(phases) - 1,
                                split_p=ph == "ffn" and phases[i + 1:i + 2] == ["ple"],
                                mixed=phases[i - 1] if i and phases[i - 1] in ("ret", "sb") else None))
            slots = {"ffn": FFN_SLOTS, "ret": RET_SLOTS, "sb": SB_SLOTS, "ple": PLE_SLOTS}[ph]
            fills = {"ffn": FFN_SLOTS, "ret": RET_FILLS, "sb": SB_FILLS, "ple": 16}[ph]
            units = {"ffn": FFN_SLOTS, "ret": RET_FILLS, "sb": SB_UNITS, "ple": 16}[ph]
            n, fill, unit, fed = n + slots, fill + fills, unit + units + 1, fed + KT
            g += sum(PIECES) * (ph == "ffn")
            ple += ph == "ple"
        self.end = dict(ss=unit % 4, fed=fed, unit=unit, norm=len(phases))


def trunk(nc, phases, xT, pT, gains, wst, ones_d, ident_d, negtri_d, cs_d, dec_d, rmask_d, smask_d, gpow_d,
          bmask_d, bcap_d, st_d, kc_d, vc_d, y_o, stp_o, sts_o, k_o, v_o):
    F, R = mybir.dt.float32, mybir.dt.float32r
    ALU, ACT = mybir.AluOpType, mybir.ActivationFunctionType
    at = At(phases)
    plan = at.of
    ctx = ExitStack()
    with ctx:
        def sb(name, shape, dt=F, on=ctx):
            return on.enter_context(nc.sbuf_tensor(name, shape, dt))

        x = sb("x", [P, KT, TOK])
        x_hi = sb("x_hi", [P, KT, TOK], R)
        x_lo = sb("x_lo", [P, KT, TOK], R)
        raw = sb("raw", [P, 4, D])
        w_hi = sb("w_hi", [P, 2, D], R)
        w_lo = sb("w_lo", [P, 2, D], R)
        sq = sb("sq", [P, 2, TOK])
        ssum = sb("ssum", [P, TOK])
        rstd = sb("rstd", [P, TOK])
        scr = sb("scr", [P, 4, TOK])
        gain = sb("gain", [P, 9, KT])
        unshift = sb("unshift", [P, 1])
        ones = sb("ones", [P, P])
        ident = sb("ident", [P, P])
        with ExitStack() as s:
            g_hi = sb("g_hi", [P, 8, TOK], R, s)
            g_lo = sb("g_lo", [P, 8, TOK], R, s)
            gate = sb("gate", [P, KT, TOK], F, s)
            p_raw = sb("p_raw", [P, 2, TOK], F, s)
            p_hi = sb("p_hi", [P, 2, TOK], R, s)
            p_lo = sb("p_lo", [P, 2, TOK], R, s)
        y_hi = sb("y_hi", [P, 4, TOK], R)
        y_lo = sb("y_lo", [P, 4, TOK], R)
        with ExitStack() as s:
            cs = sb("cs", [P, 2, TOK], F, s)
            rd = sb("rd", [P, 2, TOK], F, s)
            rmask = sb("rmask", [P, TT, P], F, s)
            smask = sb("smask", [P, STREAMS], F, s)
            gpow = sb("gpow", [P, H_RET, 2], F, s)
            qf = sb("qf", [P, TOK], F, s)
            kf = sb("kf", [P, TOK], F, s)
            kn = sb("kn", [P, TT, P], F, s)
            km = sb("km", [P, STREAMS, P], F, s)
            qm = sb("qm", [P, STREAMS * (P + STEP)], F, s)
            rstd_t = sb("rstd_t", [P, TT], F, s)
            o_n = sb("o_n", [P, 2 * TOK], F, s)
            vn = sb("vn", [P, TT, DV], F, s)
            sc = sb("sc", [P, TT, P], F, s)
            s0 = sb("s0", [P, STREAMS, DV], F, s)
            sp_ = sb("sp_", [P, 4, DV], F, s)
            stp = sb("stp", [P, DV], F, s)
            sg = sb("sg", [P, 2, TOK], F, s)
            bst = sb("bst", [P, TT, 6], F, s)
            mv = sb("mv", [P, TT, 2], F, s)
            gn = sb("gn", [P, 5, TT], F, s)
        with ExitStack() as s:
            negtri = sb("negtri", [P, 2, P], F, s)
            tri = sb("tri", [P, 2, P], R, s)
            bmask = sb("bmask", [P, 2, P], F, s)
            bcap = sb("bcap", [P, 2, P], F, s)
            bq = sb("bq", [P, 2, TOK], F, s)
            bqs = sb("bqs", [P, STREAMS, 2, STEP], F, s)
            bk = sb("bk", [P, 2, TOK], F, s)
            bvt = sb("bvt", [P, TOK], F, s)
            bv = sb("bv", [P, 2, TT, P], F, s)
            kc = sb("kc", [P, 2, STREAMS, P], F, s)
            vc = sb("vc", [P, 2, STREAMS, P], F, s)
            e = sb("e", [P, 2, ZC], F, s)
            l_hi = sb("l_hi", [P, 2, ZC], R, s)
            l_lo = sb("l_lo", [P, 2, ZC], R, s)
        ps = ctx.enter_context(nc.psum_tensor("ps", [P, 8, 512], F))

        def sem(name):
            return ctx.enter_context(nc.semaphore(name))

        s_raw = [sem(f"s_raw{r}") for r in range(4)]
        s_gain, s_const, s_p = sem("s_gain"), sem("s_const"), sem("s_p")
        s_x = [sem(f"s_x{k}") for k in range(KT)]
        s_ret_in, s_dec, s_s0 = sem("s_ret_in"), sem("s_dec"), sem("s_s0")
        s_sb_in, s_kv = sem("s_sb_in"), [sem("s_kv0"), sem("s_kv1")]
        s_y_out = [sem(f"s_y_out{k}") for k in range(4)]
        s_stp_out, s_sts_out = sem("s_stp_out"), sem("s_sts_out")
        s_k_out, s_v_out = sem("s_k_out"), sem("s_v_out")
        s_fill = sem("s_fill")
        s_ss = sem("s_ss")
        s_turn = sem("s_turn")
        s_row = sem("s_row")
        s_whi, s_xhi, s_sq, s_root = sem("s_whi"), sem("s_xhi"), sem("s_sq"), sem("s_root")
        s_silu, s_sig, s_gate, s_tri = sem("s_silu"), sem("s_sig"), sem("s_gate"), sem("s_tri")
        s_ghi, s_phi, s_ohi = sem("s_ghi"), sem("s_phi"), sem("s_ohi")
        s_swap, s_stp, s_sts, s_groot, s_yhi = sem("s_swap"), sem("s_stp"), sem("s_sts"), sem("s_groot"), sem("s_yhi")
        s_soft, s_lhi, s_att = sem("s_soft"), sem("s_lhi"), sem("s_att")
        s_free = sem("s_free")
        s_turned = sem("s_turned")
        s_wlo, s_xlo, s_rstd, s_glo, s_plo = sem("s_wlo"), sem("s_xlo"), sem("s_rstd"), sem("s_glo"), sem("s_plo")
        s_sr, s_xup, s_out = sem("s_sr"), sem("s_xup"), sem("s_out")
        s_rt, s_rot, s_kvs = sem("s_rt"), sem("s_rot"), sem("s_kvs")
        s_aggr, s_gn, s_ylo = sem("s_aggr"), sem("s_gn"), sem("s_ylo")
        s_sp, s_llo, s_cap = sem("s_sp"), sem("s_llo"), sem("s_cap")
        s_apart, s_unshift = sem("s_apart"), sem("s_unshift")
        s_ssum, s_rd, s_km, s_qm = sem("s_ssum"), sem("s_rd"), sem("s_km"), sem("s_qm")
        s_stp_kept, s_k_kept, s_v_kept = sem("s_stp_kept"), sem("s_k_kept"), sem("s_v_kept")

        def apart(eng):
            eng.sem_inc(s_apart, 1)

        def halves(ap):
            return ap.rearrange("p (b c) -> p b c", b=2)

        def acc(u):
            return ps[:, 2 * u:2 * u + 2, 0:HALF]

        def flat(u):
            return ps[:, 2 * u:2 * u + 2, :].rearrange("p b c -> p (b c)")

        def zf(piece):
            return ps[:, 2 + 3 * piece:5 + 3 * piece, :].rearrange("p b c -> p (b c)")

        def by_stream(cols, s):
            return cols.rearrange("p (h s q) -> p h s q", h=2, s=STREAMS)[:, :, s, :]

        def landed(c, m):
            n = c["n"] + m
            return n % 4, 16 * (n // 4 + 1)

        def slot_cols(kind, m):
            if kind == "ffn" and m >= FFN_SLOTS - KT:
                return PIECES[2] * P
            return D

        def next_cols(c, m):
            total = {"ffn": FFN_SLOTS, "ret": RET_SLOTS, "sb": SB_SLOTS, "ple": PLE_SLOTS}[c["kind"]]
            if m + 2 < total:
                return slot_cols(c["kind"], m + 2)
            return None if c["last"] else D

        def y_parts(what):
            top, bottom = slice(0, HD), slice(HD, P)
            return {"A": [(top, 0, slice(0, SEQ), slice(0, SEQ))],
                    "B": [(bottom, 1, slice(0, SEQ), slice(0, SEQ))],
                    "S": [(top, 0, slice(0, P), slice(SEQ, TOK)), (bottom, 0, slice(P, 2 * P), slice(SEQ, TOK))]}[what]

        block = ctx.enter_context(nc.Block())

        @block.sync
        def _(sp):

            def load(c, m, i=0, per=0, cols=D):
                n = c["n"] + m + per * i
                r, _ = landed(c, m)
                sp.wait_ge(s_wlo, CREDIT + n - 3)
                sp.dma_start(raw[:, r, 0:cols], wst[n, :, 0:cols]).then_inc(s_raw[r], 16)

            sp.dma_start(gain[:], gains).then_inc(s_gain, 16)
            sp.dma_start(raw[:, 0, :], wst[0]).then_inc(s_raw[0], 16)
            for k in range(KT):
                sp.dma_start(x[:, k, :], xT[k]).then_inc(s_x[k], 16)
                if k == 3:
                    sp.dma_start(raw[:, 1, :], wst[1]).then_inc(s_raw[1], 16)
            sp.dma_start(ones[:], ones_d).then_inc(s_const, 16)
            sp.dma_start(ident[:], ident_d).then_inc(s_const, 16)
            for m in (2, 3):
                load(plan[0], m)
            for c in plan:
                if c["kind"] == "ffn":
                    with sp.Fori(int(c["i"] == 0), (FFN_SLOTS - KT) // 4) as i:
                        for j in range(4):
                            load(c, j, i, 4)
                    with sp.Fori(0, KT // 4) as i:
                        for j in range(4):
                            load(c, FFN_SLOTS - KT + j, i, 4, PIECES[2] * P)
                elif c["kind"] in ("ret", "sb"):
                    with sp.Fori(0, {"ret": RET_SLOTS, "sb": SB_SLOTS}[c["kind"]] // 4) as i:
                        for j in range(4):
                            load(c, j, i, 4)
                else:
                    for m in range(PLE_SLOTS):
                        load(c, m)
            for d in range(KT):
                sp.wait_ge(s_out, CREDIT + d + 1)
                sp.dma_start(y_o[d], scr[:, d % 4, :]).then_inc(s_y_out[d % 4], 16)
            for s in s_y_out:
                sp.wait_ge(s, 16 * KT // 4)

        @block.tensor
        def _(pe):
            for s in (s_fill, s_ss, s_row, s_turn):
                pe.sem_inc(s, CREDIT)

            def mm3(out, wh, wl, xh, xl, start, stop):
                for q, (a, b) in enumerate(((wh, xh), (wh, xl), (wl, xh))):
                    for h in range(2):
                        last = nc.tensor.matmul(out[:, h, :], a, b[:, HALF * h:HALF * (h + 1)],
                                                start=start and q == 0, stop=stop and q == 2,
                                                skip_group_check=True)
                return last

            def project(c, m, i, per, u, blocks, src_hi, src_lo, before=None):
                p = (c["n"] + m) % 2
                for b, (wb, xb) in enumerate(blocks):
                    if before is not None:
                        before(b)
                    last = mm3(acc(u), w_hi[:, p, wb * P:(wb + 1) * P], w_lo[:, p, wb * P:(wb + 1) * P],
                               src_hi[:, xb, :], src_lo[:, xb, :], b == 0, b == len(blocks) - 1)
                last.then_inc(s_fill, 1)

            def sum_squares(c):
                u = c["ss"]
                pe.wait_ge(s_const, 32)
                pe.wait_ge(s_ssum, CREDIT + c["fed"] + KT)
                for h in range(2):
                    last = nc.tensor.matmul(acc(u)[:, h, :], ones[:], ssum[:, HALF * h:HALF * (h + 1)],
                                            start=True, stop=True)
                last.then_inc(s_ss, 1)

            def free_before(c, unit):
                return c["unit"] if c["mixed"] and unit < c["unit"] + 4 else unit - 3

            def fed(c):
                return lambda b: pe.wait_ge(s_xlo, CREDIT + c["fed"] + b + 1)

            def ffn(c):
                def step(m, i, per, first=False):
                    n, unit = c["n"] + m + per * i, c["unit"] + 1 + m + per * i
                    pe.wait_ge(s_wlo, CREDIT + n + 1)
                    pe.wait_ge(s_free, CREDIT + (free_before(c, unit) if first else unit - 3))

                m = 0
                ss_after = 0 if c["i"] else 1
                for nf_at, nf in enumerate(PIECES):
                    def body(i, m=m):
                        for j in range(4):
                            first = isinstance(i, int) and i == 0 and nf_at == 0
                            step(m + j, i, 4, first)
                            project(c, m + j, i, 4, (c["unit"] + 1 + m + j) % 4, [(k, k) for k in range(KT)],
                                    x_hi, x_lo, fed(c) if first and j == 0 else None)
                            if first and j == ss_after:
                                sum_squares(c)
                    lo = 0
                    if nf_at == 0:
                        body(0)
                        lo = 1
                    with pe.Fori(lo, nf // 2) as i:
                        body(i)
                    m += 2 * nf
                    done = c["g"] + sum(PIECES[:nf_at + 1])

                    def ready(b, nf=nf, done=done):
                        if b == 0:
                            pe.wait_ge(s_glo, CREDIT + done - 1)
                        if b == nf - 1:
                            pe.wait_ge(s_glo, CREDIT + done)
                    with pe.Fori(0, KT // 4) as i:
                        for j in range(4):
                            step(m + j, i, 4)
                            project(c, m + j, i, 4, (c["unit"] + 1 + m + j) % 4, [(k, k) for k in range(nf)],
                                    g_hi, g_lo, ready if j == 0 else None)
                    m += KT

            def ple(c):
                for n, (kind, d) in enumerate(PLE_USES):
                    unit = c["unit"] + 1 + n
                    slot = ple_slot(kind, d)
                    pe.wait_ge(s_wlo, CREDIT + c["n"] + slot + 1)
                    pe.wait_ge(s_free, CREDIT + free_before(c, unit))
                    if kind == "g":
                        project(c, slot, 0, 0, unit % 4, [(k, k) for k in range(KT)], x_hi, x_lo,
                                fed(c) if d == 0 else None)
                    else:
                        pe.wait_ge(s_plo, CREDIT + c["ple"] + 1)
                        t = d % 4
                        project(c, slot, 0, 0, unit % 4, [(2 * t, 0), (2 * t + 1, 1)], p_hi, p_lo)
                    if n == 0:
                        sum_squares(c)

            def ret(c):
                o = c["unit"] + 1 + len(RET_PRE)
                for use in RET_PRE:
                    unit, slot = c["unit"] + 1 + RET_PRE.index(use), ret_slot(use)
                    pe.wait_ge(s_free, CREDIT + free_before(c, unit))
                    pe.wait_ge(s_wlo, CREDIT + c["n"] + slot + 1)
                    project(c, slot, 0, 0, unit % 4, [(k, k) for k in range(KT)], x_hi, x_lo,
                            fed(c) if use == "q0" else None)
                    if use == "q0":
                        sum_squares(c)
                pe.wait_ge(s_rstd, CREDIT + 3 * (c["norm"] + 1))
                for t in range(TT):
                    last = nc.tensor.matmul(flat(c["ss"])[:, t:t + 1], rstd[:, t * P:(t + 1) * P], ident[:, 0:1],
                                            start=True, stop=True)
                last.then_inc(s_turn, 1)
                pe.wait_ge(s_turned, CREDIT + 1)

                def v_by_token(c, i, h, u, u2):
                    for part, use in enumerate((f"V{h}", f"U{h}")):
                        slot = ret_slot(use)
                        pe.wait_ge(s_wlo, CREDIT + c["n"] + slot + 16 * i + 1)
                        p = (c["n"] + slot) % 2
                        for t in range(TT):
                            out = flat(u)[:, t * DV:(t + 1) * DV] if t < 4 else flat(u2)[:, 0:DV]
                            for k in range(4):
                                xb, w = 4 * part + k, slice(k * DV, (k + 1) * DV)
                                xh, xl = x_hi[:, xb, t * P:(t + 1) * P], x_lo[:, xb, t * P:(t + 1) * P]
                                for q, (a, b) in enumerate(((xh, w_hi), (xh, w_lo), (xl, w_hi))):
                                    last = nc.tensor.matmul(out, a, b[:, p, w],
                                                            start=part == 0 and k == 0 and q == 0 and t % 2 == 0,
                                                            stop=part == 1 and k == 3 and q == 2,
                                                            skip_group_check=True)
                        last.then_inc(s_fill, 1)

                def body(i, uses, first=False):
                    for idx, use in enumerate(uses):
                        u = (o + idx) % 4
                        if use[0] == "U":
                            continue
                        if use[0] == "V":
                            idx += 1
                        if first:
                            pe.wait_ge(s_free, CREDIT + o + idx - 3)
                        else:
                            pe.wait_ge(s_free, CREDIT + (o + idx + len(RET_BODY) * i - (2 if idx < 2 else 4) + 1))
                        if use[0] == "V":
                            v_by_token(c, i, int(use[1]), u, (u + 1) % 4)
                            continue
                        if use[0] == "w":
                            d = int(use[1:])
                            slot = ret_slot(use, uses is RET_LAST)
                            if d == 0:
                                pe.wait_ge(s_ylo, CREDIT + 4 * i + 3)
                            if d % 2 == 0:
                                pe.wait_ge(s_wlo, CREDIT + c["n"] + slot + 16 * i + 1)

                            def last_y(b, d=d):
                                if d == 0 and b == 3:
                                    pe.wait_ge(s_ylo, CREDIT + 4 * i + 4)
                            project(c, slot, i, 16, u, [(4 * (d % 2) + k, k) for k in range(4)], y_hi, y_lo, last_y)
                            continue
                        hh = int(use[2]) if use[:2] in ("Tk", "SC", "KV", "SS", "OS", "OP", "TO") else int(use[1])
                        h = 2 * i + hh
                        if use[0] in "qkgQ" or use == "K0":
                            slot = ret_slot(use)
                            pe.wait_ge(s_wlo, CREDIT + c["n"] + slot + 16 * i + 1)
                            project(c, slot, i, 16, u, [(k, k) for k in range(KT)], x_hi, x_lo)
                            continue
                        f = flat(u)
                        if use[:2] == "Tk":
                            pe.wait_ge(s_rot, CREDIT + 2 * h + 2)
                            for t in range(TT):
                                last = nc.tensor.transpose(f[:, t * P:(t + 1) * P], kf[:, t * P:(t + 1) * P], ident[:])
                        elif use[:2] == "SC":
                            for t in range(TT):
                                last = nc.tensor.matmul(f[:, t * P:(t + 1) * P], kf[:, t * P:(t + 1) * P],
                                                        qf[:, t * P:(t + 1) * P], start=True, stop=True)
                        elif use[:2] == "KV":
                            pe.wait_ge(s_free, CREDIT + o + uses.index(f"SC{hh}") + len(RET_BODY) * i + 1)
                            for t in range(4):
                                last = nc.tensor.matmul(f[:, t * DV:(t + 1) * DV], kn[:, t, :], vn[:, t, :],
                                                        start=True, stop=True)
                        elif use[:2] == "OS":
                            pe.wait_ge(s_qm, CREDIT + h + 1)
                            pe.wait_ge(s_s0, 16 * (1) + 16 * h)
                            for s in range(STREAMS):
                                nc.tensor.matmul(f[:, 0:DV], qm[:, s * P:(s + 1) * P], s0[:, s, :],
                                                 start=s == 0, stop=False)
                            last = nc.tensor.matmul(f[:, 0:DV], sc[:, 4, :], vn[:, 4, :], start=False, stop=True)
                        elif use[:2] == "OP":
                            pe.wait_ge(s_kvs, CREDIT + 3 * h + 3)
                            for t in range(4):
                                last = nc.tensor.matmul(f[:, t * DV:(t + 1) * DV], sc[:, t, :], vn[:, t, :],
                                                        start=True, stop=t == 0)
                                if t:
                                    last = nc.tensor.matmul(f[:, t * DV:(t + 1) * DV], qf[:, t * P:(t + 1) * P],
                                                            sp_[:, t - 1, :], start=False, stop=True)
                        elif use[:2] == "SS":
                            pe.wait_ge(s_km, CREDIT + h + 1)
                            half = int(use[3])
                            for s in range(4):
                                last = nc.tensor.matmul(f[:, s * DV:(s + 1) * DV], km[:, 4 * half + s, :], vn[:, 4, :],
                                                        start=True, stop=True)
                        elif use[:2] == "TO":
                            j = int(use[3])
                            pe.wait_ge(s_free, CREDIT + o + uses.index(f"OP{hh}") + len(RET_BODY) * i + 1)
                            for t in range(TT):
                                last = nc.tensor.transpose(f[:, t * P:(t + 1) * P],
                                                           o_n[:, t * DV + j * P:t * DV + (j + 1) * P], ident[:])
                        last.then_inc(s_fill, 1)

                body(0, RET_BODY, True)
                with pe.Fori(1, RET_STEPS - 1) as i:
                    body(i, RET_BODY)
                body(RET_STEPS - 1, RET_LAST)

            def stick(c):
                def logits(z, par, head, b, z0, start):
                    rows = slice(HD * head, HD * (head + 1))
                    w, end = (P, TOK) if b == 4 else (ZW[b], SEQ)
                    return nc.tensor.matmul(z[:, z0:z0 + w], bk[rows, par, b * P:(b + 1) * P],
                                            bq[rows, par, b * P:end], start=start, stop=False, skip_group_check=True)

                def run(uses, slots, frees, t):
                    for use in uses:
                        kind, r = use[0], int(use[1] if use[0] in "qkvwyT" else use[2])
                        par = r % 2
                        half = "ab".index(use[2]) if kind in "qkvwy" else 0
                        bank = half
                        if uses is SB_PRE and kind in "qkv":
                            pe.wait_ge(s_free, CREDIT + c["unit"])
                            bank = 2 * "qkv".index(kind) + half
                        elif kind not in "ZR":
                            pe.wait_ge(s_free, CREDIT + frees + units(uses, use) - 2)
                        if kind in "qkvwy":
                            slot, blocks, src = slots(kind, r)
                            if half == 0:
                                pe.wait_ge(s_wlo, CREDIT + c["n"] + slot + 8 * t + 1)
                            p = (c["n"] + slot) % 2
                            hi, lo = (x_hi, x_lo) if src == "x" else (y_hi, y_lo)
                            cols = slice(HALF * half, HALF * (half + 1))
                            for n, (wb, xb) in enumerate(blocks):
                                if use == "q0a":
                                    pe.wait_ge(s_xlo, CREDIT + c["fed"] + n + 1)
                                wh, wl = w_hi[:, p, wb * P:(wb + 1) * P], w_lo[:, p, wb * P:(wb + 1) * P]
                                for q, (a, b) in enumerate(((wh, hi), (wh, lo), (wl, hi))):
                                    last = nc.tensor.matmul(ps[:, bank, 0:HALF], a, b[:, xb, cols],
                                                            start=n == 0 and q == 0,
                                                            stop=n == len(blocks) - 1 and q == 2)
                            last.then_inc(s_fill, 1)
                            if use == "q0b":
                                sum_squares(c)
                            continue
                        f = flat(0)
                        if kind == "T":
                            pe.wait_ge(s_free, CREDIT + frees + units(uses, f"v{r}b"))
                            for k in range(TT):
                                last = nc.tensor.transpose(f[:, k * P:(k + 1) * P], bvt[:, k * P:(k + 1) * P], ident[:])
                            last.then_inc(s_fill, 1)
                            continue
                        pair = 2 * t + r
                        piece = int(use[1] != "A")
                        z = zf(piece)
                        if kind == "Z":
                            pe.wait_ge(s_free, CREDIT + frees + units(uses, f"k{r}b"))
                            if piece == 0:
                                for n, b in enumerate((2, 0, 1, 3)):
                                    op = logits(z, par, 0, b, ZB[0, b][1], b != 3)
                                    if n == 0:
                                        op.then_inc(s_row, 1)
                                pe.wait_ge(s_row, CREDIT + 2 * pair + 1)
                                last = logits(z, par, 1, 2, ZB[1, 2][1], False)
                            else:
                                logits(z, par, 0, 4, Z_NEW, True).then_inc(s_row, 1)
                                for b in (0, 1, 3):
                                    logits(z, par, 1, b, ZB[1, b][1], b != 3)
                                pe.wait_ge(s_row, CREDIT + 2 * pair + 2)
                                logits(z, par, 1, 4, Z_NEW + P, False)
                                pe.wait_ge(s_kv[par], 32 * (t + r // 2 + 1))
                                for s in range(STREAMS):
                                    last = nc.tensor.matmul(by_stream(z[:, Z_PAST:Z_NEW], s), kc[:, par, s, :],
                                                            bqs[:, s, :, :], start=False, stop=s == STREAMS - 1,
                                                            skip_group_check=True)
                        elif kind == "R":
                            pe.wait_ge(s_llo, CREDIT + 2 * pair + 2)
                            for src in (l_hi, l_lo):
                                for (head, b), (at_piece, z0) in ZB.items():
                                    for b2 in range(b, 4):
                                        if at_piece == piece:
                                            from_piece, from_col = ZB[head, b2]
                                            last = nc.tensor.matmul(
                                                z[:, z0 + P * (b2 - b):z0 + ZW[b]], tri[:, int(b2 > b), :],
                                                src[:, from_piece, from_col:from_col + ZW[b2]], start=False,
                                                stop=False, skip_group_check=True)
                                if piece == 1:
                                    nc.tensor.matmul(z[:, Z_PAST:Z_NEW], tri[:, 0, :], src[:, 1, Z_PAST:Z_NEW],
                                                     start=False, stop=False, skip_group_check=True)
                                    nc.tensor.matmul(z[:, Z_PAST:Z_NEW], tri[:, 1, :], src[:, 1, Z_NEW:ZC],
                                                     start=False, stop=False, skip_group_check=True)
                                    last = nc.tensor.matmul(z[:, Z_NEW:ZC], tri[:, 0, :], src[:, 1, Z_NEW:ZC],
                                                            start=False, stop=src is l_lo, skip_group_check=True)
                        elif use[1] == "S":
                            f = f[:, 0:2 * P]
                            nc.tensor.matmul(f, bv[:, par, 4, :], e[:, 1, Z_NEW:ZC], start=True, stop=False,
                                             skip_group_check=True)
                            for s in range(STREAMS):
                                last = nc.tensor.matmul(by_stream(f, s), vc[:, par, s, :],
                                                        by_stream(e[:, 1, Z_PAST:Z_NEW], s),
                                                        start=False, stop=s == STREAMS - 1, skip_group_check=True)
                        else:
                            head = piece
                            pe.wait_ge(s_att, CREDIT + 2 * pair + head + 1)
                            for b in range(4):
                                at_piece, z0 = ZB[head, b]
                                last = nc.tensor.matmul(ps[:, head, b * P:SEQ], bv[:, par, b, :],
                                                        e[:, at_piece, z0:z0 + ZW[b]],
                                                        start=b == 0, stop=b == 3, skip_group_check=True)
                        last.then_inc(s_fill, 1)

                whole = [(k, k) for k in range(KT)]

                def first_slots(kind, r):
                    return "qkv".index(kind), whole, "x"

                def body_slots(kind, r):
                    if kind == "w":
                        return 9 + r // 4, [(2 * (r % 4) + k, k) for k in range(2)], "y"
                    return 3 * r + "qkv".index(kind), whole, "x"

                def last_slots(kind, r):
                    if kind in "wy":
                        first = 2 * "wy".index(kind)
                        return 4 + first + r // 4, [(2 * (r % 4) + k, first + k) for k in range(2)], "y"
                    return 1 + "qkv".index(kind), whole, "x"

                frees = c["unit"] + 1
                run(SB_PRE, first_slots, frees, 0)
                frees += units(SB_PRE)
                with pe.Fori(0, SB_STEPS) as t:
                    run(SB_BODY, body_slots, frees + units(SB_BODY) * t, t)
                frees += units(SB_BODY) * SB_STEPS
                run(SB_MID, body_slots, frees, SB_STEPS)
                run(SB_LAST, last_slots, frees + units(SB_MID), SB_STEPS + 1)

            for c in plan:
                {"ffn": ffn, "ret": ret, "sb": stick, "ple": ple}[c["kind"]](c)
            sum_squares(at.end)

        @block.scalar
        def _(act):
            for s in (s_whi, s_xhi, s_sq, s_root, s_silu, s_sig, s_gate, s_tri, s_ghi, s_phi, s_ohi, s_swap,
                      s_stp, s_sts, s_groot, s_yhi, s_soft, s_lhi, s_att):
                act.sem_inc(s, CREDIT)

            def split_hi(c, m, i, per, fill):
                cols = next_cols(c, m)
                if cols is None:
                    return
                r, value = landed(c, m + 2)
                act.wait_ge(s_raw[r], value + (4 * per) * i)
                act.wait_ge(s_fill, CREDIT + fill)
                nc.scalar.activation(w_hi[:, (c["n"] + m) % 2, 0:cols], raw[:, r, 0:cols], ACT.Copy).then_inc(s_whi, 1)

            def feed_hi(norm, d):
                nc.scalar.activation(x_hi[:, d, :], x[:, d, :], ACT.Copy,
                                     scale=gain[:, norm, d:d + 1]).then_inc(s_xhi, 1)

            def square(c_fed, norm, d, s, value):
                act.wait_ge(s, CREDIT + value)
                act.wait_ge(s_ssum, CREDIT + c_fed + d - 1)
                nc.scalar.activation(sq[:, d % 2, :], x[:, d, :], ACT.Square).then_inc(s_sq, 1)

            def feed(c_fed, norm, d, s, value):
                act.wait_ge(s, CREDIT + value)
                feed_hi(norm, d)
                square(c_fed, norm, d, s, value)

            def log_tables():
                nc.scalar.preload_act_table_set("natural_log_exp_and_others")

            def root(c):
                act.wait_ge(s_free, CREDIT + c["unit"] + 1)
                nc.scalar.activation(scr[:, 1, :], scr[:, 0, :], ACT.Ln, scale=2.0 ** LN_SHIFT).then_inc(s_root, 1)
                act.wait_ge(s_root, CREDIT + 2 * c["norm"] + 1)
                nc.scalar.activation(scr[:, 2, :], scr[:, 1, :], ACT.Exp, bias=unshift[:],
                                     scale=-0.5).then_inc(s_root, 1)

            def ffn(c):
                if c["mixed"] == "ret":
                    act.wait_ge(s_stp_kept, CREDIT + H_RET)
                    act.wait_ge(s_sts_out, 32 * H_RET)
                if c["mixed"] == "sb":
                    act.wait_ge(s_k_kept, CREDIT + PAIRS)
                    act.wait_ge(s_v_kept, CREDIT + PAIRS)
                m = 0
                o = c["unit"] + 1
                for nf_at, nf in enumerate(PIECES):
                    gbase = c["g"] + sum(PIECES[:nf_at])

                    def body(i, m=m, gbase=gbase, nf_at=nf_at):
                        first = isinstance(i, int) and i == 0 and nf_at == 0
                        if first:
                            log_tables()
                            for j in range(2):
                                split_hi(c, m + j, 0, 0, c["fill"] + m + j + 1)
                                if j == (0 if c["i"] else 1):
                                    root(c)
                        for j in range(4):
                            f = gbase + 2 * i + j // 2
                            if j >= 2 or not first:
                                if j % 2 == 0:
                                    split_hi(c, m + j, i, 4, c["fill"] + m + j + 4 * i + 1)
                            if j % 2 == 0:
                                act.wait_ge(s_free, CREDIT + o + m + j + 4 * i + 1)
                                nc.scalar.activation(scr[:, 2 + j // 2, :], scr[:, j // 2, :],
                                                     ACT.Silu).then_inc(s_silu, 1)
                            else:
                                act.wait_ge(s_free, CREDIT + o + m + j + 4 * i + 1)
                                nc.scalar.activation(g_hi[:, 2 * i + j // 2, :], scr[:, j // 2, :],
                                                     ACT.Copy).then_inc(s_ghi, 1)
                                if j >= 2 or not first:
                                    split_hi(c, m + j, i, 4, c["fill"] + m + j + 4 * i + 1)
                    lo = 0
                    if nf_at == 0:
                        body(0)
                        lo = 1
                    with act.Fori(lo, nf // 2) as i:
                        body(i)
                    m += 2 * nf
                    if nf_at == 0 and c["split_p"]:
                        act.wait_ge(s_p, 16 * (c["ple"] + 1))
                        nc.scalar.activation(p_hi[:], p_raw[:], ACT.Copy).then_inc(s_phi, 1)
                    if nf_at < 2:
                        with act.Fori(0, KT // 4) as i:
                            for j in range(4):
                                split_hi(c, m + j, i, 4, c["fill"] + m + j + 4 * i + 1)
                    else:
                        for d in range(KT):
                            split_hi(c, m + d, 0, 0, c["fill"] + m + d + 1)
                            feed(c["fed"] + KT, c["norm"] + 1, d, s_free, o + m + d + 1)
                    m += KT

            def ple(c):
                to = (at.end["fed"], 8) if c["last"] else (c["fed"] + KT, c["norm"] + 1)

                def updated(d):
                    return KT * c["ple"] + d + 1

                for n, (kind, d) in enumerate(PLE_USES):
                    if kind == "p" and d < 4:
                        if d == 3:
                            split_hi(c, ple_slot(kind, d), 0, 0, c["fill"] + n + 1)
                        continue
                    if kind == "g":
                        if d == 0:
                            log_tables()
                        split_hi(c, ple_slot(kind, d), 0, 0, c["fill"] + n + 1)
                        if d == 0:
                            root(c)
                        act.wait_ge(s_free, CREDIT + c["unit"] + 1 + n + 1)
                        nc.scalar.activation(gate[:, d, :], scr[:, d % 2, :], ACT.Sigmoid).then_inc(s_sig, 1)
                        if d >= 4:
                            square(*to, d - 4, s_xup, updated(d - 4))
                        if d == KT - 1 and not c["last"]:
                            for k in range(4):
                                feed_hi(to[1], k)
                        continue
                    if c["last"]:
                        square(*to, d, s_xup, updated(d))
                    else:
                        feed(*to, d, s_xup, updated(d))
                    if d == KT - 1:
                        split_hi(c, ple_slot(kind, d), 0, 0, c["fill"] + n + 1)

            def ret(c):
                o = c["unit"] + 1 + len(RET_PRE)
                n_u = len(RET_BODY)

                def swap(filled):
                    act.wait_ge(s_free, CREDIT + filled)
                    nc.scalar.activation(scr[0:64, 1, :], scr[64:128, 0, :], ACT.Copy).then_inc(s_swap, 1)
                    nc.scalar.activation(scr[64:128, 1, :], scr[0:64, 0, :], ACT.Copy).then_inc(s_swap, 1)

                def body(i, uses):
                    last = uses is RET_LAST

                    def fill(use):
                        return c["fill"] + len(RET_PRE) + uses.index(use) + n_u * i + 1

                    def free(use):
                        return o + uses.index(use) + n_u * i + 1

                    def split(use):
                        split_hi(c, ret_slot(use, last), i, 16, fill(use))

                    def to(hh):
                        for j in range(2):
                            act.wait_ge(s_free, CREDIT + free(f"TO{hh}{j}"))
                            nc.scalar.activation(y_hi[:, 2 * hh + j, :], scr[:, 2 + j, :], ACT.Copy).then_inc(s_yhi, 1)

                    def gate(use, j):
                        split(use)
                        act.wait_ge(s_free, CREDIT + free(use))
                        nc.scalar.activation(sg[:, j, :], sg[:, j, :], ACT.Silu).then_inc(s_gate, 1)

                    def states(hh):
                        for half in range(2):
                            act.wait_ge(s_free, CREDIT + free(f"SS{hh}{half}"))
                            apart(act)
                            four = s0[:, 4 * half:4 * half + 4, :]
                            nc.scalar.activation(four, four, ACT.Copy,
                                                 scale=gpow[:, 2 * i + hh, 1:2]).then_inc(s_sts, 1)

                    for hh in range(2):
                        h = 2 * i + hh
                        if hh:
                            swap(free("q1"))
                            split("q1")
                            to(0)
                            swap(free("k1"))
                            split("k1")
                        split(f"V{hh}")
                        split(f"U{hh}")
                        late = last and hh == 1
                        gate(f"g{hh}0", 0)
                        if not late:
                            gate(f"g{hh}1", 1)
                        act.wait_ge(s_free, CREDIT + free(f"KV{hh}"))
                        act.wait_ge(s_stp_kept, CREDIT + h)
                        apart(act)
                        nc.scalar.activation(stp[:], sp_[:, 3, :], ACT.Copy,
                                             scale=gpow[:, h, 0:1]).then_inc(s_stp, 1)
                        act.wait_ge(s_gn, CREDIT + 7 * h + 2)
                        nc.scalar.activation(gn[:, 1, :], gn[:, 0, :], ACT.Sqrt).then_inc(s_groot, 1)
                        if late:
                            gate("g11", 1)
                        else:
                            states(hh)
                    if not last:
                        swap(free("Q0"))
                        split("Q0")
                    to(1)
                    if last:
                        states(1)
                    if not last:
                        swap(free("K0"))
                        split("K0")
                    for d in range(KT):
                        if d % 2:
                            split(f"w{d}")
                        if last:
                            feed(c["fed"] + KT, c["norm"] + 1, d, s_free, free(f"w{d}"))

                act.wait_ge(s_ret_in, 64)
                log_tables()
                split_hi(c, 0, 0, 0, c["fill"] + 1)
                root(c)
                swap(c["unit"] + 2)
                split_hi(c, 1, 0, 0, c["fill"] + 2)
                swap(c["unit"] + 3)
                body(0, RET_BODY)
                with act.Fori(1, RET_STEPS - 1) as i:
                    body(i, RET_BODY)
                body(RET_STEPS - 1, RET_LAST)

            def stick(c):
                act.wait_ge(s_sb_in, 48)
                nc.scalar.activation(tri[:], negtri[:], ACT.Copy).then_inc(s_tri, 1)

                def soft(hh, pair, k, filled):
                    if k == 0:
                        act.wait_ge(s_fill, CREDIT + filled)
                        nc.scalar.activation(e[:, hh, :], zf(hh), ACT.Abs).then_inc(s_soft, 1)
                        return
                    act.wait_ge(s_soft, CREDIT + 6 * pair + 2 * (k - 1) + hh + 1)
                    if k == 1:
                        nc.scalar.activation(e[:, hh, :], e[:, hh, :], ACT.Exp, scale=-1.0).then_inc(s_soft, 1)
                    else:
                        nc.scalar.activation(e[:, hh, :], e[:, hh, :], ACT.Ln, bias=1.0).then_inc(s_soft, 1)

                def soft_rest(pair):
                    for k in (1, 2):
                        for hh in range(2):
                            soft(hh, pair, k, 0)

                def lhi(pair, hh):
                    act.wait_ge(s_sp, CREDIT + 2 * (2 * pair + hh) + 2)
                    nc.scalar.activation(l_hi[:, hh, :], e[:, hh, :], ACT.Copy).then_inc(s_lhi, 1)

                def att(pair, hh):
                    act.wait_ge(s_cap, CREDIT + 2 * pair + hh + 1)
                    nc.scalar.activation(e[:, hh, :], zf(hh), ACT.Exp).then_inc(s_att, 1)

                def yhi(what, a, filled):
                    act.wait_ge(s_fill, CREDIT + filled)
                    for rows, bank, src, dst in y_parts(what):
                        nc.scalar.activation(y_hi[rows, a, dst], ps[rows, bank, src], ACT.Copy).then_inc(s_ohi, 1)

                def section(uses, fills, slot, t, r, a, tile):
                    def fill(use):
                        return fills + uses.index(use) + 1

                    split_hi(c, slot, t, 8, fill(f"q{r}b"))
                    lhi(2 * t + a, 0)
                    lhi(2 * t + a, 1)
                    split_hi(c, slot + 1, t, 8, fill(f"k{r}b"))
                    split_hi(c, slot + 2, t, 8, fill(f"v{r}b"))
                    att(2 * t + a, 0)
                    att(2 * t + a, 1)
                    yhi("A", tile, fill(f"AA{a}"))
                    yhi("B", tile, fill(f"AB{a}"))
                    soft(0, 2 * t + r, 0, fill(f"ZA{r}"))
                    yhi("S", tile, fill(f"AS{a}"))
                    soft(1, 2 * t + r, 0, fill(f"ZB{r}"))
                    soft_rest(2 * t + r)

                fills = c["fill"]
                log_tables()
                for m, name in enumerate("qkv"):
                    split_hi(c, m, 0, 0, fills + SB_PRE.index(f"{name}0b") + 1)
                    if m == 0:
                        root(c)
                soft(0, 0, 0, fills + SB_PRE.index("ZA0") + 1)
                soft(1, 0, 0, fills + SB_PRE.index("ZB0") + 1)
                soft_rest(0)
                fills += len(SB_PRE)
                with act.Fori(0, SB_STEPS) as t:
                    before = fills + len(SB_BODY) * t
                    section(SB_BODY, before, 3, t, 1, 0, 0)
                    section(SB_BODY, before, 6, t, 2, 1, 1)
                    split_hi(c, 9, t, 8, before + SB_BODY.index("w3b") + 1)
                    split_hi(c, 10, t, 8, before + SB_BODY.index("w7b") + 1)
                fills += len(SB_BODY) * SB_STEPS
                section(SB_MID, fills, 3, SB_STEPS, 1, 0, 0)
                section(SB_MID, fills, 6, SB_STEPS, 2, 1, 1)
                fills += len(SB_MID)
                t = SB_STEPS + 1
                section(SB_LAST, fills, 1, t, 1, 0, 2)
                split_hi(c, 4 + 8 * t, 0, 0, fills + SB_LAST.index("w3b") + 1)
                lhi(2 * t + 1, 0)
                lhi(2 * t + 1, 1)
                split_hi(c, 5 + 8 * t, 0, 0, fills + SB_LAST.index("w7b") + 1)
                att(2 * t + 1, 0)
                att(2 * t + 1, 1)
                for what in "ABS":
                    yhi(what, 3, fills + SB_LAST.index(f"A{what}1") + 1)
                frees = c["unit"] + 1 + SB_UNITS - units(SB_LAST)
                for d in range(KT):
                    feed(c["fed"] + KT, c["norm"] + 1, d, s_free, frees + units(SB_LAST, f"y{d}b"))
                    if d % 4 == 3:
                        split_hi(c, 6 + d // 4 + 8 * t, 0, 0, fills + SB_LAST.index(f"y{d}b") + 1)

            log_tables()
            act.wait_ge(s_unshift, 1)
            act.wait_ge(s_gain, 16)
            for d in range(KT):
                if d in (0, 4):
                    n = d // 4
                    act.wait_ge(s_raw[n], 16)
                    nc.scalar.activation(w_hi[:, n, :], raw[:, n, :], ACT.Copy).then_inc(s_whi, 1)
                act.wait_ge(s_x[d], 16)
                feed(0, 0, d, s_xup, 0)
            for c in plan:
                {"ffn": ffn, "ret": ret, "sb": stick, "ple": ple}[c["kind"]](c)
            log_tables()
            root(at.end)

        @block.gpsimd
        def _(pool):
            for s in (s_ssum, s_rd, s_km, s_qm, s_stp_kept, s_k_kept, s_v_kept):
                pool.sem_inc(s, CREDIT)

            def add_squares(fed, norm):
                for d in range(KT):
                    pool.wait_ge(s_sq, CREDIT + fed + d + 1)
                    if d == 0:
                        pool.wait_ge(s_ss, CREDIT + norm)
                        nc.gpsimd.tensor_copy(ssum[:], sq[:, 0, :]).then_inc(s_ssum, 1)
                    else:
                        pool.wait_ge(s_ssum, CREDIT + fed + d)
                        nc.gpsimd.tensor_tensor(ssum[:], ssum[:], sq[:, d % 2, :], ALU.add).then_inc(s_ssum, 1)

            def ffn(c):
                if c["split_p"]:
                    pool.wait_ge(s_fill, CREDIT + c["fill"])
                    pool.dma_start(p_raw[:], pT[c["ple"]].rearrange("k p t -> p k t")).then_inc(s_p, 16)

            def ret(c):
                o = c["unit"] + 1 + len(RET_PRE)
                n_u = len(RET_BODY)
                pool.wait_ge(s_fill, CREDIT + c["fill"])
                pool.dma_start(cs[:], cs_d).then_inc(s_ret_in, 16)
                pool.dma_start(rmask[:], rmask_d).then_inc(s_ret_in, 16)
                pool.dma_start(smask[:], smask_d).then_inc(s_ret_in, 16)
                pool.dma_start(gpow[:], gpow_d).then_inc(s_ret_in, 16)
                pool.dma_start(rd[:], dec_d[0]).then_inc(s_dec, 16)
                pool.dma_start(s0[:], st_d[0]).then_inc(s_s0, 16)
                nc.gpsimd.memset(qm[:], 0.0)
                pool.wait_ge(s_rstd, CREDIT + 3 * (c["norm"] + 1))

                def decay(h):
                    pool.wait_ge(s_dec, 16 * (h + 1))
                    nc.gpsimd.tensor_tensor(rd[:, 0, :], rd[:, 0, :], rstd[:], ALU.mult).then_inc(s_rd, 1)
                    nc.gpsimd.tensor_tensor(rd[:, 1, :], rd[:, 1, :], rstd[:], ALU.mult).then_inc(s_rd, 1)

                decay(0)
                pool.wait_ge(s_ret_in, 64)

                def body(i, last):
                    for hh in range(2):
                        h = 2 * i + hh
                        pool.wait_ge(s_rot, CREDIT + 2 * h + 1)
                        apart(pool)
                        nc.gpsimd.tensor_copy(qm[:].rearrange("p (s c) -> p s c", s=STREAMS)[:, :, 0:STEP],
                                              qf[:, SEQ:TOK].rearrange("p (s c) -> p s c", s=STREAMS)).then_inc(s_qm, 1)
                        pool.wait_ge(s_free, CREDIT + o + RET_BODY.index(f"Tk{hh}") + n_u * i + 1)
                        nc.gpsimd.tensor_tensor(km[:], kn[:, 4, :].unsqueeze(1).to_broadcast([P, STREAMS, P]),
                                                smask[:].unsqueeze(2).to_broadcast([P, STREAMS, P]),
                                                ALU.mult).then_inc(s_km, 1)
                        if not (last and hh):
                            apart(pool)
                            pool.dma_start(rd[:], dec_d[h + 1]).then_inc(s_dec, 16)
                            decay(h + 1)
                        pool.wait_ge(s_stp, CREDIT + h + 1)
                        apart(pool)
                        pool.dma_start(stp_o[h], stp[:]).then_inc(s_stp_out, 16)
                        for half in range(2):
                            pool.wait_ge(s_sts, CREDIT + 2 * h + half + 1)
                            apart(pool)
                            pool.dma_start(sts_o[h, :, 4 * half:4 * half + 4, :],
                                           s0[:, 4 * half:4 * half + 4, :]).then_inc(s_sts_out, 16)
                        pool.wait_ge(s_stp_out, 16 * (h + 1))
                        pool.sem_inc(s_stp_kept, 1)
                        if not (last and hh):
                            pool.wait_ge(s_sts_out, 32 * (h + 1))
                            apart(pool)
                            pool.dma_start(s0[:], st_d[h + 1]).then_inc(s_s0, 16)

                body(0, False)
                with pool.Fori(1, 3) as i:
                    body(i, False)
                body(3, True)
                pool.wait_ge(s_stp_out, 16 * H_RET)
                pool.wait_ge(s_sts_out, 32 * H_RET)

            def stick(c):
                o = c["unit"] + 1
                pool.wait_ge(s_fill, CREDIT + c["fill"])
                pool.dma_start(negtri[:], negtri_d).then_inc(s_sb_in, 16)
                pool.dma_start(bmask[:], bmask_d).then_inc(s_sb_in, 16)
                pool.dma_start(bcap[:], bcap_d).then_inc(s_sb_in, 16)

                def load(pair, par):
                    pool.dma_start(kc[:, par, :, :], kc_d[pair]).then_inc(s_kv[par], 16)
                    pool.dma_start(vc[:, par, :, :], vc_d[pair]).then_inc(s_kv[par], 16)

                def store(pair, par, k_free, v_free):
                    pool.wait_ge(s_free, CREDIT + k_free)
                    apart(pool)
                    pool.dma_start(k_o[pair], bk[:, par, :]).then_inc(s_k_out, 16)
                    pool.wait_ge(s_k_out, 16 * pair + 16)
                    pool.sem_inc(s_k_kept, 1)
                    pool.wait_ge(s_free, CREDIT + v_free)
                    apart(pool)
                    pool.dma_start(v_o[pair], bvt[:]).then_inc(s_v_out, 16)
                    pool.wait_ge(s_v_out, 16 * pair + 16)
                    pool.sem_inc(s_v_kept, 1)

                load(0, 0)
                load(1, 1)
                store(0, 0, o + units(SB_PRE, "k0b"), o + units(SB_PRE, "v0b"))
                o += units(SB_PRE)
                fills = c["fill"] + len(SB_PRE)

                def step(uses, t):
                    for r, a in ((1, 0), (2, 1)):
                        store(2 * t + r, r % 2, o + units(uses, f"k{r}b") + units(SB_BODY) * t,
                              o + units(uses, f"v{r}b") + units(SB_BODY) * t)
                        pool.wait_ge(s_fill, CREDIT + fills + uses.index(f"AS{a}") + 1 + len(SB_BODY) * t)
                        apart(pool)
                        load(2 * t + a + 2, a)

                with pool.Fori(0, SB_STEPS) as t:
                    step(SB_BODY, t)
                step(SB_MID, SB_STEPS)
                o += units(SB_BODY) * SB_STEPS + units(SB_MID)
                store(PAIRS - 1, 1, o + units(SB_LAST, "k1b"), o + units(SB_LAST, "v1b"))
                pool.wait_ge(s_k_out, 16 * PAIRS)
                pool.wait_ge(s_v_out, 16 * PAIRS)

            nc.gpsimd.memset(unshift[:], 0.5 * LN_SHIFT * math.log(2.0)).then_inc(s_unshift, 1)
            add_squares(0, 0)
            for c in plan:
                {"ffn": ffn, "ret": ret, "sb": stick, "ple": lambda c: None}[c["kind"]](c)
                add_squares(c["fed"] + KT, c["norm"] + 1)

        @block.vector
        def _(dve):
            for s in (s_turned, s_free, s_wlo, s_xlo, s_rstd, s_glo, s_plo, s_sr, s_xup, s_out, s_rt, s_rot, s_kvs,
                      s_aggr, s_gn, s_ylo, s_sp, s_llo, s_cap):
                dve.sem_inc(s, CREDIT)
            tt, ts, stt = nc.vector.tensor_tensor, nc.vector.tensor_scalar, nc.vector.scalar_tensor_tensor

            def split_lo(c, m, i, per):
                cols = next_cols(c, m)
                if cols is None:
                    return
                n = c["n"] + m + 2 + per * i
                r, _ = landed(c, m + 2)
                p = (c["n"] + m) % 2
                dve.wait_ge(s_whi, CREDIT + n + 1)
                tt(w_lo[:, p, 0:cols], raw[:, r, 0:cols], w_hi[:, p, 0:cols].bitcast(F),
                   ALU.subtract).then_inc(s_wlo, 1)

            def feed_lo(c_fed, norm, d):
                dve.wait_ge(s_xhi, CREDIT + c_fed + d + 1)
                stt(out=x_lo[:, d, :], in0=x[:, d, :], scalar=gain[:, norm, d:d + 1],
                    in1=x_hi[:, d, :].bitcast(F), op0=ALU.mult, op1=ALU.subtract).then_inc(s_xlo, 1)

            def one_over_rms(c, slot=None):
                k = 3 * c["norm"]
                dve.wait_ge(s_ss, CREDIT + c["norm"] + 1)
                ts(halves(scr[:, 0, :]), acc(c["ss"]), 1.0 / D, EPS, ALU.mult, ALU.add).then_inc(s_free, 1)
                if slot is not None:
                    split_lo(c, slot, 0, 0)
                dve.wait_ge(s_root, CREDIT + 2 * c["norm"] + 2)
                tt(scr[:, 3, :], scr[:, 2, :], scr[:, 2, :], ALU.mult).then_inc(s_rstd, 1)
                dve.wait_ge(s_rstd, CREDIT + k + 1)
                stt(out=scr[:, 1, :], in0=scr[:, 3, :], scalar=-0.5, in1=scr[:, 0, :],
                    op0=ALU.mult, op1=ALU.mult).then_inc(s_rstd, 1)
                dve.wait_ge(s_rstd, CREDIT + k + 2)
                stt(out=rstd[:], in0=scr[:, 1, :], scalar=1.5, in1=scr[:, 2, :],
                    op0=ALU.add, op1=ALU.mult).then_inc(s_rstd, 1)
                dve.wait_ge(s_rstd, CREDIT + k + 3)

            def ffn(c):
                m = 0
                o = c["unit"] + 1
                for nf_at, nf in enumerate(PIECES):
                    gbase = c["g"] + sum(PIECES[:nf_at])

                    def body(i, m=m, gbase=gbase, nf_at=nf_at):
                        first = isinstance(i, int) and i == 0 and nf_at == 0
                        if first:
                            for j in range(2):
                                if j == (0 if c["i"] else 1):
                                    one_over_rms(c, m + j)
                                else:
                                    split_lo(c, m + j, 0, 0)
                        for j in range(4):
                            u = (o + m + j) % 4
                            f = gbase + 2 * i + j // 2
                            t = scr[:, j // 2, :]
                            dve.wait_ge(s_fill, CREDIT + c["fill"] + m + j + 4 * i + 1)
                            if j % 2 == 0:
                                dve.wait_ge(s_glo, CREDIT + f - 1)
                                tt(halves(t), acc(u), halves(rstd[:]), ALU.mult).then_inc(s_free, 1)
                                if j or not first:
                                    split_lo(c, m + j, i, 4)
                                dve.wait_ge(s_silu, CREDIT + f + 1)
                                tt(scr[:, 2 + j // 2, :], scr[:, 2 + j // 2, :], rstd[:], ALU.mult).then_inc(s_sr, 1)
                            else:
                                dve.wait_ge(s_sr, CREDIT + f + 1)
                                tt(halves(t), acc(u), halves(scr[:, 2 + j // 2, :]), ALU.mult).then_inc(s_free, 1)
                                dve.wait_ge(s_ghi, CREDIT + f + 1)
                                fi = 2 * i + j // 2
                                tt(g_lo[:, fi, :], t, g_hi[:, fi, :].bitcast(F), ALU.subtract).then_inc(s_glo, 1)
                                if j >= 2 or not first:
                                    split_lo(c, m + j, i, 4)
                    lo = 0
                    if nf_at == 0:
                        body(0)
                        lo = 1
                    with dve.Fori(lo, nf // 2) as i:
                        body(i)
                    m += 2 * nf
                    if nf_at == 0 and c["split_p"]:
                        dve.wait_ge(s_phi, CREDIT + c["ple"] + 1)
                        tt(p_lo[:], p_raw[:], p_hi[:].bitcast(F), ALU.subtract).then_inc(s_plo, 1)

                    def down(i, j, feed, m=m):
                        u = (o + m + j) % 4
                        d = 4 * i + j
                        dve.wait_ge(s_fill, CREDIT + c["fill"] + m + d + 1)
                        xd = halves(x[:, d, :])
                        stt(out=xd, in0=acc(u), scalar=0.5, in1=xd, op0=ALU.mult, op1=ALU.add).then_inc(s_free, 1)
                        split_lo(c, m + j, i, 4) if not isinstance(i, int) else split_lo(c, m + d, 0, 0)
                        if feed:
                            feed_lo(c["fed"] + KT, c["norm"] + 1, d)
                    if nf_at < 2:
                        with dve.Fori(0, KT // 4) as i:
                            for j in range(4):
                                down(i, j, False)
                    else:
                        for d in range(KT):
                            down(d // 4, d % 4, True)
                    m += KT

            def ple(c):
                for n, (kind, d) in enumerate(PLE_USES):
                    slot = ple_slot(kind, d)
                    fill, u = c["fill"] + n + 1, (c["unit"] + 1 + n) % 4
                    if n == 0:
                        one_over_rms(c, slot)
                    dve.wait_ge(s_fill, CREDIT + fill)
                    if kind == "g":
                        dve.wait_ge(s_sig, CREDIT + KT * c["ple"] + d - 1)
                        tt(halves(scr[:, d % 2, :]), acc(u), halves(rstd[:]), ALU.mult).then_inc(s_free, 1)
                        if n:
                            split_lo(c, slot, 0, 0)
                        continue
                    t = scr[:, 2 + d % 2, :]
                    dve.wait_ge(s_sig, CREDIT + KT * c["ple"] + d + 1)
                    tt(halves(t), acc(u), halves(gate[:, d, :]), ALU.mult).then_inc(s_free, 1)
                    dve.wait_ge(s_free, CREDIT + c["unit"] + 1 + n + 1)
                    tt(x[:, d, :], x[:, d, :], t, ALU.add).then_inc(s_xup, 1)
                    if d >= 4 and not c["last"]:
                        feed_lo(c["fed"] + KT, c["norm"] + 1, d - 4)
                    if d % 4 == 3:
                        split_lo(c, slot, 0, 0)
                if not c["last"]:
                    for d in range(4, KT):
                        feed_lo(c["fed"] + KT, c["norm"] + 1, d)

            def ret(c):
                o = c["unit"] + 1 + len(RET_PRE)
                n_u = len(RET_BODY)
                dve.wait_ge(s_ret_in, 64)

                def rot(n, h, part, fill, free):
                    out = (qf, kf)[n]
                    dve.wait_ge(s_fill, CREDIT + fill)
                    dve.wait_ge(s_rd, CREDIT + 2 * h + n + 1)
                    tt(halves(scr[:, 0, :]), acc(part), halves(rd[:, n, :]), ALU.mult).then_inc(s_free, 1)
                    dve.wait_ge(s_free, CREDIT + free)
                    tt(out[:], scr[:, 0, :], cs[:, 0, :], ALU.mult).then_inc(s_rt, 1)
                    dve.wait_ge(s_swap, CREDIT + 4 * h + 2 * n + 2)
                    tt(scr[:, 1, :], scr[:, 1, :], cs[:, 1, :], ALU.mult).then_inc(s_rt, 1)
                    dve.wait_ge(s_rt, CREDIT + 4 * h + 2 * n + 2)
                    tt(out[:], out[:], scr[:, 1, :], ALU.add).then_inc(s_rot, 1)

                def body(i, uses):
                    last = uses is RET_LAST

                    def u(use):
                        return (o + uses.index(use)) % 4

                    def fill(use):
                        return c["fill"] + len(RET_PRE) + uses.index(use) + n_u * i + 1

                    def split(use):
                        split_lo(c, ret_slot(use, last), i, 16)

                    def turn(use, h):
                        rot("qk".index(use[0].lower()), h, u(use), fill(use), o + uses.index(use) + n_u * i + 1)
                        split(use)

                    def to(ho):
                        for j in range(2):
                            use = f"TO{ho}{j}"
                            hcount = 2 * i + ho
                            dve.wait_ge(s_fill, CREDIT + fill(use))
                            dve.wait_ge(s_gate, CREDIT + 2 * hcount + j + 1)
                            dve.wait_ge(s_ylo, CREDIT + 2 * hcount + j - 1)
                            tt(scr[:, 2 + j, :], flat(u(use))[:, 0:TOK], sg[:, j, :], ALU.mult).then_inc(s_free, 1)
                            dve.wait_ge(s_yhi, CREDIT + 2 * hcount + j + 1)
                            tt(y_lo[:, 2 * ho + j, :], scr[:, 2 + j, :], y_hi[:, 2 * ho + j, :].bitcast(F),
                               ALU.subtract).then_inc(s_ylo, 1)

                    def states(hh):
                        for half in range(2):
                            use = f"SS{hh}{half}"
                            dve.wait_ge(s_fill, CREDIT + fill(use))
                            s4 = s0[:, 4 * half:4 * half + 4, :].rearrange("p s c -> p (s c)")
                            tt(s4, s4, flat(u(use)), ALU.add).then_inc(s_free, 1)

                    for hh in range(2):
                        h = 2 * i + hh
                        gk = 7 * h
                        if hh:
                            turn("q1", h)
                            to(0)
                            turn("k1", h)
                        use = f"V{hh}"
                        dve.wait_ge(s_fill, CREDIT + fill(use))
                        split(use)
                        dve.wait_ge(s_fill, CREDIT + fill(f"U{hh}"))
                        tt(vn[:, 0:4, :], flat(u(use)).rearrange("p (t c) -> p t c", t=4),
                           rstd_t[:, 0:4].unsqueeze(2).to_broadcast([P, 4, DV]), ALU.mult).then_inc(s_free, 1)
                        use = f"U{hh}"
                        ts(vn[:, 4, :], flat(u(use))[:, 0:DV], rstd_t[:, 4:5], None, ALU.mult).then_inc(s_free, 1)
                        split(use)
                        dve.wait_ge(s_fill, CREDIT + fill(f"Tk{hh}"))
                        nc.vector.tensor_copy(kn[:].rearrange("p t c -> p (t c)"),
                                              flat(u(f"Tk{hh}"))[:, 0:TOK]).then_inc(s_free, 1)

                        dve.wait_ge(s_fill, CREDIT + fill(f"SC{hh}"))
                        tt(sc[:].rearrange("p t c -> p (t c)"), flat(u(f"SC{hh}"))[:, 0:TOK],
                           rmask[:].rearrange("p t c -> p (t c)"), ALU.mult).then_inc(s_free, 1)

                        def gate(j):
                            use = f"g{hh}{j}"
                            dve.wait_ge(s_fill, CREDIT + fill(use))
                            tt(halves(sg[:, j, :]), acc(u(use)), halves(rstd[:]), ALU.mult).then_inc(s_free, 1)
                            split(use)
                        late = last and hh == 1
                        gate(0)
                        if not late:
                            gate(1)
                        dve.wait_ge(s_fill, CREDIT + fill(f"KV{hh}"))
                        dve.wait_ge(s_stp, CREDIT + h)
                        kv = flat(u(f"KV{hh}"))
                        nc.vector.tensor_copy(sp_[:, 0, :], kv[:, 0:DV]).then_inc(s_kvs, 1)
                        for t in range(1, 4):
                            dve.wait_ge(s_kvs, CREDIT + 3 * h + t)
                            tt(sp_[:, t, :], kv[:, t * DV:(t + 1) * DV], sp_[:, t - 1, :],
                               ALU.add).then_inc(s_kvs if t < 3 else s_free, 1)
                        dve.wait_ge(s_fill, CREDIT + fill(f"OS{hh}"))
                        osf = flat(u(f"OS{hh}"))
                        nc.vector.bn_stats(bst[:, 4, :], osf[:, 0:DV])
                        dve.wait_ge(s_fill, CREDIT + fill(f"OP{hh}"))
                        opf = flat(u(f"OP{hh}"))
                        for t in range(4):
                            op = nc.vector.bn_stats(bst[:, t, :], opf[:, t * DV:(t + 1) * DV])
                        op.then_inc(s_gn, 1)
                        dve.wait_ge(s_gn, CREDIT + gk + 1)
                        apart(dve)
                        for t in range(TT):
                            op = nc.vector.bn_aggr(mv[:, t, :], bst[:, t, :])
                        op.then_inc(s_aggr, 1)
                        dve.wait_ge(s_aggr, CREDIT + h + 1)
                        ts(gn[:, 0, :], mv[:, :, 1], GN_EPS, None, ALU.add).then_inc(s_gn, 1)
                        dve.wait_ge(s_groot, CREDIT + h + 1)
                        nc.vector.reciprocal(gn[:, 2, :], gn[:, 1, :]).then_inc(s_gn, 1)
                        dve.wait_ge(s_gn, CREDIT + gk + 3)
                        tt(gn[:, 3, :], gn[:, 2, :], gn[:, 2, :], ALU.mult).then_inc(s_gn, 1)
                        dve.wait_ge(s_gn, CREDIT + gk + 4)
                        tt(gn[:, 3, :], gn[:, 3, :], gn[:, 0, :], ALU.mult).then_inc(s_gn, 1)
                        dve.wait_ge(s_gn, CREDIT + gk + 5)
                        ts(gn[:, 3, :], gn[:, 3, :], -0.5, 1.5, ALU.mult, ALU.add).then_inc(s_gn, 1)
                        dve.wait_ge(s_gn, CREDIT + gk + 6)
                        tt(gn[:, 4, :], gn[:, 2, :], gn[:, 3, :], ALU.mult).then_inc(s_gn, 1)
                        dve.wait_ge(s_gn, CREDIT + gk + 7)
                        for t in (4, 0, 1, 2, 3):
                            src = osf[:, 0:DV] if t == 4 else opf[:, t * DV:(t + 1) * DV]
                            op = ts(o_n[:, t * DV:(t + 1) * DV], src, mv[:, t, 0:1], gn[:, 4, t:t + 1],
                                    ALU.subtract, ALU.mult)
                            if t in (3, 4):
                                op.then_inc(s_free, 1)
                        if late:
                            gate(1)
                        else:
                            states(hh)
                    if not last:
                        turn("Q0", 2 * i + 2)
                    to(1)
                    if last:
                        states(1)
                    if not last:
                        turn("K0", 2 * i + 2)
                    for d in range(KT):
                        use = f"w{d}"
                        dve.wait_ge(s_fill, CREDIT + fill(use))
                        xd = halves(x[:, d, :])
                        tt(xd, xd, acc(u(use)), ALU.add).then_inc(s_free, 1)
                        if d % 2:
                            split(use)
                        if last:
                            feed_lo(c["fed"] + KT, c["norm"] + 1, d)

                one_over_rms(c, 0)
                dve.wait_ge(s_turn, CREDIT + 1)
                nc.vector.tensor_copy(rstd_t[:], flat(c["ss"])[:, 0:TT]).then_inc(s_turned, 1)
                rot(0, 0, (c["unit"] + 1) % 4, c["fill"] + 1, c["unit"] + 2)
                split_lo(c, 1, 0, 0)
                rot(1, 0, (c["unit"] + 2) % 4, c["fill"] + 2, c["unit"] + 3)
                body(0, RET_BODY)
                with dve.Fori(1, RET_STEPS - 1) as i:
                    body(i, RET_BODY)
                body(RET_STEPS - 1, RET_LAST)

            def stick(c):
                dve.wait_ge(s_sb_in, 48)

                def masked(t, piece, table, op):
                    by_bank = t.rearrange("p (b c) -> p b c", b=3)
                    last_two = t[:, 768:ZC].rearrange("p (b c) -> p b c", b=2)[:, :, P:2 * P]
                    if piece == 0:
                        first = by_bank[:, :, 0:P]
                        tt(first, first, table[:, 0:1, :].to_broadcast([P, 3, P]), op)
                        return tt(last_two, last_two, table[:, 0:1, :].to_broadcast([P, 2, P]), op)
                    first, end = by_bank[:, 0:2, 0:P], t[:, Z_NEW + P:ZC]
                    tt(first, first, table[:, 0:1, :].to_broadcast([P, 2, P]), op)
                    tt(last_two, last_two, table[:], op)
                    return tt(end, end, table[:, 1, :], op)

                def softplus(piece, pair):
                    dve.wait_ge(s_soft, CREDIT + 6 * pair + 4 + piece + 1)
                    stt(out=e[:, piece, :], in0=zf(piece), scalar=0.0, in1=e[:, piece, :],
                        op0=ALU.max, op1=ALU.add).then_inc(s_sp, 1)
                    dve.wait_ge(s_sp, CREDIT + 2 * (2 * pair + piece) + 1)
                    masked(e[:, piece, :], piece, bmask, ALU.mult).then_inc(s_sp, 1)

                def llo(piece, pair):
                    dve.wait_ge(s_lhi, CREDIT + 2 * pair + piece + 1)
                    tt(l_lo[:, piece, :], e[:, piece, :], l_hi[:, piece, :].bitcast(F), ALU.subtract).then_inc(s_llo, 1)

                def cap(piece, filled):
                    dve.wait_ge(s_fill, CREDIT + filled)
                    masked(zf(piece), piece, bcap, ALU.min).then_inc(s_cap, 1)

                def ylo(what, pair, a):
                    for n, (rows, bank, src, dst) in enumerate(y_parts(what)):
                        dve.wait_ge(s_ohi, CREDIT + 4 * pair + "ABS".index(what) + n + 1)
                        op = tt(y_lo[rows, a, dst], ps[rows, bank, src], y_hi[rows, a, dst].bitcast(F), ALU.subtract)
                    op.then_inc(s_free, 2 if what == "S" else 1)

                def half(name, pair, par, h, filled, bank=0):
                    cols = slice(HALF * h, HALF * (h + 1))
                    dve.wait_ge(s_fill, CREDIT + filled)
                    if name == "q":
                        op = stt(out=bq[:, par, cols], in0=ps[:, bank + h, 0:HALF], scalar=HD ** -0.5,
                                 in1=rstd[:, cols], op0=ALU.mult, op1=ALU.mult)
                        for head in range(2 * h):
                            rows = slice(HD * head, HD * (head + 1))
                            op = stt(out=bqs[rows, :, head, :],
                                     in0=ps[rows, bank + 1, SEQ - HALF:HALF].rearrange("p (s q) -> p s q", s=STREAMS),
                                     scalar=HD ** -0.5,
                                     in1=rstd[rows, SEQ:TOK].rearrange("p (s q) -> p s q", s=STREAMS),
                                     op0=ALU.mult, op1=ALU.mult)
                        op.then_inc(s_free, 1)
                    elif name == "k":
                        if h == 0:
                            dve.wait_ge(s_k_kept, CREDIT + pair - 1)
                        tt(bk[:, par, cols], ps[:, bank + h, 0:HALF], rstd[:, cols], ALU.mult).then_inc(s_free, 1)
                    else:
                        if h == 0:
                            dve.wait_ge(s_v_kept, CREDIT + pair)
                        tt(bvt[:, cols], ps[:, bank + h, 0:HALF], rstd[:, cols], ALU.mult).then_inc(s_free, 1)

                def by_token(par, filled):
                    dve.wait_ge(s_fill, CREDIT + filled)
                    nc.vector.tensor_copy(bv[:, par, :, :].rearrange("p t c -> p (t c)"),
                                          flat(0)[:, 0:TOK]).then_inc(s_free, 2)

                def section(uses, fills, slot, t, r, a, tile):
                    def fill(use):
                        return fills + uses.index(use) + 1

                    pr, pa, par = 2 * t + r, 2 * t + a, r % 2
                    half("q", pr, par, 0, fill(f"q{r}a"))
                    softplus(0, pa)
                    half("q", pr, par, 1, fill(f"q{r}b"))
                    split_lo(c, slot, t, 8)
                    softplus(1, pa)
                    half("k", pr, par, 0, fill(f"k{r}a"))
                    llo(0, pa)
                    half("k", pr, par, 1, fill(f"k{r}b"))
                    llo(1, pa)
                    split_lo(c, slot + 1, t, 8)
                    half("v", pr, par, 0, fill(f"v{r}a"))
                    half("v", pr, par, 1, fill(f"v{r}b"))
                    split_lo(c, slot + 2, t, 8)
                    cap(0, fill(f"RA{a}"))
                    by_token(par, fill(f"T{r}"))
                    cap(1, fill(f"RB{a}"))
                    for what in "ABS":
                        ylo(what, pa, tile)

                def add(d, h, filled):
                    cols = slice(HALF * h, HALF * (h + 1))
                    dve.wait_ge(s_fill, CREDIT + filled)
                    tt(x[:, d, cols], x[:, d, cols], ps[:, h, 0:HALF], ALU.add).then_inc(s_free, 1)

                nc.vector.memset(bqs[0:HD, :, 1, :], 0.0)
                nc.vector.memset(bqs[HD:P, :, 0, :], 0.0)
                fills = c["fill"]
                for m, name in enumerate("qkv"):
                    if m == 0:
                        one_over_rms(c, m)
                    for h in range(2):
                        half(name, 0, 0, h, fills + SB_PRE.index(f"{name}0{'ab'[h]}") + 1, 2 * m)
                    if m:
                        split_lo(c, m, 0, 0)
                by_token(0, fills + SB_PRE.index("T0") + 1)
                fills += len(SB_PRE)
                with dve.Fori(0, SB_STEPS) as t:
                    before = fills + len(SB_BODY) * t
                    section(SB_BODY, before, 3, t, 1, 0, 0)
                    section(SB_BODY, before, 6, t, 2, 1, 1)
                    for d in range(KT):
                        for h in range(2):
                            add(d, h, before + SB_BODY.index(f"w{d}{'ab'[h]}") + 1)
                        if d % 4 == 3:
                            split_lo(c, 9 + d // 4, t, 8)
                fills += len(SB_BODY) * SB_STEPS
                section(SB_MID, fills, 3, SB_STEPS, 1, 0, 0)
                section(SB_MID, fills, 6, SB_STEPS, 2, 1, 1)
                fills += len(SB_MID)
                t = SB_STEPS + 1
                section(SB_LAST, fills, 1, t, 1, 0, 2)
                for d in range(KT):
                    for h in range(2):
                        add(d, h, fills + SB_LAST.index(f"w{d}{'ab'[h]}") + 1)
                    if d in (4, 5):
                        softplus(d - 4, 2 * t + 1)
                    if d in (6, 7):
                        llo(d - 6, 2 * t + 1)
                    if d % 4 == 3:
                        split_lo(c, 4 + d // 4 + 8 * t, 0, 0)
                for piece in range(2):
                    cap(piece, fills + SB_LAST.index(f"R{'AB'[piece]}1") + 1)
                for what in "ABS":
                    ylo(what, 2 * t + 1, 3)
                for d in range(KT):
                    for h in range(2):
                        add(d, h, fills + SB_LAST.index(f"y{d}{'ab'[h]}") + 1)
                    if d:
                        feed_lo(c["fed"] + KT, c["norm"] + 1, d - 1)
                    if d % 4 == 3:
                        split_lo(c, 6 + d // 4 + 8 * t, 0, 0)
                feed_lo(c["fed"] + KT, c["norm"] + 1, KT - 1)

            dve.wait_ge(s_gain, 16)
            for d in range(KT):
                if d in (0, 4):
                    n = d // 4
                    dve.wait_ge(s_whi, CREDIT + n + 1)
                    tt(w_lo[:, n, :], raw[:, n, :], w_hi[:, n, :].bitcast(F), ALU.subtract).then_inc(s_wlo, 1)
                feed_lo(0, 0, d)
            for c in plan:
                {"ffn": ffn, "ret": ret, "sb": stick, "ple": ple}[c["kind"]](c)
            one_over_rms(at.end)
            for d in range(KT):
                if d >= 4:
                    dve.wait_ge(s_y_out[d % 4], 16 * (d // 4))
                stt(out=scr[:, d % 4, :], in0=x[:, d, :], scalar=gain[:, len(plan), d:d + 1], in1=rstd[:],
                    op0=ALU.mult, op1=ALU.mult).then_inc(s_out, 1)


PHASES = ["ffn", "ret", "ffn", "ple", "ffn", "sb", "ffn", "ple"]


def _slots(w, np):
    k, n = w.shape[0] // P, w.shape[1] // P
    return w.reshape(k, P, n, P).transpose(2, 1, 0, 3)


def _stream(inputs, phases, np):
    out, ffn_at, ret_at, sb_at, ple_at = [], 0, 0, 0, 0

    def put(blocks):
        for b in blocks:
            b = b.reshape(P, -1)
            if b.shape[1] < D:
                b = np.concatenate([b, np.zeros((P, D - b.shape[1]), b.dtype)], 1)
            out.append(b)

    def w_out_part(w, i):
        s = _slots(w[4 * i * P:4 * (i + 1) * P], np)
        put(np.concatenate([s[2 * t], s[2 * t + 1]], 1) for t in range(KT // 2))

    for ph in phases:
        if ph == "ffn":
            ab, layer = "ab"[ffn_at % 2], ffn_at // 2
            gu = _slots(inputs[f"w_ffn_{ab}_gu"][layer], np)
            down = inputs[f"w_ffn_{ab}_down"][layer]
            f0 = 0
            for nf in PIECES:
                for f in range(f0, f0 + nf):
                    put([gu[f], gu[D_FF // P + f]])
                put(_slots(down[f0 * P:(f0 + nf) * P], np))
                f0 += nf
            ffn_at += 1
        elif ph == "ret":
            s = _slots(inputs["ret_w_in"][ret_at], np)
            put([s[0], s[8]])
            for i in range(RET_STEPS):
                for h in (2 * i, 2 * i + 1):
                    v = np.stack([s[16 + 2 * h], s[17 + 2 * h]], 2)
                    put([v[:, 0:4], v[:, 4:8], s[32 + 2 * h], s[33 + 2 * h]])
                    if h + 1 < H_RET:
                        put([s[h + 1], s[9 + h]])
                w_out_part(inputs["ret_w_out"][ret_at], i)
            ret_at += 1
        elif ph == "sb":
            s = _slots(inputs["sb_w_qkv"][sb_at], np)
            w = _slots(inputs["sb_w_out"][sb_at], np)

            def qkv(p):
                put([s[p], s[8 + p], s[16 + p]])

            qkv(0)
            def w_out(p):
                put(np.concatenate([w[d][:, p:p + 2] for d in range(4 * m, 4 * m + 4)], 1) for m in range(2))

            for t in range(PAIRS // 2 - 1):
                qkv(2 * t + 1)
                qkv(2 * t + 2)
                if t < SB_STEPS:
                    w_out(2 * t)
            qkv(PAIRS - 1)
            w_out(PAIRS - 4)
            w_out(PAIRS - 2)
            sb_at += 1
        else:
            gate, s = _slots(inputs["ple_w_gate"][ple_at], np), _slots(inputs["ple_w_proj"][ple_at], np)
            for m in range(2):
                put(gate[4 * m:4 * m + 4])
                put([np.concatenate([s[4 * m + t] for t in range(4)], 1)])
            ple_at += 1
    return np.stack(out)


def _constants(np):
    f32 = np.float32
    pos = np.concatenate([np.arange(SEQ), np.tile(128 + np.arange(STEP), STREAMS)]).astype(f32)
    idx = np.concatenate([np.arange(SEQ), np.tile(np.arange(STEP), STREAMS)]).astype(np.float64)
    freqs = (f32(10000.0) ** (-np.arange(64, dtype=f32) / f32(64))).astype(f32)
    ang = (freqs[:, None] * pos[None, :]).astype(f32).astype(np.float64)
    cos, sin = np.cos(ang), np.sin(ang)
    cs = np.stack([np.concatenate([cos, cos]), np.concatenate([-sin, sin])], 1)
    log_g = np.log1p(-(2.0 ** (-5.0 - np.arange(H_RET))))
    dq = np.exp((idx[None] + 1) * log_g[:, None])
    dk = np.exp(-(idx[None] + 1) * log_g[:, None]) * P ** -0.5
    dec = np.broadcast_to(np.stack([dq, dk], 1)[:, None], (H_RET, P, 2, TOK))
    gpow = np.broadcast_to(np.stack([np.exp(SEQ * log_g), np.exp(STEP * log_g)], 1)[None], (P, H_RET, 2))
    a = np.arange(P)
    same = a[:, None] // STEP == a[None, :] // STEP
    incl, strict = a[:, None] <= a[None, :], a[:, None] < a[None, :]
    rmask = np.stack([incl] * 4 + [incl & same], 1)
    seen = np.stack([strict, strict & same], 1)
    smask = a[:, None] // STEP == np.arange(STREAMS)[None, :]
    negtri = np.stack([-(a[:, None] >= a[None, :]).astype(f32), -np.ones((P, P), f32)], 1)
    out = dict(ones_d=np.ones((P, P)), ident_d=np.eye(P), negtri_d=negtri, cs_d=cs, dec_d=dec, rmask_d=rmask,
               smask_d=smask, gpow_d=gpow, bmask_d=seen, bcap_d=np.where(seen, 3e38, -1e30))
    return {k: np.ascontiguousarray(v, dtype=f32) for k, v in out.items()}


def _lay_out(inputs, phases, np):
    def tokens(prompt, sample):
        t = np.concatenate([prompt.reshape(SEQ, -1), sample.reshape(TOK - SEQ, -1)])
        return t.T.reshape(-1, P, TOK)

    a = dict(xT=tokens(inputs["x_prompt"], inputs["x_sample"]))
    a["pT"] = np.stack([tokens(inputs["p_prompt"][i], inputs["p_sample"][i]) for i in range(2)])
    layers = [inputs[n][i] for i in range(2) for n in ("norm_ffn_a", "norm_mix", "norm_ffn_b", "norm_ple")]
    gains = np.stack(layers[:len(phases)] + [inputs["norm_final"]] * (9 - len(layers[:len(phases)])))
    a["gains"] = gains.reshape(9, KT, P).transpose(2, 0, 1)
    a["wst"] = _stream(inputs, phases, np)
    a.update(_constants(np))
    a["st_d"] = inputs["state_ret"][0].transpose(1, 2, 0, 3)
    k, v = inputs["cache_sb_k"][0], inputs["cache_sb_v"][0]
    a["kc_d"] = k.reshape(STREAMS, P, PAIRS, P).transpose(2, 3, 0, 1)
    a["vc_d"] = v.reshape(STREAMS, P, PAIRS, P).transpose(2, 1, 0, 3)
    return {k: np.ascontiguousarray(v) for k, v in a.items()}


_ORDER = ["xT", "pT", "gains", "wst", "ones_d", "ident_d", "negtri_d", "cs_d", "dec_d", "rmask_d", "smask_d", "gpow_d",
          "bmask_d", "bcap_d", "st_d", "kc_d", "vc_d"]
_OUTS = [("y_o", (KT, P, TOK)), ("stp_o", (H_RET, P, DV)), ("sts_o", (H_RET, P, STREAMS, DV)),
         ("k_o", (PAIRS, P, TOK)), ("v_o", (PAIRS, P, TOK))]


def _program(nc, arrays, phases, mybir):
    args = [nc.dram_tensor(n, arrays[n].shape, mybir.dt.float32, kind="ExternalInput").ap() for n in _ORDER]
    args += [nc.dram_tensor(n, shape, mybir.dt.float32, kind="ExternalOutput").ap() for n, shape in _OUTS]
    trunk(nc, phases, *args)


def kernel(**inputs):
    import numpy as np
    import concourse.bacc as bacc
    from concourse import mybir
    from concourse.bass_utils import run_bass_kernel_spmd

    inputs = {k: np.asarray(v) for k, v in inputs.items()}
    arrays = _lay_out(inputs, PHASES, np)
    nc = bacc.Bacc("TRN2", target_bir_lowering=False, num_devices=1)
    _program(nc, arrays, PHASES, mybir)
    r = run_bass_kernel_spmd(nc, [arrays], core_ids=[0]).results[0]

    def back(t, tail):
        t = t.reshape(D, TOK).T
        return (np.ascontiguousarray(t[:SEQ]).reshape((1, SEQ) + tail),
                np.ascontiguousarray(t[SEQ:]).reshape((STREAMS, STEP) + tail))

    y_p, y_s = back(r["y_o"], (D,))
    k_p, k_s = back(r["k_o"], (H_SB, HD))
    v_p, v_s = back(r["v_o"], (H_SB, HD))
    st_p = np.ascontiguousarray(r["stp_o"]).reshape(1, 1, H_RET, P, DV)
    st_s = np.ascontiguousarray(r["sts_o"].transpose(2, 0, 1, 3))[None]
    return y_p, y_s, st_p, st_s, k_p[None], v_p[None], k_s[None], v_s[None]
```
